# Optimizing a Trainium2 kernel written in Bass

```python
import jax, jax.numpy as jnp
from jax import lax
import numpy as np

D_MODEL = 1024
BATCH = 1
SEQ = 512
DEPTH = 1

CHUNK = 64
HEAD_DIM = 64
SWA_HEADS = 8
SWA_KV_HEADS = 2
SWA_WINDOW = 128
SWA_WIN_CHUNKS = SWA_WINDOW // CHUNK
NUM_BUCKETS = 32
MAX_DISTANCE = 128
SSD_INNER = D_MODEL
SSD_HEAD_DIM = 64
SSD_HEADS = SSD_INNER // SSD_HEAD_DIM
SSD_GROUPS = 2
SSD_STATE = 128
SSD_CONV = 4
SSD_BLOCK = 64
SSD_CONV_DIM = SSD_INNER + 2 * SSD_GROUPS * SSD_STATE
SB_HEADS = 8
SB_BLOCK = 128
SWA_WIDTH = SWA_HEADS * HEAD_DIM
SWA_KV_WIDTH = SWA_KV_HEADS * HEAD_DIM
SB_WIDTH = SB_HEADS * HEAD_DIM
MIX_WIDTH = SWA_WIDTH + SSD_INNER + SB_WIDTH
N_BRANCHES = 3
D_FF = 4 * D_MODEL
IN_SPLITS = (SWA_WIDTH, SWA_KV_WIDTH, SWA_KV_WIDTH, SSD_INNER, SSD_CONV_DIM, SSD_HEADS,
             SB_WIDTH, SB_WIDTH, SB_WIDTH, N_BRANCHES * D_MODEL)
IN_COLS = sum(IN_SPLITS)
EPS = 1e-6

kernel_name = "hybrid_gated_swa_ssd_stickbreak_block"

def rms_norm(x, w):
    xf = x.astype(jnp.float32)
    y = xf * lax.rsqrt(jnp.mean(xf * xf, axis=-1, keepdims=True) + EPS)
    return (y * w.astype(jnp.float32)).astype(x.dtype)

def split_cols(p):
    idx = np.cumsum(IN_SPLITS)[:-1].tolist()
    return jnp.split(p, idx, axis=-1)

def t5_relative_buckets():
    q = np.arange(CHUNK)[:, None]
    s = np.arange(SWA_WIN_CHUNKS * CHUNK)[None, :]
    rel = (s - (SWA_WIN_CHUNKS - 1) * CHUNK) - q
    nb = NUM_BUCKETS // 2
    max_exact = nb // 2
    n = np.abs(rel)
    large = max_exact + (np.log(np.maximum(n, 1) / max_exact) / np.log(MAX_DISTANCE / max_exact)
                         * (nb - max_exact)).astype(np.int32)
    large = np.minimum(large, nb - 1)
    return (np.where(rel > 0, nb, 0) + np.where(n < max_exact, n, large)).astype(np.int32)

def swa_sink_attention(q, k, v, sinks, rel_bias):
    b, l = q.shape[:2]
    nc = l // CHUNK
    g = SWA_HEADS // SWA_KV_HEADS
    kw = SWA_WIN_CHUNKS * CHUNK
    qc = q.reshape(b, nc, CHUNK, SWA_KV_HEADS, g, HEAD_DIM)
    kc = k.reshape(b, nc, CHUNK, SWA_KV_HEADS, HEAD_DIM)
    vc = v.reshape(b, nc, CHUNK, SWA_KV_HEADS, HEAD_DIM)

    def band(t):
        parts = [jnp.pad(t, ((0, 0), (j, 0), (0, 0), (0, 0), (0, 0)))[:, :nc]
                 for j in range(SWA_WIN_CHUNKS - 1, -1, -1)]
        return jnp.concatenate(parts, axis=2)

    kb, vb = band(kc), band(vc)
    s = jnp.einsum("bcqkgd,bcskd->bkgcqs", qc, kb).astype(jnp.float32) * (HEAD_DIM ** -0.5)
    bias = rel_bias.astype(jnp.float32)[t5_relative_buckets()]
    bias = bias.transpose(2, 0, 1).reshape(SWA_KV_HEADS, g, 1, CHUNK, kw)
    key_chunk = np.arange(nc)[:, None] - (SWA_WIN_CHUNKS - 1) + np.arange(kw)[None, :] // CHUNK
    valid = (key_chunk >= 0)[:, None, :]
    s = jnp.where(valid, s + bias, -jnp.inf)
    sink = sinks.astype(jnp.float32).reshape(SWA_KV_HEADS, g, 1, 1, 1)
    m = jnp.maximum(jnp.max(s, axis=-1, keepdims=True), sink)
    p = jnp.exp(s - m)
    p = p / (jnp.sum(p, axis=-1, keepdims=True) + jnp.exp(sink - m))
    o = jnp.einsum("bkgcqs,bcskd->bcqkgd", p.astype(v.dtype), vb)
    return o.reshape(b, l, SWA_WIDTH)

def causal_depthwise_conv(u, w, bias):
    k = w.shape[0]
    out = lax.conv_general_dilated(u, w[:, None, :], window_strides=(1,), padding=[(k - 1, 0)],
                                   dimension_numbers=("NWC", "WIO", "NWC"),
                                   feature_group_count=u.shape[-1])
    return out + bias

def ssd_chunked_scan(x, dt, a, bm, cm):
    b, l, h, p = x.shape
    nc = l // SSD_BLOCK
    hg = SSD_HEADS // SSD_GROUPS
    xc = x.astype(jnp.float32).reshape(b, nc, SSD_BLOCK, SSD_GROUPS, hg, p)
    dtc = dt.reshape(b, nc, SSD_BLOCK, SSD_GROUPS, hg)
    bc = bm.astype(jnp.float32).reshape(b, nc, SSD_BLOCK, SSD_GROUPS, SSD_STATE)
    cc = cm.astype(jnp.float32).reshape(b, nc, SSD_BLOCK, SSD_GROUPS, SSD_STATE)
    a_cum = jnp.cumsum(dtc * a.reshape(SSD_GROUPS, hg), axis=2)
    seg = a_cum[:, :, :, None] - a_cum[:, :, None]
    causal = np.tril(np.ones((SSD_BLOCK, SSD_BLOCK), dtype=bool))[:, :, None, None]
    decay = jnp.exp(jnp.where(causal, seg, -jnp.inf))
    cb = jnp.einsum("bctgn,bcsgn->bctsg", cc, bc)
    y_diag = jnp.einsum("bctsg,bctsgh,bcsgh,bcsghp->bctghp", cb, decay, dtc, xc)
    decay_to_end = jnp.exp(a_cum[:, :, -1:] - a_cum)
    states = jnp.einsum("bcsgn,bcsgh,bcsghp->bcghpn", bc, decay_to_end * dtc, xc)
    chunk_decay = jnp.exp(a_cum[:, :, -1])

    def step(carry, inp):
        st, dec = inp
        return dec[..., None, None] * carry + st, carry

    init = jnp.zeros((b, SSD_GROUPS, hg, p, SSD_STATE), jnp.float32)
    _, prev = lax.scan(step, init, (jnp.moveaxis(states, 1, 0), jnp.moveaxis(chunk_decay, 1, 0)))
    prev = jnp.moveaxis(prev, 0, 1)
    y_off = jnp.einsum("bctgn,bcghpn,bctgh->bctghp", cc, prev, jnp.exp(a_cum))
    return (y_diag + y_off).reshape(b, l, h, p)

def ssd_mixer(z, xbc, dt_raw, conv_w, conv_b, dt_bias, a_log, d_skip, norm_w):
    b, l, _ = z.shape
    xbc = jax.nn.silu(causal_depthwise_conv(xbc, conv_w, conv_b))
    xs, bm, cm = jnp.split(xbc, [SSD_INNER, SSD_INNER + SSD_GROUPS * SSD_STATE], axis=-1)
    xs = xs.reshape(b, l, SSD_HEADS, SSD_HEAD_DIM)
    bm = bm.reshape(b, l, SSD_GROUPS, SSD_STATE)
    cm = cm.reshape(b, l, SSD_GROUPS, SSD_STATE)
    dt = jax.nn.softplus(dt_raw.astype(jnp.float32) + dt_bias.astype(jnp.float32))
    a = -jnp.exp(a_log.astype(jnp.float32))
    y = ssd_chunked_scan(xs, dt, a, bm, cm) + d_skip.astype(jnp.float32)[:, None] * xs.astype(jnp.float32)
    y = y.reshape(b, l, SSD_INNER) * jax.nn.silu(z.astype(jnp.float32))
    yg = y.reshape(b, l, SSD_GROUPS, SSD_INNER // SSD_GROUPS)
    yg = yg * lax.rsqrt(jnp.mean(yg * yg, axis=-1, keepdims=True) + EPS)
    return (yg.reshape(b, l, SSD_INNER) * norm_w.astype(jnp.float32)).astype(z.dtype)

def stick_breaking_attention(q, k, v):
    b, l = q.shape[:2]
    qh, kh, vh = (jnp.swapaxes(t, 1, 2) for t in (q, k, v))
    scale = HEAD_DIM ** -0.5
    outs = []
    for blk in range(l // SB_BLOCK):
        q0 = blk * SB_BLOCK
        kl = q0 + SB_BLOCK
        logits = jnp.einsum("bhqd,bhkd->bhqk", qh[:, :, q0:kl], kh[:, :, :kl]).astype(jnp.float32) * scale
        mask = np.arange(kl)[None, :] < (q0 + np.arange(SB_BLOCK))[:, None]
        log_stay = jnp.where(mask, jax.nn.log_sigmoid(-logits), 0.0)
        log_w = jax.nn.log_sigmoid(logits) + lax.cumsum(log_stay, axis=3, reverse=True) - log_stay
        w = jnp.where(mask, jnp.exp(log_w), 0.0)
        outs.append(jnp.einsum("bhqk,bhkd->bhqd", w.astype(v.dtype), vh[:, :, :kl]))
    return jnp.swapaxes(jnp.concatenate(outs, axis=2), 1, 2).reshape(b, l, SB_WIDTH)

def setup_inputs(seed: int = 0) -> dict:
    key = jax.random.key(seed)
    ks = jax.random.split(key, 20)
    f32 = jnp.float32

    def nrm(k, shape, scale):
        return jax.random.normal(k, shape, f32) * scale

    x = nrm(ks[0], (BATCH, SEQ, D_MODEL), 1.0)
    norm_mix_w = 1.0 + nrm(ks[1], (DEPTH, D_MODEL), 0.02)
    w_in = nrm(ks[2], (DEPTH, D_MODEL, IN_COLS), D_MODEL ** -0.5)
    swa_sinks = nrm(ks[3], (DEPTH, SWA_HEADS), 0.5)
    rel_bias = nrm(ks[4], (NUM_BUCKETS, SWA_HEADS), 0.5)
    conv_w = nrm(ks[5], (DEPTH, SSD_CONV, SSD_CONV_DIM), SSD_CONV ** -0.5)
    conv_b = nrm(ks[6], (DEPTH, SSD_CONV_DIM), 0.02)
    dt0 = jnp.exp(jax.random.uniform(ks[7], (DEPTH, SSD_HEADS), f32,
                                     float(np.log(1e-3)), float(np.log(1e-1))))
    dt_bias = dt0 + jnp.log(-jnp.expm1(-dt0))
    a_log = jnp.log(jax.random.uniform(ks[8], (DEPTH, SSD_HEADS), f32, 1.0, 16.0))
    d_skip = 1.0 + nrm(ks[9], (DEPTH, SSD_HEADS), 0.02)
    ssd_norm_w = 1.0 + nrm(ks[10], (DEPTH, SSD_INNER), 0.02)
    w_out = jnp.concatenate([nrm(ks[11], (DEPTH, SWA_WIDTH, D_MODEL), SWA_WIDTH ** -0.5),
                             nrm(ks[12], (DEPTH, SSD_INNER, D_MODEL), SSD_INNER ** -0.5),
                             nrm(ks[13], (DEPTH, SB_WIDTH, D_MODEL), SB_WIDTH ** -0.5)], axis=1)
    w_merge = nrm(ks[14], (DEPTH, D_MODEL, D_MODEL), D_MODEL ** -0.5)
    norm_ffn_w = 1.0 + nrm(ks[15], (DEPTH, D_MODEL), 0.02)
    w_ff1 = nrm(ks[16], (DEPTH, D_MODEL, D_FF), D_MODEL ** -0.5)
    w_ff2 = nrm(ks[17], (DEPTH, D_FF, D_MODEL), D_FF ** -0.5)
    final_norm_w = 1.0 + nrm(ks[18], (D_MODEL,), 0.02)
    return {"x": x, "norm_mix_w": norm_mix_w, "w_in": w_in, "swa_sinks": swa_sinks, "rel_bias": rel_bias,
            "conv_w": conv_w, "conv_b": conv_b, "dt_bias": dt_bias, "a_log": a_log, "d_skip": d_skip,
            "ssd_norm_w": ssd_norm_w, "w_out": w_out, "w_merge": w_merge, "norm_ffn_w": norm_ffn_w,
            "w_ff1": w_ff1, "w_ff2": w_ff2, "final_norm_w": final_norm_w}

def reference(x, norm_mix_w, w_in, swa_sinks, rel_bias, conv_w, conv_b, dt_bias, a_log, d_skip,
              ssd_norm_w, w_out, w_merge, norm_ffn_w, w_ff1, w_ff2, final_norm_w):
    b, l, _ = x.shape
    a_end = SWA_WIDTH
    b_end = SWA_WIDTH + SSD_INNER
    for i in range(DEPTH):
        h = rms_norm(x, norm_mix_w[i])
        qa, ka, va, z, xbc, dt_raw, qs, ks_, vs, gate_logits = split_cols(h @ w_in[i])
        oa = swa_sink_attention(qa.reshape(b, l, SWA_HEADS, HEAD_DIM),
                                ka.reshape(b, l, SWA_KV_HEADS, HEAD_DIM),
                                va.reshape(b, l, SWA_KV_HEADS, HEAD_DIM), swa_sinks[i], rel_bias)
        ob = ssd_mixer(z, xbc, dt_raw, conv_w[i], conv_b[i], dt_bias[i], a_log[i], d_skip[i], ssd_norm_w[i])
        oc = stick_breaking_attention(qs.reshape(b, l, SB_HEADS, HEAD_DIM),
                                      ks_.reshape(b, l, SB_HEADS, HEAD_DIM),
                                      vs.reshape(b, l, SB_HEADS, HEAD_DIM))
        gates = jax.nn.sigmoid(gate_logits.astype(jnp.float32)).astype(x.dtype)
        gates = gates.reshape(b, l, N_BRANCHES, D_MODEL)
        wo = w_out[i]
        ua = oa @ wo[:a_end]
        ub = ob @ wo[a_end:b_end]
        uc = oc @ wo[b_end:]
        merged = gates[:, :, 0] * ua + gates[:, :, 1] * ub + gates[:, :, 2] * uc
        x = x + merged @ w_merge[i]
        h = rms_norm(x, norm_ffn_w[i])
        x = x + jnp.square(jax.nn.relu(h @ w_ff1[i])) @ w_ff2[i]
    return rms_norm(x, final_norm_w)


_drawn_inputs = setup_inputs


def setup_inputs(seed=0):
    import zlib

    import numpy as np

    out = dict(_drawn_inputs(seed))
    spreads = {}
    factors = {'norm_mix_w': 3.105,
     'swa_sinks': 64.0,
     'conv_b': 3.851,
     'd_skip': 200.0,
     'ssd_norm_w': 54.203,
     'norm_ffn_w': 11.183,
     'final_norm_w': 24.851,
     'rel_bias': 3.775}
    for name, (base, spread) in spreads.items():
        noise = np.random.default_rng([zlib.crc32(name.encode()), seed]).standard_normal(out[name].shape)
        drawn = base * np.exp(spread * noise) if base else spread * noise
        out[name] = __import__('jax').numpy.asarray(drawn.astype(out[name].dtype))
    for name, factor in factors.items():
        out[name] = (out[name] * factor).astype(out[name].dtype)
    return out
```

```python
from contextlib import ExitStack

import concourse.bass as bass
import numpy as np
from concourse import mybir

F32 = mybir.dt.float32
F32R = mybir.dt.float32r
ALU = mybir.AluOpType
ACT = mybir.ActivationFunctionType
AX = mybir.AxisListType

P = 128
T = 512
TT = T // P
D = 1024
KT = D // P
HD = 64
EPS = 1e-6
KIB = 1024

SWA_HEADS, KV_HEADS, CHUNK, BUCKETS, MAX_DIST = 8, 2, 64, 32, 128
KEYS = P + CHUNK
REL = P + KEYS - 1
SB_HEADS = 8
SSD_HEADS = 16
CONV = 4
CONV_T = 12
DFF = 4096

C_QA, C_KA, C_Z, C_XBC, C_DT, C_QS, C_KS, C_VS, C_G = 0, 512, 768, 1792, 3328, 3344, 3856, 4368, 4880
BC = 256
V_MIX, V_CW, V_CB, V_SSDN, V_FFN, V_FIN, V_ROWS = 0, 8, 56, 68, 76, 84, 92


def plan():
    blocks, steps = [], []

    def block(kind, matrix, row, kts, col, first):
        blocks.append((kind, matrix, row, kts, col, first))
        return ("block", len(blocks) - 1)

    def w_in(kind, col, n):
        return [block(kind, "w_in", 0, KT, col + BC * i, 2 * i) for i in range(n)]

    def branch(b, row, kts):
        out = []
        for i in range(D // BC):
            out.append(block("gate", "w_in", 0, KT, C_G + b * D + BC * i, 2 * i))
            out.append(block("u%d" % b, "w_out", row, kts, BC * i, 2 * i))
        return out

    def weave(blks, others):
        out, done = [], 0
        for i, s in enumerate(blks):
            out.append(s)
            upto = (i + 1) * len(others) // len(blks)
            out += others[done:upto]
            done = upto
        return out + others[done:]

    sb = [("sb_scores", 0)]
    for h in range(SB_HEADS):
        sb.append(("sb_cum", h))
        sb.append(("sb_av", h))
    swa = [("swa_scores", 0)]
    for u in range(8):
        if u < 7:
            swa.append(("swa_scores", u + 1))
        swa += [("swa_turn", u), ("swa_pv", u)]
    ssd = []
    for c in range(TT):
        ssd.append(("ssd_prep", c))
        for r in range(4):
            ssd.append(("ssd_y", (c, r)))
        if c < TT - 1:
            ssd.append(("ssd_state", c))

    steps += [("load", 0), ("norm", 0)]
    steps += w_in("qs", C_QS, 2) + w_in("ks", C_KS, 2) + w_in("vs", C_VS, 2) + [("vs_turn", 0), ("dt", 0)]
    steps += weave(w_in("qa", C_QA, 2) + w_in("kava", C_KA, 1) + w_in("xbc", C_XBC, 6), sb)
    steps += [("va_turn", 0), ("bias", 0), ("silu", 0), ("split_c", 0)]
    steps += weave(branch(2, 1536, 4), swa)
    steps += [("split_a", 0)]
    steps += weave(branch(0, 0, 4), ssd)
    steps += w_in("z", C_Z, 4)
    steps += [("split_b", 0)]
    steps += branch(1, 512, 8)
    steps += [("split_m", 0)]
    steps += [block("merge", "w_merge", 0, KT, BC * i, 2 * i) for i in range(4)]
    steps += [("norm", 1)]
    return blocks, steps


BLOCKS, STEPS = plan()
NB = len(BLOCKS)
X_BLOCKS = [("sb", h) for h in range(8)]


def tile_of(kind, i=0):
    return [2 * n for n, b in enumerate(BLOCKS) if b[0] == kind][i // 2] + i % 2


def build(nc, ins, out):
    with ExitStack() as ctx:
        def sem(name):
            return ctx.enter_context(nc.semaphore(name))

        base = -(-nc.sbuf_base // 32) * 32
        arena = ctx.enter_context(nc.sbuf_tensor("arena", [P, 207 * KIB // 4], F32))
        del arena

        def at(name, kib, shape, dt=F32):
            return nc.alloc_sbuf_tensor_at(name, [P] + shape, dt, offset=base + int(kib * KIB))

        raw = at("raw", 0, [2, KT, BC])
        w_hi = at("w_hi", 16, [2, KT, BC], F32R)
        w_lo = at("w_lo", 32, [2, KT, BC], F32R)
        xT = at("xT", 48, [KT, T])
        hH = at("hH", 64, [KT, T], F32R)
        hL = at("hL", 80, [KT, T], F32R)
        ident = at("ident", 96, [P])
        flip = at("flip", 96.5, [P])
        tri = at("tri", 97, [P])
        ones = at("ones", 97.5, [P])
        neg_tri = at("neg_tri", 98, [P])
        neg_one = at("neg_one", 98.5, [P])
        vec = at("vec", 99, [96])
        dtb = at("dtb", 99.5, [16])
        nega = at("nega", 99.5625, [16])
        sink = at("sink", 99.625, [8])
        dsk = at("dsk", 99.65625, [8])
        small = at("small", 99.6875, [80])
        dta = at("dta", 100, [TT, 16])
        dtv = at("dtv", 100.25, [TT, 16])
        dtt = at("dtt", 100.5, [4, TT * 16])
        rstd = at("rstd", 102, [T])
        tbias = at("tbias", 104, [SWA_HEADS, KEYS])
        xin = at("xin", 110, [TT, D])
        sq = at("sq", 174, [KT, T])
        hf = at("hf", 190, [2, T])
        vrow = at("vrow", 194, [P])
        onehot = at("onehot", 194.5, [320])
        relb = at("relb", 196, [8])
        frow = at("frow", 196.25, [320])
        wdt = at("wdt", 198, [KT, 16])
        wdtH = at("wdtH", 198.5, [KT, 16], F32R)
        wdtL = at("wdtL", 199, [KT, 16], F32R)
        trev = at("trev", 200, [SWA_HEADS, KEYS])
        qs = at("qs", 110, [4, T])
        ks = at("ks", 118, [4, T])
        vs = at("vs", 126, [TT, 512])
        sp = at("sp", 134, [1280])
        sw = at("sw", 139, [1280])
        qa = at("qa", 144, [4, T])
        kd = at("kd", 152, [KV_HEADS, T])
        va = at("va", 156, [TT, P])
        xs = at("xs", 158, [12, T])
        vsT = at("vsT", 158, [4, T])
        vaT = at("vaT", 182, [T])
        pr = at("pr", 118, [4, 256])
        pT = at("pT", 122, [2, T])
        oH = at("oH", 126, [4, T], F32R)
        oL = at("oL", 134, [4, T], F32R)
        mg = at("mg", 184, [KT, T])
        gt = at("gt", 200, [2, T])
        gu = at("gu", 204, [T])
        xd = at("xd", 110, [D])
        xw = at("xw", 114, [D])
        bt = at("bt", 118, [2, P])
        cbm = at("cbm", 119, [2, P])
        st = at("st", 120, [D])
        mt = at("mt", 124, [4, P])
        e2 = at("e2", 104, [2, P])
        t1 = at("t1", 105, [2, P])
        obH = at("obH", 110, [KT, T], F32R)
        obL = at("obL", 126, [KT, T], F32R)
        ysq = at("ysq", 142, [KT, T])
        mH = at("mH", 142, [KT, T], F32R)
        mL = at("mL", 158, [KT, T], F32R)
        aH = at("aH", 110, [16, T], F32R)
        aL = at("aL", 142, [16, T], F32R)
        rel = at("rel", 194, [2, T])
        rsq = at("rsq", 198, [2, T])
        yout = at("yout", 110, [KT, T])
        yrow = at("yrow", 126, [TT, D])

        pj = [ctx.enter_context(nc.psum_tensor("pj%d" % i, [P, 512], F32)) for i in range(2)]
        mx = ctx.enter_context(nc.psum_tensor("mx", [P, 6, 512], F32))
        mxf = mx[:, :, :].rearrange("p b n -> p (b n)")
        scr = nc.dram_tensor("rel_rows", [SWA_HEADS, 320], F32).ap()

        x_in, vec_in, row_in, rel_in = sem("x_in"), sem("vec_in"), sem("row_in"), sem("rel_in")
        scr_out, trev_in, dt_in, done = sem("scr_out"), sem("trev_in"), sem("dt_in"), sem("done")
        w_in_s = [sem("w_in%d" % i) for i in range(2)]
        hi_s, lo_s, tile_s = sem("w_hi_made"), sem("w_lo_made"), sem("tile_done")
        free_s = [sem("pj_read%d" % i) for i in range(2)]
        cst = sem("constants")
        v_tr, v_cp, x_tr, x_cp = sem("vec_turned"), sem("vec_ready"), sem("x_turned"), sem("x_ready")
        sq_s, ms_s, hf_s, hhi_s, hlo_s = sem("squares"), sem("mean_sq"), sem("normed"), sem("h_hi"), sem("h_lo")
        x1_s = sem("residual")
        ri_s, ro_s = sem("root_in"), sem("root_out")
        vt_s, vc_s = sem("v_turned"), sem("v_copied")
        dws, dw, dtm, dtx, dte, dtf = (sem("dt_w_hi"), sem("dt_w_lo"), sem("dt_product"), sem("dt_raw"),
                                       sem("dt_exp"), sem("dt_ready"))
        b_f, b_fc, b_t, b_tc = sem("bias_rows"), sem("bias_copied"), sem("bias_flipped"), sem("bias_ready")
        zp_s, th_s, si_s = sem("p_zeroed"), sem("conv_tanh"), sem("conv_silu")
        s_sc, s_cl, s_ln, s_sp, s_spm = (sem("sb_scored"), sem("sb_clipped"), sem("sb_softplus"),
                                         sem("sb_stay"), sem("sb_stay_masked"))
        s_cu, s_w, s_wm, s_av, s_o = (sem("sb_summed"), sem("sb_weights"), sem("sb_weights_masked"),
                                      sem("sb_product"), sem("sb_out"))
        a_sc, a_p, a_m, a_e, a_n = (sem("swa_scored"), sem("swa_biased"), sem("swa_max"), sem("swa_exp"),
                                    sem("swa_normed"))
        a_t, a_tc, a_pv, a_o = sem("swa_turned"), sem("swa_pt"), sem("swa_product"), sem("swa_out")
        d_pr, d_da, d_w, d_xw = sem("ssd_prepared"), sem("ssd_decays"), sem("ssd_decay_exp"), sem("ssd_xw")
        d_ab, d_d, d_e, d_m, d_y, d_yc = (sem("ssd_cumsum"), sem("ssd_diff"), sem("ssd_exp"), sem("ssd_m"),
                                          sem("ssd_product"), sem("ssd_y"))
        d_st, d_stc = sem("ssd_states"), sem("ssd_state")
        shi, slo = sem("split_hi"), sem("split_lo")
        gt_s, gu_s, zt_s, zy_s, ysq_s, gms_s, gr_s = (sem("gate_tanh"), sem("gate_used"), sem("z_tanh"),
                                                      sem("y_gated"), sem("y_squares"), sem("y_mean_sq"),
                                                      sem("y_rstd"))
        r_s, rq_s, ah_s, al_s = sem("relu"), sem("relu_sq"), sem("act_hi"), sem("act_lo")
        yt_s, yc_s = sem("y_turned"), sem("y_row")
        own_a, own_v, own_g = sem("scalar_chain"), sem("vector_chain"), sem("pool_chain")

        block = ctx.enter_context(nc.Block())

        matrices = {k: ins[k][0] for k in ("w_in", "w_out", "w_merge", "w_ff1", "w_ff2")}
        NX = len([1 for s in STEPS if s[0] == "block"])
        assert NX == NB

        SPLITS = {"split_c": 0, "split_a": 4, "split_b": 8, "split_m": 16}

        def extra(c):
            return sum(1 for n, b in enumerate(BLOCKS) for s in range(2)
                       if 2 * n + s <= c and (2 * n + s) % 2 == c % 2 and b[0] in ("gate", "merge"))

        def cumsum(pe, c, r):
            n = 4 * c + r
            if n >= 2:
                pe.wait_ge(d_e, n - 1)
            for hh in range(4):
                h = 4 * r + hh
                m = pe.matmul(mx[:, 4 + r % 2, P * hh:P * hh + P],
                              dta[:, c, h:h + 1].broadcast_to([P, P]), tri[:, :], start=True, stop=True)
            m.then_inc(d_ab, 1)

        @block.sync
        def _(sp_):
            for t in range(TT):
                sp_.dma_start(xin[:, t, :], ins["x"][0, P * t:P * t + P, :]).then_inc(x_in, 16)
            sp_.dma_start(vrow[V_MIX:V_CW, :], ins["norm_mix_w"][0].rearrange("(a p) -> a p", p=P)).then_inc(vec_in, 16)
            sp_.dma_start(vrow[V_CW:V_CB, :], ins["conv_w"][0].rearrange("k (a p) -> (k a) p", p=P)).then_inc(vec_in, 16)
            sp_.dma_start(vrow[V_CB:V_SSDN, :], ins["conv_b"][0].rearrange("(a p) -> a p", p=P)).then_inc(vec_in, 16)
            sp_.dma_start(vrow[V_SSDN:V_FFN, :], ins["ssd_norm_w"][0].rearrange("(a p) -> a p", p=P)).then_inc(vec_in, 16)
            sp_.dma_start(vrow[V_FFN:V_FIN, :], ins["norm_ffn_w"][0].rearrange("(a p) -> a p", p=P)).then_inc(vec_in, 16)
            sp_.dma_start(vrow[V_FIN:V_ROWS, :], ins["final_norm_w"].rearrange("(a p) -> a p", p=P)).then_inc(vec_in, 16)

            def load_block(n):
                _, matrix, row, kts, col, _ = BLOCKS[n]
                if n >= 2:
                    sp_.wait_ge(lo_s, n - 1)
                src = matrices[matrix][row:row + P * kts, col:col + BC].rearrange("(k p) c -> p k c", p=P)
                sp_.dma_start(raw[:, n % 2, 0:kts, :], src).then_inc(w_in_s[n % 2], 16)

            load_block(0)
            load_block(1)
            bc = lambda a, n: a[0:1, :].broadcast_to([P, n])
            sp_.dma_start(dtb[:, :], bc(ins["dt_bias"], 16)).then_inc(row_in, 16)
            sp_.dma_start(nega[:, :], bc(ins["a_log"], 16)).then_inc(row_in, 16)
            sp_.dma_start(sink[:, :], bc(ins["swa_sinks"], 8)).then_inc(row_in, 16)
            for half in range(2):
                src = ins["d_skip"].rearrange("a (q two) -> a two q", two=2)[0:1, half, :]
                sp_.dma_start(dsk[64 * half:64 * half + 64, :], src.broadcast_to([64, 8]),
                              allow_slow_non_contiguous=True).then_inc(row_in, 16)
            sp_.dma_start(onehot[0:BUCKETS, :], ins["onehot"]).then_inc(rel_in, 16)
            sp_.dma_start(relb[0:BUCKETS, :], ins["rel_bias"]).then_inc(rel_in, 16)
            src = matrices["w_in"][:, C_DT:C_DT + 16].rearrange("(k p) c -> p k c", p=P)
            sp_.dma_start(wdt[:, :, :], src).then_inc(dt_in, 16)
            sp_.wait_ge(b_fc, 1)
            sp_.dma_start(scr, frow[0:SWA_HEADS, :]).then_inc(scr_out, 16)
            sp_.wait_ge(scr_out, 16)
            for n in range(4):
                src = bass.AP(tensor=scr.tensor, offset=320 * (4 * (n // 2) + n % 2), ap=[[1, P], [640, 2], [1, KEYS]])
                sp_.dma_start(trev[:, 2 * n:2 * n + 2, :], src).then_inc(trev_in, 16)
            for n in range(2, NB):
                load_block(n)
            with sp_.Fori(0, 2) as half:
                with sp_.Fori(0, 4) as i:
                    for s in range(2):
                        sp_.wait_ge(lo_s, half * 16 + i * 2 + (NB + s - 1))
                        src = matrices["w_ff1"][:, bass.ds(half * 2048 + i * 512 + s * BC, BC)]
                        sp_.dma_start(raw[:, (NB + s) % 2, :, :], src.rearrange("(k p) c -> p k c", p=P)
                                      ).then_inc(w_in_s[(NB + s) % 2], 16)
                with sp_.Fori(0, 4) as i:
                    for s in range(2):
                        sp_.wait_ge(lo_s, half * 16 + i * 2 + (NB + 8 + s - 1))
                        src = matrices["w_ff2"][bass.ds(half * 2048 + s * 1024, 1024), bass.ds(i * BC, BC)]
                        sp_.dma_start(raw[:, (NB + s) % 2, :, :], src.rearrange("(k p) c -> p k c", p=P)
                                      ).then_inc(w_in_s[(NB + s) % 2], 16)
            for t in range(TT):
                sp_.wait_ge(yc_s, 2 * (t + 1))
                sp_.dma_start(out[0, P * t:P * t + P, :], yrow[:, t, :]).then_inc(done, 16)
            sp_.wait_ge(done, 16 * TT)

        @block.gpsimd
        def _(g):
            n_own = [0]

            def own(i):
                i.then_inc(own_g, 1)
                n_own[0] += 1
                g.wait_ge(own_g, n_own[0])

            def sel(t, op, fill, mult, step, base_=0):
                own(g.affine_select(out=t, in_=t, compare_op=op, fill=fill, base=base_,
                                    pattern=[[step, P]], channel_multiplier=mult))

            own(g.memset(ident[:, :], 0.0))
            sel(ident[:, :], ALU.not_equal, 1.0, 1, -1)
            own(g.memset(flip[:, :], 0.0))
            sel(flip[:, :], ALU.not_equal, 1.0, 1, 1, -(P - 1))
            own(g.memset(ones[:, :], 1.0))
            own(g.memset(tri[:, :], 1.0))
            sel(tri[:, :], ALU.is_ge, 0.0, -1, 1)
            own(g.memset(neg_one[:, :], -1.0))
            own(g.memset(neg_tri[:, :], -1.0))
            sel(neg_tri[:, :], ALU.is_ge, 0.0, 1, -1)
            g.memset(ident[0:1, 0:1], 1.0).then_inc(cst, 1)

            def low(n):
                kts = BLOCKS[n][3]
                g.wait_ge(hi_s, n + 1)
                g.tensor_tensor(w_lo[:, n % 2, 0:kts, :], raw[:, n % 2, 0:kts, :],
                                w_hi[:, n % 2, 0:kts, :].bitcast(F32), ALU.subtract).then_inc(lo_s, 1)

            def diag(t, s):
                v3 = t[:, 0:1152].rearrange("p (a b) -> p a b", b=128)[:, 0:9:4, :]
                v1 = t[:, 896:1024]
                g.affine_select(out=v3, in_=v3, compare_op=ALU.is_gt, fill=0.0, base=0,
                                pattern=[[0, 3], [1, P]], channel_multiplier=-1).then_inc(s, 1)
                g.affine_select(out=v1, in_=v1, compare_op=ALU.is_gt, fill=0.0, base=0,
                                pattern=[[1, P]], channel_multiplier=-1).then_inc(s, 1)

            low(0)
            for kind, k in STEPS:
                if kind == "block" and k + 1 < NB:
                    low(k + 1)
                elif kind == "sb_cum":
                    g.wait_ge(s_sp, k + 1)
                    diag(sp, s_spm)
                elif kind == "sb_av":
                    g.wait_ge(s_w, k + 1)
                    diag(sw, s_wm)
            with g.Fori(0, 2) as half:
                for ph in range(2):
                    with g.Fori(0, 4) as i:
                        for s in range(2):
                            g.wait_ge(hi_s, half * 16 + i * 2 + (NB + 8 * ph + s + 1))
                            g.tensor_tensor(w_lo[:, (NB + s) % 2], raw[:, (NB + s) % 2],
                                            w_hi[:, (NB + s) % 2].bitcast(F32), ALU.subtract).then_inc(lo_s, 1)

        @block.scalar
        def _(a):
            n_own = [0]

            def own(i):
                i.then_inc(own_a, 1)
                n_own[0] += 1
                a.wait_ge(own_a, n_own[0])

            def high(n):
                kts = BLOCKS[n][3]
                a.wait_ge(w_in_s[n % 2], 16 * (n // 2 + 1))
                if n >= 2:
                    a.wait_ge(tile_s, 2 * (n - 1))
                a.activation(w_hi[:, n % 2, 0:kts, :], raw[:, n % 2, 0:kts, :], ACT.Copy).then_inc(hi_s, 1)

            def norm(n):
                for k in range(KT):
                    if n == 0:
                        a.wait_ge(x_cp, k + 1)
                    elif n == 1:
                        a.wait_ge(x1_s, k + 1)
                    else:
                        a.wait_ge(x1_s, 24)
                    a.activation(sq[:, k, :], xT[:, k, :], ACT.Square).then_inc(sq_s, 1)

            roots = [0]

            def root():
                roots[0] += 1
                a.wait_ge(ri_s, roots[0])
                a.activation(rstd[:, :], rstd[:, :], ACT.Sqrt).then_inc(ro_s, 1)

            def h_high(n):
                root()
                for k in range(KT):
                    a.wait_ge(hf_s, 8 * n + k + 1)
                    a.activation(hH[:, k, :], hf[:, k % 2, :], ACT.Copy).then_inc(hhi_s, 1)

            def split(name, src, dst, m, scale=1.0):
                for k in range(m):
                    a.activation(dst[:, k, :], src[:, k, :], ACT.Copy, scale=scale).then_inc(shi, 1)

            seen_z = [0]
            for kind, k in STEPS:
                if kind == "norm":
                    norm(k)
                    if k == 0:
                        high(0)
                    h_high(k)
                elif kind == "block":
                    if k + 1 < NB:
                        high(k + 1)
                    what, _, _, _, _, first = BLOCKS[k]
                    for s in range(2):
                        c, ct = 2 * k + s, first + s
                        if what == "gate":
                            a.wait_ge(tile_s, c + 1)
                            gi = sum(1 for b in BLOCKS[:k] if b[0] == "gate") * 2 + s
                            if gi >= 2:
                                a.wait_ge(gu_s, gi - 1)
                            else:
                                a.wait_ge(th_s, CONV_T)
                            if gi in (16, 17):
                                a.wait_ge(zy_s, KT)
                            a.activation(gt[:, s, :], pj[c % 2][:, :], ACT.Tanh, scale=0.5).then_inc(gt_s, 1)
                        if what == "z":
                            a.wait_ge(tile_s, c + 1)
                            if ct >= 2:
                                a.wait_ge(zy_s, ct - 1)
                            else:
                                a.wait_ge(gu_s, 16)
                            a.activation(gt[:, s, :], pj[c % 2][:, :], ACT.Tanh, scale=0.5).then_inc(zt_s, 1)
                            if ct >= 1:
                                a.wait_ge(zy_s, ct)
                                a.activation(ysq[:, ct - 1, :], xs[:, ct - 1, :], ACT.Square).then_inc(ysq_s, 1)
                            if ct == 7:
                                a.wait_ge(zy_s, 8)
                                a.activation(ysq[:, 7, :], xs[:, 7, :], ACT.Square).then_inc(ysq_s, 1)
                elif kind == "dt":
                    a.wait_ge(dt_in, 16)
                    a.activation(wdtH[:, :, :], wdt[:, :, :], ACT.Copy).then_inc(dws, 1)
                    a.wait_ge(row_in, 80)
                    own(a.activation(nega[:, :], nega[:, :], ACT.Exp))
                    a.wait_ge(dtx, 1)
                    own(a.activation(dtt[:, 1, :], dtt[:, 1, :], ACT.Exp))
                    a.wait_ge(dtx, 2)
                    a.activation(dtt[:, 3, :], dtt[:, 2, :], ACT.Ln).then_inc(dte, 1)
                elif kind in ("sb_scores", "sb_av", "sb_cum"):
                    if kind == "sb_av":
                        a.wait_ge(s_cu, k + 1)
                        a.activation(sw[:, :], mxf[:, 0:1280], ACT.Exp).then_inc(s_w, 1)
                    h = 0 if kind == "sb_scores" else k + 1
                    if kind != "sb_cum" and h < SB_HEADS:
                        a.wait_ge(s_cl, h + 1)
                        own(a.activation(sw[:, :], sw[:, :], ACT.Exp))
                        a.activation(sw[:, :], sw[:, :], ACT.Ln, bias=1.0).then_inc(s_ln, 1)
                elif kind == "silu":
                    for c in range(CONV_T):
                        a.wait_ge(si_s, c + 1)
                        if c >= 2:
                            a.wait_ge(th_s, c - 1)
                        a.activation(gt[:, c % 2, :], xs[:, c, :], ACT.Tanh).then_inc(zp_s, 1)
                elif kind == "swa_turn":
                    a.wait_ge(a_m, k + 1)
                    k0 = P if k // 2 == 0 else CHUNK
                    for hh in range(4):
                        own(a.activation(pr[:, hh, k0:256], pr[:, hh, k0:256], ACT.Exp,
                                         bias=small[:, 4 + hh:5 + hh], accum_out=small[:, 12 + hh:13 + hh]))
                    a.activation(small[:, 8:12], small[:, 8:12], ACT.Exp).then_inc(a_e, 1)
                elif kind == "swa_pv":
                    a.wait_ge(a_t, k + 1)
                    lo = 1 if k // 2 == 0 else 0
                    a.activation(pT[:, lo:2, :], mx[:, 2 + lo:4, :], ACT.Copy).then_inc(a_tc, 1)
                elif kind == "split_c":
                    a.wait_ge(s_o, 4)
                    split(kind, qs, oH, 4)
                elif kind == "split_a":
                    a.wait_ge(a_o, 8)
                    a.wait_ge(tile_s, tile_of("u2", 7) + 1)
                    split(kind, qa, oH, 4)
                elif kind == "split_b":
                    for k2 in range(KT):
                        if k2 % 4 == 0:
                            root()
                        a.wait_ge(gr_s, k2 + 1)
                        a.activation(obH[:, k2, :], xs[:, k2, :], ACT.Copy).then_inc(shi, 1)
                elif kind == "split_m":
                    a.wait_ge(gu_s, 24)
                    a.wait_ge(slo, 16)
                    split(kind, mg, mH, 8, 0.5)
                elif kind == "ssd_prep":
                    a.wait_ge(d_da, k + 1)
                    a.activation(small[:, 32:64], small[:, 32:64], ACT.Exp).then_inc(d_w, 1)
                elif kind == "ssd_y":
                    c, r = k
                    n = 4 * c + r
                    a.wait_ge(d_d, n + 1)
                    b = mx[:, 4 + r % 2, :].rearrange("p (q two t) -> p q two t", two=2, t=P)
                    if c > 0:
                        own(a.activation(e2[0:64, :, :], b[0:64, :, 0, :], ACT.Exp))
                        own(a.activation(e2[64:128, :, :], b[64:128, :, 1, :], ACT.Exp))
                    a.activation(mt[:, :, :], mt[:, :, :], ACT.Exp).then_inc(d_e, 1)

            def ff_high(b, s):
                slot = (NB + s) % 2
                a.wait_ge(w_in_s[slot], b * 8 + 16 * ((NB + s) // 2 + 1))
                a.wait_ge(tile_s, b * 2 + 2 * (NB + s - 1))
                a.activation(w_hi[:, slot], raw[:, slot], ACT.Copy).then_inc(hi_s, 1)

            with a.Fori(0, 2) as half:
                with a.Fori(0, 4) as i:
                    ff_high(half * 16 + i * 2, 0)
                    ff_high(half * 16 + i * 2, 1)
                    for s in range(4):
                        n = half * 16 + i * 4 + s
                        a.wait_ge(r_s, n + 2)
                        a.activation(rsq[:, s % 2, :], rel[:, s % 2, :], ACT.Square).then_inc(rq_s, 1)
                        a.wait_ge(rq_s, n + 1)
                        a.activation(aH[:, bass.ds(i * 4 + s, 1), :], rsq[:, s % 2, :].unsqueeze(1),
                                     ACT.Copy).then_inc(ah_s, 1)
                with a.Fori(0, 4) as i:
                    ff_high(half * 16 + i * 2 + 8, 0)
                    ff_high(half * 16 + i * 2 + 8, 1)
            norm(2)
            root()

        @block.vector
        def _(v):
            n_own = [0]

            def own(i):
                i.then_inc(own_v, 1)
                n_own[0] += 1
                v.wait_ge(own_v, n_own[0])

            roots = [0]

            def root(src, m):
                own(v.tensor_scalar(rstd[:, :], src, 1.0 / m, EPS, ALU.mult, ALU.add))
                v.reciprocal(rstd[:, :], rstd[:, :]).then_inc(ri_s, 1)
                roots[0] += 1
                v.wait_ge(ro_s, roots[0])

            def norm(n, col):
                v.wait_ge(ms_s, n + 1)
                root(mx[:, 5, :], D)

                def lo(k):
                    v.wait_ge(hhi_s, 8 * n + k + 1)
                    v.tensor_tensor(hL[:, k, :], hf[:, k % 2, :], hH[:, k, :].bitcast(F32),
                                    ALU.subtract).then_inc(hlo_s, 1)
                for k in range(KT):
                    if k >= 2:
                        v.wait_ge(hlo_s, 8 * n + k - 1)
                    v.scalar_tensor_tensor(out=hf[:, k % 2, :], in0=xT[:, k, :], scalar=vec[:, col + k:col + k + 1],
                                           in1=rstd[:, :], op0=ALU.mult, op1=ALU.mult).then_inc(hf_s, 1)
                    if k >= 1:
                        lo(k - 1)
                lo(KT - 1)

            def split(base_, src, hi, dst, m, scale=None):
                for k in range(m):
                    v.wait_ge(shi, base_ + k + 1)
                    if scale is None:
                        v.tensor_tensor(dst[:, k, :], src[:, k, :], hi[:, k, :].bitcast(F32),
                                        ALU.subtract).then_inc(slo, 1)
                    else:
                        v.scalar_tensor_tensor(out=dst[:, k, :], in0=src[:, k, :], scalar=scale,
                                               in1=hi[:, k, :].bitcast(F32), op0=ALU.mult,
                                               op1=ALU.subtract).then_inc(slo, 1)

            def clip(h):
                v.wait_ge(s_sc, h + 1)
                if h:
                    v.wait_ge(s_av, h)
                v.tensor_scalar(sw[:, :], mxf[:, 0:1280], 40.0, None, ALU.min).then_inc(s_cl, 1)
                v.wait_ge(s_ln, h + 1)
                v.tensor_tensor(sp[:, :], mxf[:, 0:1280], sw[:, :], ALU.max).then_inc(s_sp, 1)

            def biased(u):
                i, gq = u // 2, u % 2
                k0 = CHUNK if i == 0 else 0
                s4 = mxf[:, 0:1024].rearrange("p (h k) -> p h k", h=4)
                v.wait_ge(a_sc, u + 1)
                if u:
                    v.wait_ge(a_t, u)
                own(v.scalar_tensor_tensor(out=pr[:, :, CHUNK + k0:256], in0=s4[:, :, k0:KEYS], scalar=HD ** -0.5,
                                           in1=tbias[:, 4 * gq:4 * gq + 4, k0:KEYS], op0=ALU.mult, op1=ALU.add))
                own(v.tensor_reduce(small[:, 0:4], pr[:, :, CHUNK + k0:256], AX.X, ALU.max))
                own(v.tensor_tensor(small[:, 0:4], small[:, 0:4], small[:, 64 + 4 * gq:68 + 4 * gq], ALU.max))
                own(v.tensor_scalar(small[:, 4:8], small[:, 0:4], -1.0, None, ALU.mult))
                v.tensor_tensor(small[:, 8:12], small[:, 64 + 4 * gq:68 + 4 * gq], small[:, 4:8], ALU.add).then_inc(a_m, 1)

            gates = [0]
            for kind, k in STEPS:
                if kind == "load":
                    v.memset(small[:, :], 0.0).then_inc(own_v, 1)
                    n_own[0] += 1
                    v.wait_ge(v_tr, 1)
                    own(v.tensor_copy(vec[:, 0:V_ROWS], mx[:, 5, 0:V_ROWS]))
                    v.tensor_scalar(vec[:, V_CW:V_SSDN], vec[:, V_CW:V_SSDN], 0.5, None, ALU.mult).then_inc(v_cp, 1)
                    for t in range(KT):
                        v.wait_ge(x_tr, t + 1)
                        v.tensor_copy(xT[:, t, :], mx[:, t % 5, :]).then_inc(x_cp, 1)
                    v.wait_ge(b_f, 1)
                    v.tensor_copy(frow[0:SWA_HEADS, :], mx[0:SWA_HEADS, 4, 0:320]).then_inc(b_fc, 1)
                elif kind == "norm":
                    if k == 0:
                        v.wait_ge(v_cp, 1)
                    norm(k, V_MIX if k == 0 else V_FFN)
                elif kind == "block":
                    what, _, _, _, _, first = BLOCKS[k]
                    for s in range(2):
                        c, ct = 2 * k + s, first + s
                        src = pj[c % 2][:, :]
                        fs = free_s[c % 2]
                        v.wait_ge(tile_s, c + 1)
                        if what == "qs":
                            v.tensor_scalar(qs[:, ct, :], src, HD ** -0.5, None, ALU.mult).then_inc(fs, 1)
                        elif what == "ks":
                            v.tensor_copy(ks[:, ct, :], src).then_inc(fs, 1)
                        elif what == "vs":
                            v.tensor_copy(vsT[:, ct, :], src).then_inc(fs, 1)
                        elif what == "qa":
                            v.tensor_copy(qa[:, ct, :], src).then_inc(fs, 1)
                        elif what == "kava" and s == 0:
                            for g2 in range(2):
                                for half in range(2):
                                    o = v.tensor_copy(kd[64 * half:64 * half + 64, g2, :],
                                                      pj[c % 2][64 * g2:64 * g2 + 64, :])
                            o.then_inc(fs, 1)
                        elif what == "kava":
                            v.tensor_copy(vaT[:, :], src).then_inc(fs, 1)
                        elif what == "xbc":
                            if ct < 4:
                                v.wait_ge(vt_s, 4)
                            w = lambda j: vec[:, V_CW + 12 * j + ct:V_CW + 12 * j + ct + 1]
                            own(v.tensor_scalar(xs[:, ct, :], src, w(3), vec[:, V_CB + ct:V_CB + ct + 1],
                                                ALU.mult, ALU.add))
                            for j in range(3):
                                sh = 3 - j
                                ins_ = v.scalar_tensor_tensor(
                                    out=xs[:, ct, sh:T], in0=pj[c % 2][:, 0:T - sh], scalar=w(j),
                                    in1=xs[:, ct, sh:T], op0=ALU.mult, op1=ALU.add)
                                if j < 2:
                                    own(ins_)
                            ins_.then_inc(fs, 1)
                        elif what == "gate":
                            gates[0] += 1
                        elif what in ("u0", "u1", "u2"):
                            gi = gates[0] - 2 + s
                            v.wait_ge(gt_s, gi + 1)
                            dst = mg[:, ct, :] if what == "u2" else gu[:, :]
                            ins_ = v.scalar_tensor_tensor(out=dst, in0=gt[:, s, :], scalar=1.0, in1=src,
                                                          op0=ALU.add, op1=ALU.mult)
                            ins_.then_inc(fs, 1)
                            v.wait_ge(fs, c // 2 + 1 - extra(c))
                            if what == "u2":
                                v.tensor_copy(small[:, 79:80], small[:, 78:79]).then_inc(gu_s, 1)
                            else:
                                v.tensor_tensor(mg[:, ct, :], mg[:, ct, :], gu[:, :], ALU.add).then_inc(gu_s, 1)
                                v.wait_ge(gu_s, gi + 1)
                        elif what == "z":
                            v.wait_ge(zt_s, ct + 1)
                            v.scalar_tensor_tensor(out=gt[:, s, :], in0=gt[:, s, :], scalar=1.0, in1=src,
                                                   op0=ALU.add, op1=ALU.mult).then_inc(fs, 1)
                            v.wait_ge(fs, c // 2 + 1 - extra(c))
                            v.scalar_tensor_tensor(out=xs[:, ct, :], in0=gt[:, s, :], scalar=0.5, in1=xs[:, ct, :],
                                                   op0=ALU.mult, op1=ALU.mult).then_inc(zy_s, 1)
                        elif what == "merge":
                            v.tensor_tensor(xT[:, ct, :], xT[:, ct, :], src, ALU.add).then_inc(x1_s, 1)
                elif kind == "vs_turn":
                    for ct in range(4):
                        v.wait_ge(vt_s, ct + 1)
                        v.tensor_copy(vs[:, :, P * ct:P * ct + P],
                                      mx[:, ct, :].rearrange("p (t c) -> p t c", t=TT)).then_inc(vc_s, 1)
                elif kind == "va_turn":
                    v.wait_ge(vt_s, 5)
                    v.tensor_copy(va[:, :, :], mx[:, 4, :].rearrange("p (t c) -> p t c", t=TT)).then_inc(vc_s, 1)
                elif kind == "dt":
                    v.wait_ge(dws, 1)
                    v.tensor_tensor(wdtL[:, :, :], wdt[:, :, :], wdtH[:, :, :].bitcast(F32),
                                    ALU.subtract).then_inc(dw, 1)
                    v.wait_ge(dtm, 1)
                    v.wait_ge(row_in, 80)
                    x_, u_, w_, l_ = (dtt[:, j, :] for j in range(4))
                    own(v.tensor_tensor(x_.rearrange("p (t h) -> p t h", t=TT),
                                        mx[:, 5, 0:64].rearrange("p (t h) -> p t h", t=TT),
                                        dtb[:, :].unsqueeze(1).broadcast_to([P, TT, 16]), ALU.add))
                    own(v.tensor_scalar(u_, x_, -1.0, None, ALU.mult))
                    v.tensor_tensor(u_, u_, x_, ALU.min).then_inc(dtx, 1)
                    v.wait_ge(own_a, 2)
                    v.tensor_scalar(w_, u_, 1.0, None, ALU.add).then_inc(dtx, 1)
                    v.wait_ge(dte, 1)
                    m_, d_ = dta[:, :, :].rearrange("p t h -> p (t h)"), dtv[:, :, :].rearrange("p t h -> p (t h)")
                    own(v.tensor_scalar(m_, w_, 1.0, None, ALU.is_equal))
                    own(v.tensor_scalar(d_, w_, -1.0, None, ALU.add))
                    own(v.tensor_tensor(d_, d_, m_, ALU.add))
                    own(v.tensor_tensor(l_, l_, m_, ALU.add))
                    own(v.reciprocal(d_, d_))
                    own(v.tensor_tensor(l_, l_, u_, ALU.mult))
                    own(v.tensor_tensor(l_, l_, d_, ALU.mult))
                    own(v.scalar_tensor_tensor(out=d_, in0=x_, scalar=0.0, in1=l_, op0=ALU.max, op1=ALU.add))
                    v.scalar_tensor_tensor(out=dta[:, :, :], in0=dtv[:, :, :], scalar=-1.0,
                                           in1=nega[:, :].unsqueeze(1).broadcast_to([P, TT, 16]),
                                           op0=ALU.mult, op1=ALU.mult).then_inc(dtf, 1)
                elif kind == "sb_scores":
                    clip(0)
                elif kind == "sb_av":
                    if k % 2:
                        v.wait_ge(s_av, k + 1)
                        v.tensor_copy(qs[:, k // 2, :], mx[:, 3 + k // 2 % 2, :]).then_inc(s_o, 1)
                    if k + 1 < SB_HEADS:
                        clip(k + 1)
                elif kind == "bias":
                    v.wait_ge(b_t, 1)
                    own(v.tensor_copy(tbias[:, :, :].rearrange("p h k -> p (h k)"), mxf[:, 0:1536]))
                    own(v.tensor_copy(small[:, 64:72].rearrange("p (g two q) -> p g q two", g=2, two=2),
                                      sink[:, :].rearrange("p (g q two) -> p g q two", g=2, two=2)))
                    own(v.memset(tbias[0:64, :, P:KEYS], -3.0e38))
                    own(v.memset(tbias[64:128, :, 0:CHUNK], -3.0e38))
                    v.memset(pr[:, :, 0:CHUNK], 0.0).then_inc(b_tc, 1)
                elif kind == "silu":
                    v.wait_ge(own_v, n_own[0])
                    v.tensor_copy(small[:, 77:78], small[:, 78:79]).then_inc(si_s, CONV_T)
                    for c in range(CONV_T):
                        v.wait_ge(zp_s, c + 1)
                        v.scalar_tensor_tensor(out=xs[:, c, :], in0=gt[:, c % 2, :], scalar=1.0, in1=xs[:, c, :],
                                               op0=ALU.add, op1=ALU.mult).then_inc(th_s, 1)
                elif kind == "swa_scores":
                    biased(k) if k == 0 else None
                elif kind == "swa_turn":
                    v.wait_ge(a_e, k + 1)
                    k0 = P if k // 2 == 0 else CHUNK
                    own(v.tensor_tensor(small[:, 8:12], small[:, 8:12], small[:, 12:16], ALU.add))
                    own(v.reciprocal(small[:, 8:12], small[:, 8:12]))
                    v.tensor_tensor(pr[:, :, k0:256], pr[:, :, k0:256],
                                    small[:, 8:12].unsqueeze(2).broadcast_to([P, 4, 256 - k0]),
                                    ALU.mult).then_inc(a_n, 1)
                elif kind == "swa_pv":
                    if k + 1 < 8:
                        biased(k + 1)
                    i, gq = k // 2, k % 2
                    v.wait_ge(a_pv, k + 1)
                    v.tensor_copy(qa[:, 2 * gq:2 * gq + 2, P * i:P * i + P],
                                  mx[:, 4, 0:256].rearrange("p (q t) -> p q t", q=2)).then_inc(a_o, 1)
                elif kind == "split_c":
                    split(0, qs, oH, oL, 4)
                elif kind == "split_a":
                    split(4, qa, oH, oL, 4)
                elif kind == "split_b":
                    for g2 in range(2):
                        v.wait_ge(gms_s, g2 + 1)
                        root(mx[:, 4 + g2, :], 512)
                        for k2 in range(4 * g2, 4 * g2 + 4):
                            v.scalar_tensor_tensor(out=xs[:, k2, :], in0=xs[:, k2, :],
                                                   scalar=vec[:, V_SSDN + k2:V_SSDN + k2 + 1], in1=rstd[:, :],
                                                   op0=ALU.mult, op1=ALU.mult).then_inc(gr_s, 1)
                            if k2 % 4 == 3:
                                v.wait_ge(gr_s, k2 + 1)
                    split(8, xs, obH, obL, 8)
                elif kind == "split_m":
                    split(16, mg, mH, mL, 8, 0.5)
                elif kind == "ssd_prep":
                    v.wait_ge(d_pr, k + 1)
                    own(v.tensor_copy(small[:, 16:32], mx[:, 3, 0:16]))
                    own(v.tensor_tensor(small[:, 32:48], mx[:, 3, 16:32], small[:, 16:32], ALU.subtract))
                    v.tensor_copy(small[:, 48:64], mx[:, 3, 16:32]).then_inc(d_da, 1)
                    own(v.tensor_copy(bt[:, :, :].rearrange("p g n -> p (g n)"), mx[:, 2, 0:256]))
                    own(v.tensor_tensor(cbm[:, :, :], mx[:, 2, 256:512].rearrange("p (g t) -> p g t", g=2),
                                        tri[:, :].unsqueeze(1).broadcast_to([P, 2, P]), ALU.mult))
                    own(v.tensor_tensor(xd[:, :].rearrange("p (h e) -> p h e", h=16),
                                        mxf[:, 0:1024].rearrange("p (h e) -> p h e", h=16),
                                        dtv[:, k, :].unsqueeze(2).broadcast_to([P, 16, HD]), ALU.mult))
                    v.wait_ge(d_w, k + 1)
                    v.tensor_tensor(xw[:, :].rearrange("p (h e) -> p h e", h=16),
                                    xd[:, :].rearrange("p (h e) -> p h e", h=16),
                                    small[:, 32:48].unsqueeze(2).broadcast_to([P, 16, HD]),
                                    ALU.mult).then_inc(d_xw, 1)
                elif kind == "ssd_y":
                    c, r = k
                    n = 4 * c + r
                    v.wait_ge(d_ab, n + 1)
                    b = mx[:, 4 + r % 2, :].rearrange("p (h t) -> p h t", h=4)
                    for hh in range(4):
                        ins_ = v.tensor_scalar(mt[:, hh, :], b[:, hh, :], small[:, 16 + 4 * r + hh:17 + 4 * r + hh],
                                               0.0, ALU.subtract, ALU.min)
                    ins_.then_inc(d_d, 1)
                    v.wait_ge(d_e, n + 1)
                    v.tensor_tensor(mt[:, :, :], mt[:, :, :],
                                    cbm[:, r // 2, :].unsqueeze(1).broadcast_to([P, 4, P]), ALU.mult).then_inc(d_m, 1)
                    v.wait_ge(d_y, n + 1)
                    yd = mx[:, 3, 0:256].rearrange("p (q t) -> p q t", q=2)
                    yo = mx[:, 3, 256:512].rearrange("p (q t) -> p q t", q=2)
                    if c > 0:
                        own(v.tensor_tensor(t1[:, :, :], yo, e2[:, :, :], ALU.mult))
                        own(v.tensor_tensor(t1[:, :, :], t1[:, :, :], yd, ALU.add))
                    for q in range(2):
                        pt = 2 * r + q
                        src = t1[:, q, :] if c > 0 else yd[:, q, :]
                        tile = xs[:, pt, P * c:P * c + P]
                        v.scalar_tensor_tensor(out=tile, in0=tile, scalar=dsk[:, pt:pt + 1], in1=src,
                                               op0=ALU.mult, op1=ALU.add).then_inc(d_yc, 1)
                    v.wait_ge(d_yc, 2 * n + 2)
                elif kind == "ssd_state":
                    v.wait_ge(d_st, k + 1)
                    new = mxf[:, 0:1024]
                    if k == 0:
                        v.tensor_copy(st[:, :], new).then_inc(d_stc, 1)
                    else:
                        own(v.tensor_tensor(st[:, :].rearrange("p (h e) -> p h e", h=16),
                                            st[:, :].rearrange("p (h e) -> p h e", h=16),
                                            small[:, 48:64].unsqueeze(2).broadcast_to([P, 16, HD]), ALU.mult))
                        v.tensor_tensor(st[:, :], st[:, :], new, ALU.add).then_inc(d_stc, 1)
                    v.wait_ge(d_stc, k + 1)

            v.tensor_copy(small[:, 76:77], small[:, 78:79]).then_inc(r_s, 1)
            with v.Fori(0, 2) as half:
                with v.Fori(0, 4) as i:
                    for s in range(4):
                        n = half * 16 + i * 4 + s
                        v.wait_ge(tile_s, half * 32 + i * 4 + (2 * NB + s + 1))
                        v.wait_ge(rq_s, half * 16 + i * 4 + (s - 1)) if s >= 2 else None
                        v.tensor_scalar(rel[:, s % 2, :], pj[s % 2][:, :], 0.0, None, ALU.max).then_inc(r_s, 1)
                        v.wait_ge(ah_s, n + 1)
                        v.tensor_tensor(aL[:, bass.ds(i * 4 + s, 1), :], rsq[:, s % 2, :].unsqueeze(1),
                                        aH[:, bass.ds(i * 4 + s, 1), :].bitcast(F32), ALU.subtract).then_inc(al_s, 1)
                        v.wait_ge(al_s, n + 1)
                with v.Fori(0, 4) as i:
                    for s in range(2):
                        v.wait_ge(tile_s, half * 32 + i * 4 + (2 * NB + 16 + 3 + s))
                        o = xT[:, bass.ds(i * 2 + s, 1), :]
                        v.tensor_tensor(o, o, pj[s][:, :].unsqueeze(1), ALU.add).then_inc(x1_s, 1)
                        v.wait_ge(x1_s, half * 8 + i * 2 + (8 + s + 1))
            v.wait_ge(ms_s, 3)
            root(mx[:, 5, :], D)
            for k in range(KT):
                v.scalar_tensor_tensor(out=yout[:, k, :], in0=xT[:, k, :], scalar=vec[:, V_FIN + k:V_FIN + k + 1],
                                       in1=rstd[:, :], op0=ALU.mult, op1=ALU.mult).then_inc(hf_s, 1)
            for n in range(8):
                v.wait_ge(yt_s, n + 1)
                t, hh = n // 2, n % 2
                v.tensor_copy(yrow[:, t, 512 * hh:512 * hh + 512], mx[:, n % 4, :]).then_inc(yc_s, 1)

        @block.tensor
        def _(pe):
            def bank_free(c):
                if c < 2:
                    return
                what, p = BLOCKS[(c - 2) // 2][0], c - 2
                if what == "gate":
                    gi = sum(1 for b in BLOCKS[:p // 2] if b[0] == "gate") * 2 + p % 2
                    pe.wait_ge(gt_s, gi + 1)
                elif what == "merge":
                    pe.wait_ge(x1_s, BLOCKS[p // 2][5] + p % 2 + 1)
                else:
                    pe.wait_ge(free_s[p % 2], p // 2 + 1 - extra(p))

            def product(dst, slot, s, hi, lo, kts, k0=0, start=True, stop=True):
                for k in range(kts):
                    wh = w_hi[:, slot, k, P * s:P * s + P]
                    wl = w_lo[:, slot, k, P * s:P * s + P]
                    pe.matmul(dst, wh, hi[:, k0 + k, :], start=start and k == 0, stop=False)
                    pe.matmul(dst, wh, lo[:, k0 + k, :], start=False, stop=False)
                    m = pe.matmul(dst, wl, hi[:, k0 + k, :], start=False, stop=stop and k == kts - 1)
                return m

            pe.wait_ge(cst, 1)
            turned = [0]
            cols = [0, 512, 1024, 896]
            for kind, k in STEPS:
                if kind == "load":
                    pe.wait_ge(vec_in, 96)
                    pe.transpose(mx[:, 5, 0:V_ROWS], vrow[0:V_ROWS, :], ident[0:V_ROWS, 0:V_ROWS]).then_inc(v_tr, 1)
                    pe.wait_ge(x_in, 64)
                    for t in range(KT):
                        if t >= 5:
                            pe.wait_ge(x_cp, t - 4)
                        for j in range(TT):
                            m = pe.transpose(mx[:, t % 5, P * j:P * j + P], xin[:, j, P * t:P * t + P], ident[:, :])
                        m.then_inc(x_tr, 1)
                    pe.wait_ge(rel_in, 32)
                    pe.wait_ge(x_cp, 5)
                    pe.matmul(mx[0:SWA_HEADS, 4, 0:320], relb[0:BUCKETS, :], onehot[0:BUCKETS, :],
                              start=True, stop=True).then_inc(b_f, 1)
                elif kind == "norm":
                    if k == 0:
                        pe.wait_ge(v_cp, 1)
                    for t in range(KT):
                        pe.wait_ge(sq_s, 8 * k + t + 1)
                        m = pe.matmul(mx[:, 5, :], ones[:, :], sq[:, t, :], start=t == 0, stop=t == KT - 1)
                    m.then_inc(ms_s, 1)
                    pe.wait_ge(hlo_s, 8 * k + 8)
                elif kind == "block":
                    what, _, _, kts, _, first = BLOCKS[k]
                    hi, lo = hH, hL
                    if what in ("u0", "u2"):
                        pe.wait_ge(slo, 4 if what == "u2" else 8)
                        hi, lo = oH, oL
                    elif what == "u1":
                        pe.wait_ge(slo, 16)
                        hi, lo = obH, obL
                    elif what == "merge":
                        pe.wait_ge(slo, 24)
                        hi, lo = mH, mL
                    pe.wait_ge(lo_s, k + 1)
                    for s in range(2):
                        c = 2 * k + s
                        bank_free(c)
                        product(pj[c % 2][:, :], k % 2, s, hi, lo, kts).then_inc(tile_s, 1)
                        if what == "z" and first + s == 7:
                            for t in range(KT):
                                pe.wait_ge(ysq_s, t + 1)
                                m = pe.matmul(mx[:, 4 + t // 4, :], ones[:, :], ysq[:, t, :],
                                              start=t % 4 == 0, stop=t % 4 == 3)
                                if t % 4 == 3:
                                    m.then_inc(gms_s, 1)
                elif kind == "vs_turn":
                    for ct in range(4):
                        cc = tile_of("vs", ct)
                        pe.wait_ge(free_s[cc % 2], cc // 2 + 1 - extra(cc))
                        for t in range(TT):
                            m = pe.transpose(mx[:, ct, P * t:P * t + P], vsT[:, ct, P * t:P * t + P], ident[:, :])
                        m.then_inc(vt_s, 1)
                elif kind == "va_turn":
                    cc = tile_of("kava", 1)
                    pe.wait_ge(free_s[cc % 2], cc // 2 + 1 - extra(cc))
                    pe.wait_ge(s_o, 4)
                    for t in range(TT):
                        m = pe.transpose(mx[:, 4, P * t:P * t + P], vaT[:, P * t:P * t + P], ident[:, :])
                    m.then_inc(vt_s, 1)
                elif kind == "dt":
                    pe.wait_ge(dw, 1)
                    for t in range(TT):
                        for kt in range(KT):
                            for n, (l, r) in enumerate(((hH, wdtH), (hL, wdtH), (hH, wdtL))):
                                m = pe.matmul(mx[:, 5, 16 * t:16 * t + 16], l[:, kt, P * t:P * t + P], r[:, kt, :],
                                              start=kt == 0 and n == 0, stop=kt == KT - 1 and n == 2)
                    m.then_inc(dtm, 1)
                elif kind in ("sb_scores", "sb_av"):
                    if kind == "sb_av":
                        r0 = 64 * (k % 2)
                        pe.wait_ge(s_wm, 2 * (k + 1))
                        if k >= 4 and k % 2 == 0:
                            pe.wait_ge(s_o, k // 2 - 1)
                        for j in range(TT):
                            m = pe.matmul(mx[r0:r0 + 64, 3 + k // 2 % 2, P * j:T], vs[:, j, HD * k:HD * k + HD],
                                          sw[:, cols[j]:cols[j] + T - P * j], start=j == 0, stop=j == TT - 1,
                                          skip_group_check=True)
                        m.then_inc(s_av, 1)
                    else:
                        cc = tile_of("ks", 3)
                        pe.wait_ge(free_s[cc % 2], cc // 2 + 1 - extra(cc))
                        pe.wait_ge(vc_s, 4)
                    h = 0 if kind == "sb_scores" else k + 1
                    if h < SB_HEADS:
                        r0, pt = 64 * (h % 2), h // 2
                        if h:
                            pe.wait_ge(s_w, h)
                        for j in range(TT):
                            m = pe.matmul(mxf[:, cols[j]:cols[j] + T - P * j], ks[r0:r0 + 64, pt, P * j:P * j + P],
                                          qs[r0:r0 + 64, pt, P * j:T], start=j < 3, stop=False, skip_group_check=True)
                        m.then_inc(s_sc, 1)
                elif kind == "sb_cum":
                    pe.wait_ge(s_spm, 2 * (k + 1))
                    for j in range(TT):
                        for i in range(j, TT):
                            dst = mxf[:, cols[j] + P * (i - j):cols[j] + T - P * j]
                            m = pe.matmul(dst, (neg_tri if i == j else neg_one)[:, :],
                                          sp[:, cols[i]:cols[i] + T - P * i], start=False, stop=i == TT - 1,
                                          skip_group_check=True)
                    m.then_inc(s_cu, 1)
                elif kind == "bias":
                    pe.wait_ge(trev_in, 64)
                    pe.wait_ge(vc_s, 5)
                    tr = trev[:, :, :].rearrange("p h k -> p (h k)")
                    for j in range(3):
                        m = pe.matmul(mx[:, j, :], flip[:, :], tr[:, 512 * j:512 * j + 512], start=True, stop=True)
                    m.then_inc(b_t, 1)
                elif kind == "swa_scores":
                    i, gq = k // 2, k % 2
                    k0 = CHUNK if i == 0 else 0
                    if k == 0:
                        cc = tile_of("kava", 1)
                        pe.wait_ge(free_s[cc % 2], cc // 2 + 1 - extra(cc))
                        pe.wait_ge(b_tc, 1)
                    else:
                        pe.wait_ge(a_m, k)
                    for hh in range(4):
                        h = 4 * gq + 2 * (hh % 2) + hh // 2
                        r0 = 64 * (h % 2)
                        m = pe.matmul(mxf[:, 256 * hh + k0:256 * hh + KEYS], qa[r0:r0 + 64, h // 2, P * i:P * i + P],
                                      kd[r0:r0 + 64, gq, P * i - CHUNK + k0:P * i + P], start=True, stop=True)
                    m.then_inc(a_sc, 1)
                elif kind == "swa_turn":
                    pe.wait_ge(a_n, k + 1)
                    if k:
                        pe.wait_ge(a_tc, k)
                    for part in range(1 if k // 2 == 0 else 0, 2):
                        for hh in range(4):
                            m = pe.transpose(mx[:, 2 + part, P * hh:P * hh + P],
                                             pr[:, hh, P * part:P * part + P], ident[:, :])
                    m.then_inc(a_t, 1)
                elif kind == "swa_pv":
                    i, gq = k // 2, k % 2
                    pe.wait_ge(a_tc, k + 1)
                    if k:
                        pe.wait_ge(a_o, k)
                    for par in range(2):
                        for part in range(1 if i == 0 else 0, 2):
                            m = pe.matmul(mx[64 * par:64 * par + 64, 4, 0:256],
                                          va[:, i - 1 + part, HD * gq:HD * gq + HD],
                                          pT[:, part, 256 * par:256 * par + 256],
                                          start=part == 0 or i == 0, stop=part == 1)
                    m.then_inc(a_pv, 1)
                elif kind == "ssd_prep":
                    c = k
                    if c == 0:
                        pe.wait_ge(dtf, 1)
                        pe.wait_ge(th_s, CONV_T)
                        pe.wait_ge(a_o, 8)
                    else:
                        pe.wait_ge(d_stc, c)
                        pe.wait_ge(d_yc, 8 * c)
                    for t in range(8):
                        pe.transpose(mxf[:, P * t:P * t + P], xs[:, t, P * c:P * c + P], ident[:, :])
                    for g2 in range(2):
                        pe.transpose(mx[:, 2, P * g2:P * g2 + P], xs[:, 8 + g2, P * c:P * c + P], ident[:, :])
                    for g2 in range(2):
                        pe.matmul(mx[:, 2, 256 + P * g2:256 + P * g2 + P], xs[:, 8 + g2, P * c:P * c + P],
                                  xs[:, 10 + g2, P * c:P * c + P], start=True, stop=True)
                    pe.matmul(mx[:, 3, 0:16], tri[:, :], dta[:, c, :], start=True, stop=True)
                    pe.matmul(mx[:, 3, 16:32], ones[:, :], dta[:, c, :], start=True, stop=True).then_inc(d_pr, 1)
                elif kind == "ssd_y":
                    c, r = k
                    n = 4 * c + r
                    if r == 0:
                        cumsum(pe, c, 0)
                    if r < 3:
                        cumsum(pe, c, r + 1)
                    pe.wait_ge(d_m, n + 1)
                    pe.wait_ge(d_xw, c + 1)
                    if n:
                        pe.wait_ge(d_yc, 2 * n)
                    for hh in range(4):
                        h = 4 * r + hh
                        par, q = hh % 2, hh // 2
                        m = pe.matmul(mx[64 * par:64 * par + 64, 3, P * q:P * q + P], xd[:, HD * h:HD * h + HD],
                                      mt[:, hh, :], start=True, stop=True)
                    if c > 0:
                        for q in range(2):
                            pt = 2 * r + q
                            m = pe.matmul(mx[:, 3, 256 + P * q:256 + P * q + P], st[:, P * pt:P * pt + P],
                                          xs[:, 10 + r // 2, P * c:P * c + P], start=True, stop=True)
                    m.then_inc(d_y, 1)
                elif kind == "ssd_state":
                    for g2 in range(2):
                        m = pe.matmul(mx[:, g2, :], bt[:, g2, :], xw[:, 512 * g2:512 * g2 + 512],
                                      start=True, stop=True)
                    m.then_inc(d_st, 1)

            with pe.Fori(0, 2) as half:
                with pe.Fori(0, 4) as i:
                    for s in range(4):
                        if s % 2 == 0:
                            pe.wait_ge(lo_s, half * 16 + i * 2 + (NB + s // 2 + 1))
                        if s >= 2:
                            pe.wait_ge(r_s, half * 16 + i * 4 + s)
                        else:
                            pe.wait_ge(r_s, half * 16 + i * 4 + 1)
                            pe.wait_ge(x1_s, half * 8 + 8)
                        product(pj[s % 2][:, :], (NB + s // 2) % 2, s % 2, hH, hL, KT).then_inc(tile_s, 1)
                with pe.Fori(0, 4) as i:
                    pe.wait_ge(al_s, half * 16 + 16)
                    pe.wait_ge(x1_s, half * 8 + i * 2 + 8)
                    for b in range(2):
                        pe.wait_ge(lo_s, half * 16 + i * 2 + (NB + 8 + b + 1))
                        for s in range(2):
                            product(pj[s][:, :], (NB + b) % 2, s, aH, aL, KT, k0=8 * b, start=b == 0,
                                    stop=b == 1).then_inc(tile_s, 1)
            for t in range(KT):
                pe.wait_ge(sq_s, 16 + t + 1)
                m = pe.matmul(mx[:, 5, :], ones[:, :], sq[:, t, :], start=t == 0, stop=t == KT - 1)
            m.then_inc(ms_s, 1)
            pe.wait_ge(hf_s, 24)
            for n in range(8):
                t, hh = n // 2, n % 2
                if n >= 4:
                    pe.wait_ge(yc_s, n - 3)
                for j in range(4):
                    m = pe.transpose(mx[:, n % 4, P * j:P * j + P], yout[:, 4 * hh + j, P * t:P * t + P], ident[:, :])
                m.then_inc(yt_s, 1)



def relative_onehot():
    r = np.arange(320) - (P + CHUNK - 1)
    nb = BUCKETS // 2
    exact = nb // 2
    n = np.abs(r)
    large = exact + (np.log(np.maximum(n, 1) / exact) / np.log(MAX_DIST / exact) * (nb - exact)).astype(np.int32)
    b = np.where(r > 0, nb, 0) + np.where(n < exact, n, np.minimum(large, nb - 1))
    return (np.arange(BUCKETS)[:, None] == b[None, :]).astype(np.float32)


INS = ["x", "norm_mix_w", "w_in", "swa_sinks", "rel_bias", "conv_w", "conv_b", "dt_bias", "a_log", "d_skip",
       "ssd_norm_w", "w_out", "w_merge", "norm_ffn_w", "w_ff1", "w_ff2", "final_norm_w"]


def kernel(**inputs):
    import concourse.bacc as bacc
    from concourse.bass_utils import run_bass_kernel_spmd

    nc = bacc.Bacc("TRN2", target_bir_lowering=False, num_devices=1)
    arrays = {n: np.ascontiguousarray(inputs[n]) for n in INS}
    arrays["onehot"] = relative_onehot()
    args = {n: nc.dram_tensor(n, a.shape, mybir.dt.from_np(a.dtype), kind="ExternalInput").ap()
            for n, a in arrays.items()}
    out = nc.dram_tensor("out", (1, T, D), F32, kind="ExternalOutput").ap()
    build(nc, args, out)
    r = run_bass_kernel_spmd(nc, [arrays], core_ids=[0])
    return r.results[0]["out"]
```

```python
from contextlib import ExitStack

import concourse.bass as bass
import numpy as np
from concourse import mybir

F32 = mybir.dt.float32
F32R = mybir.dt.float32r
ALU = mybir.AluOpType
ACT = mybir.ActivationFunctionType
AX = mybir.AxisListType

P = 128
T = 512
TT = T // P
D = 1024
KT = D // P
HD = 64
EPS = 1e-6
KIB = 1024

SWA_HEADS, KV_HEADS, CHUNK, BUCKETS, MAX_DIST = 8, 2, 64, 32, 128
KEYS = P + CHUNK
REL = P + KEYS - 1
SB_HEADS = 8
SSD_HEADS = 16
CONV = 4
CONV_T = 12
DFF = 4096

C_QA, C_KA, C_Z, C_XBC, C_DT, C_QS, C_KS, C_VS, C_G = 0, 512, 768, 1792, 3328, 3344, 3856, 4368, 4880
BC = 256
V_MIX, V_CW, V_CB, V_SSDN, V_FFN, V_FIN, V_ROWS = 0, 8, 56, 68, 76, 84, 92


def plan():
    blocks, fused = [], set()

    def block(kind, matrix, row, kts, col, first):
        blocks.append((kind, matrix, row, kts, col, first))
        return [("tile", 2 * len(blocks) - 2), ("tile", 2 * len(blocks) - 1)]

    def w_in(kind, col, n):
        return sum([block(kind, "w_in", 0, KT, col + BC * i, 2 * i) for i in range(n)], [])

    def gate(b, i):
        return block("gate", "w_in", 0, KT, C_G + b * D + BC * i, 2 * i)

    def branch_out(b, row, kts, i):
        if i == 0:
            fused.add(len(blocks))
        return block("u%d" % b, "w_out", row, kts, BC * i, 2 * i)

    def branch(b, row, kts):
        return sum([gate(b, i) + branch_out(b, row, kts, i) for i in range(D // BC)], [])

    def weave(tiles, others):
        out, at = [], 0
        for i, s in enumerate(tiles):
            out.append(s)
            upto = (i + 1) * len(others) // len(tiles)
            out += others[at:upto]
            at = upto
        return sum([o if isinstance(o, list) else [o] for o in out + others[at:]], [])

    sb = [("sb_scores", 0), ("sb_scores", 1)]
    for h in range(SB_HEADS):
        sb.append(("sb_cum", h))
        sb.append([("sb_av", h)] + ([("sb_scores", h + 2)] if h + 2 < SB_HEADS else []))
    swa = [[("p_zero", 0), ("swa_scores", 0)]]
    for u in range(8):
        swa.append([("swa_scores", u + 1)] if u < 7 else [])
        swa.append([("swa_turn", u), ("silu", u + (u + 1) // 2)])
        swa.append([("swa_pv", u)] + ([("silu", 3 * u // 2 + 1)] if u % 2 == 0 else []))
    ssd = [("ssd_prep", 0), ("ssd_sum", 0)]
    for c in range(TT):
        for r in range(4):
            n = 4 * c + r
            ssd.append([("ssd_sum", n + 1), ("ssd_y", (c, r))] if n < 15 else ("ssd_y", (c, r)))
            if r == 0 and c < TT - 1:
                ssd.append(("ssd_state", c))
        if c < TT - 1:
            ssd.append(("ssd_prep", c + 1))

    fused.add(0)
    steps = [("load", 0), ("norm", 0)]
    steps += w_in("qs", C_QS, 2) + [("bias", 0)] + w_in("ks", C_KS, 2) + [("dt", 0)]
    steps += w_in("vs", C_VS, 2) + [("vs_turn", 0)]
    steps += weave(w_in("qa", C_QA, 2) + w_in("kava", C_KA, 1) + w_in("xbc", C_XBC, 6), sb)
    steps += gate(2, 0)[:1] + [("va_turn", 0), ("decay", 0), ("split_c", 0), ("tile", 2 * len(blocks) - 1)]
    rest = branch_out(2, 1536, 4, 0)
    for i in range(1, 4):
        rest += gate(2, i) + branch_out(2, 1536, 4, i)
    steps += weave(rest, swa)
    steps += gate(0, 0) + [("split_a", 0)]
    rest = branch_out(0, 0, 4, 0)
    for i in range(1, 4):
        rest += gate(0, i) + branch_out(0, 0, 4, i)
    steps += weave(rest, ssd)
    steps += w_in("z", C_Z, 4)
    g11 = gate(1, 0) + [("y_norm", 0)] + gate(1, 1)
    steps += g11[:-1] + [("y_spread", 0), ("split_b", 0)] + g11[-1:]
    steps += branch_out(1, 512, 8, 0) + gate(1, 2) + branch_out(1, 512, 8, 1)
    steps += gate(1, 3) + branch_out(1, 512, 8, 2) + branch_out(1, 512, 8, 3)
    steps += [("split_m", 0)]
    fused.add(len(blocks))
    for i in range(4):
        steps += block("merge", "w_merge", 0, KT, BC * i, 2 * i)
    steps += [("norm", 1)]
    return blocks, steps, fused


BLOCKS, STEPS, FUSED = plan()
NB = len(BLOCKS)


def gate_of(c):
    kind, ct = BLOCKS[c // 2][0], BLOCKS[c // 2][5] + c % 2
    if kind != "gate":
        return {"u2": 0, "u0": 8, "u1": 16}[kind] + ct
    return {2: 0, 0: 8, 1: 16}[(BLOCKS[c // 2][4] - C_G) // D] + ct


def tile_of(kind, i=0):
    return [2 * n for n, b in enumerate(BLOCKS) if b[0] == kind][i // 2] + i % 2


def build(nc, ins, out):
    with ExitStack() as ctx:
        def sem(name):
            return ctx.enter_context(nc.semaphore(name))

        base = -(-nc.sbuf_base // 32) * 32
        arena = ctx.enter_context(nc.sbuf_tensor("arena", [P, 207 * KIB // 4], F32))
        del arena

        def at(name, kib, shape, dt=F32):
            return nc.alloc_sbuf_tensor_at(name, [P] + shape, dt, offset=base + int(kib * KIB))

        raw = at("raw", 0, [2, KT, BC])
        w_hi = at("w_hi", 16, [2, KT, BC], F32R)
        w_lo = at("w_lo", 32, [2, KT, BC], F32R)
        xT = at("xT", 48, [KT, T])
        hH = at("hH", 64, [KT, T], F32R)
        hL = at("hL", 80, [KT, T], F32R)
        ident = at("ident", 96, [P])
        flip = at("flip", 96.5, [P])
        tri = at("tri", 97, [P])
        ones = at("ones", 97.5, [P])
        neg_tri = at("neg_tri", 98, [P])
        neg_one = at("neg_one", 98.5, [P])
        vec = at("vec", 99, [96])
        dtb = at("dtb", 99.5, [16])
        nega = at("nega", 99.5625, [16])
        sink = at("sink", 99.625, [8])
        dsk = at("dsk", 99.65625, [8])
        small = at("small", 99.6875, [80])
        stat = at("stat", 99.375, [32])
        dta = at("dta", 100, [TT, 16])
        dtv = at("dtv", 100.25, [TT, 16])
        dtt = at("dtt", 100.5, [4, TT * 16])
        acum = at("acum", 101.5, [TT, 16])
        dec = at("dec", 100.5, [2, TT, 16])
        neg_triR = at("neg_triR", 102, [P], F32R)
        neg_oneR = at("neg_oneR", 102.5, [P], F32R)
        triR = at("triR", 103, [P], F32R)
        dtaH = at("dtaH", 103.5, [TT, 16], F32R)
        dtaL = at("dtaL", 103.75, [TT, 16], F32R)
        tbias = at("tbias", 104, [SWA_HEADS, KEYS])
        xin = at("xin", 110, [TT, D])
        sq = at("sq", 174, [KT, T])
        hf = at("hf", 190, [4, T])
        vrow = at("vrow", 144, [P])
        onehot = at("onehot", 144.5, [320])
        relb = at("relb", 146, [8])
        frow = at("frow", 146.25, [320])
        wdt = at("wdt", 148, [KT, 16])
        wdtH = at("wdtH", 148.5, [KT, 16], F32R)
        wdtL = at("wdtL", 149, [KT, 16], F32R)
        trev = at("trev", 136, [SWA_HEADS, KEYS])
        qs = at("qs", 110, [4, T])
        ks = at("ks", 118, [4, T])
        vs = at("vs", 126, [TT, 512])
        sp = at("sp", 134, [1280])
        spH = at("spH", 184, [1280], F32R)
        spL = at("spL", 189, [1280], F32R)
        sw = [at("sw0", 139, [1280]), at("sw1", 194, [1280])]
        qa = at("qa", 144, [4, T])
        kd = at("kd", 152, [KV_HEADS, T])
        va = at("va", 156, [TT, P])
        xs = at("xs", 158, [12, T])
        vsT = at("vsT", 158, [4, T])
        vaT = at("vaT", 182, [T])
        pr = [at("pr0", 118, [4, 256]), at("pr1", 110, [4, 256])]
        cth = at("cth", 114, [2, T])
        pT = at("pT", 122, [2, T])
        oH = at("oH", 126, [4, T], F32R)
        oL = at("oL", 134, [4, T], F32R)
        mg = at("mg", 184, [KT, T])
        gt = at("gt", 200, [2, T])
        gu = at("gu", 204, [T])
        xd = at("xd", 110, [D])
        xw = at("xw", 114, [D])
        bt = at("bt", 118, [2, P])
        cbm = at("cbm", 119, [2, P])
        st = [at("st0", 120, [D]), at("st1", 152, [D])]
        mt = [at("mt0", 124, [4, P]), at("mt1", 156, [4, P])]
        e2 = [at("e20", 104, [2, P]), at("e21", 105, [2, P])]
        t1 = at("t1", 106, [2, P])
        gt1 = at("gt1", 174, [4, T])
        obH = at("obH", 110, [KT, T], F32R)
        obL = at("obL", 126, [KT, T], F32R)
        ysq = at("ysq", 142, [KT, T])
        mH = at("mH", 142, [KT, T], F32R)
        mL = at("mL", 158, [KT, T], F32R)
        aH = at("aH", 110, [16, T], F32R)
        aL = at("aL", 142, [16, T], F32R)
        rel = at("rel", 194, [2, T])
        rsq = at("rsq", 198, [2, T])
        wrow = at("wrow", 202, [D])
        yrow = at("yrow", 110, [TT, D])

        pj = [ctx.enter_context(nc.psum_tensor("pj%d" % i, [P, 512], F32)) for i in range(2)]
        mx = ctx.enter_context(nc.psum_tensor("mx", [P, 6, 512], F32))
        mxf = mx[:, :, :].rearrange("p b n -> p (b n)")
        scr = nc.dram_tensor("rel_rows", [SWA_HEADS, 320], F32).ap()

        x_in = [sem("x_in%d" % i) for i in range(TT)]
        vec_in, row_in, rel_in = sem("vec_in"), sem("row_in"), sem("rel_in")
        scr_out, trev_in, dt_in, done = sem("scr_out"), sem("trev_in"), sem("dt_in"), sem("done")
        w_in_s = [sem("w_in%d" % i) for i in range(2)]
        hi_s, lo_s, tile_s = sem("w_hi_made"), sem("w_lo_made"), sem("tile_done")
        free_s = [sem("pj_read%d" % i) for i in range(2)]
        cst = sem("constants")
        v_tr, v_cp, x_tr, x_cp = sem("vec_turned"), sem("vec_ready"), sem("x_turned"), sem("x_ready")
        sq_s, ms_s, hf_s, hhi_s, hlo_s = sem("squares"), sem("mean_sq"), sem("normed"), sem("h_hi"), sem("h_lo")
        x1_s = sem("residual")
        ri_s, ro_s, bc_s = sem("root_in"), sem("root_out"), sem("rstd_spread")
        x_cpa, glo_s, wr_in = sem("x_ready_odd"), sem("h_lo_odd"), sem("final_w_in")
        s_hi, s_lo, d_ac, d_dh = sem("sb_stay_hi"), sem("sb_stay_lo"), sem("ssd_cumsums"), sem("ssd_dta_parts")
        cR, y_a, y_m = sem("constants_r"), sem("row_scaled"), sem("row_out_pool")
        own_t, y1_s, y2_s, gsq_s = sem("row_out_vector"), sem("rows_turned0"), sem("rows_turned1"), sem("squares_summed")
        v_set, dtu, d_dl = sem("stat_set"), sem("dt_exp_made"), sem("ssd_dta_low")
        vt_s, vc_s = sem("v_turned"), sem("v_copied")
        dws, dw, dtm, dtx, dte, dtf = (sem("dt_w_hi"), sem("dt_w_lo"), sem("dt_product"), sem("dt_raw"),
                                       sem("dt_exp"), sem("dt_ready"))
        b_f, b_fc, b_t, b_tc = sem("bias_rows"), sem("bias_copied"), sem("bias_flipped"), sem("bias_ready")
        zp_s, th_s, si_s = sem("p_zeroed"), sem("conv_tanh"), sem("conv_silu")
        s_sc, s_cl, s_ln, s_sp, s_spm = (sem("sb_scored"), sem("sb_clipped"), sem("sb_softplus"),
                                         sem("sb_stay"), sem("sb_stay_masked"))
        s_cu, s_w, s_wm, s_av, s_o = (sem("sb_summed"), sem("sb_weights"), sem("sb_weights_masked"),
                                      sem("sb_product"), sem("sb_out"))
        a_sc, a_p, a_m, a_e, a_n = (sem("swa_scored"), sem("swa_biased"), sem("swa_max"), sem("swa_exp"),
                                    sem("swa_normed"))
        a_t, a_tc, a_pv, a_o = sem("swa_turned"), sem("swa_pt"), sem("swa_product"), sem("swa_out")
        d_pr, d_da, d_w, d_xw = sem("ssd_prepared"), sem("ssd_decays"), sem("ssd_decay_exp"), sem("ssd_xw")
        d_ab, d_d, d_e, d_m, d_y, d_yc = (sem("ssd_cumsum"), sem("ssd_diff"), sem("ssd_exp"), sem("ssd_m"),
                                          sem("ssd_product"), sem("ssd_y"))
        d_st, d_stc = sem("ssd_states"), sem("ssd_state")
        shi, slo = sem("split_hi"), sem("split_lo")
        gt_s, gu_s, zt_s, zy_s, ysq_s, gms_s, gr_s = (sem("gate_tanh"), sem("gate_used"), sem("z_tanh"),
                                                      sem("y_gated"), sem("y_squares"), sem("y_mean_sq"),
                                                      sem("y_rstd"))
        r_s, rq_s, ah_s, al_s = sem("relu"), sem("relu_sq"), sem("act_hi"), sem("act_lo")
        yt_s, yc_s = sem("y_turned"), sem("y_row")
        own_a, own_v, own_g = sem("scalar_chain"), sem("vector_chain"), sem("pool_chain")

        block = ctx.enter_context(nc.Block())

        matrices = {k: ins[k][0] for k in ("w_in", "w_out", "w_merge", "w_ff1", "w_ff2")}
        SPLIT = {"split_c": 0, "split_a": 4, "split_b": 8, "split_m": 16}
        cols = [0, 512, 1024, 896]
        ffb = [pj[0][:, :], pj[1][:, :], mx[:, 0, :], mx[:, 1, :]]
        outb = [ffb, [mx[:, 2, :], mx[:, 3, :], mx[:, 5, :], mx[:, 4, :]]]

        def read_count(c):
            return sum(1 for p in range(c % 2, c + 1, 2) if BLOCKS[p // 2][0] not in ("gate", "merge"))

        def bank(c):
            return pj[c % 2][:, :]

        @block.sync
        def _(sy):
            for t in range(TT):
                sy.dma_start(xin[:, t, :], ins["x"][0, P * t:P * t + P, :]).then_inc(x_in[t], 16)
            for row, end, src in ((V_MIX, V_CW, ins["norm_mix_w"][0]), (V_CB, V_SSDN, ins["conv_b"][0]),
                                  (V_SSDN, V_FFN, ins["ssd_norm_w"][0]), (V_FFN, V_FIN, ins["norm_ffn_w"][0]),
                                  (V_FIN, V_ROWS, ins["final_norm_w"])):
                sy.dma_start(vrow[row:end, :], src.rearrange("(a p) -> a p", p=P)).then_inc(vec_in, 16)
            sy.dma_start(vrow[V_CW:V_CB, :], ins["conv_w"][0].rearrange("k (a p) -> (k a) p", p=P)).then_inc(vec_in, 16)

            def load_block(n):
                _, matrix, row, kts, col, _ = BLOCKS[n]
                if n >= 2:
                    sy.wait_ge(lo_s, n - 1)
                src = matrices[matrix][row:row + P * kts, col:col + BC].rearrange("(k p) c -> p k c", p=P)
                sy.dma_start(raw[:, n % 2, 0:kts, :], src).then_inc(w_in_s[n % 2], 16)

            load_block(0)
            sy.dma_start(onehot[0:BUCKETS, :], ins["onehot"]).then_inc(rel_in, 16)
            sy.dma_start(relb[0:BUCKETS, :], ins["rel_bias"]).then_inc(rel_in, 16)
            load_block(1)

            def on_all(row, n):
                return row[0:1, :].broadcast_to([P, n])

            sy.dma_start(dtb[:, :], on_all(ins["dt_bias"], 16)).then_inc(row_in, 16)
            sy.dma_start(nega[:, :], on_all(ins["a_log"], 16)).then_inc(row_in, 16)
            sy.dma_start(sink[:, :], on_all(ins["swa_sinks"], 8)).then_inc(row_in, 16)
            for half in range(2):
                src = ins["d_skip"].rearrange("a (q two) -> a two q", two=2)[0:1, half, :]
                sy.dma_start(dsk[64 * half:64 * half + 64, :], src.broadcast_to([64, 8]),
                             allow_slow_non_contiguous=True).then_inc(row_in, 16)
            src = matrices["w_in"][:, C_DT:C_DT + 16].rearrange("(k p) c -> p k c", p=P)
            sy.dma_start(wdt[:, :, :], src).then_inc(dt_in, 16)
            sy.wait_ge(b_fc, 1)
            sy.dma_start(scr, frow[0:SWA_HEADS, :]).then_inc(scr_out, 16)
            sy.wait_ge(scr_out, 16)
            for n in range(4):
                src = bass.AP(tensor=scr.tensor, offset=320 * (4 * (n // 2) + n % 2), ap=[[1, P], [640, 2], [1, KEYS]])
                sy.dma_start(trev[:, 2 * n:2 * n + 2, :], src).then_inc(trev_in, 16)
            for n in range(2, NB):
                load_block(n)
            sy.wait_ge(gu_s, 24)
            sy.dma_start(wrow[:, :], ins["final_norm_w"].rearrange("(a n) -> a n", a=1).broadcast_to([P, D])
                         ).then_inc(wr_in, 16)
            with sy.Fori(0, 2) as half:
                with sy.Fori(0, 4) as i:
                    for s in range(2):
                        sy.wait_ge(lo_s, half * 16 + i * 2 + (NB + s - 1))
                        src = matrices["w_ff1"][:, bass.ds(half * 2048 + i * 512 + s * BC, BC)]
                        sy.dma_start(raw[:, (NB + s) % 2, :, :], src.rearrange("(k p) c -> p k c", p=P)
                                     ).then_inc(w_in_s[(NB + s) % 2], 16)
                with sy.Fori(0, 4) as i:
                    for s in range(2):
                        sy.wait_ge(lo_s, half * 16 + i * 2 + (NB + 8 + s - 1))
                        src = matrices["w_ff2"][bass.ds(half * 2048 + s * 1024, 1024), bass.ds(i * BC, BC)]
                        sy.dma_start(raw[:, (NB + s) % 2, :, :], src.rearrange("(k p) c -> p k c", p=P)
                                     ).then_inc(w_in_s[(NB + s) % 2], 16)
            for t in range(TT):
                sy.wait_ge(own_t, t + 2)
                if t:
                    sy.wait_ge(y_m, t)
                sy.dma_start(out[0, P * t:P * t + P, :], yrow[:, t, :]).then_inc(done, 16)
            sy.wait_ge(done, 16 * TT)

        @block.gpsimd
        def _(g):
            n_own = [0]

            def own(i):
                i.then_inc(own_g, 1)
                n_own[0] += 1
                g.wait_ge(own_g, n_own[0])

            def sel(t, op, fill, mult, step, start=0):
                own(g.affine_select(out=t, in_=t, compare_op=op, fill=fill, base=start,
                                    pattern=[[step, P]], channel_multiplier=mult))

            own(g.memset(ident[:, :], 0.0))
            sel(ident[:, :], ALU.not_equal, 1.0, 1, -1)
            own(g.memset(flip[:, :], 0.0))
            sel(flip[:, :], ALU.not_equal, 1.0, 1, 1, -(P - 1))
            own(g.memset(ones[:, :], 1.0))
            own(g.memset(tri[:, :], 1.0))
            sel(tri[:, :], ALU.is_ge, 0.0, -1, 1)
            own(g.memset(neg_one[:, :], -1.0))
            own(g.memset(neg_tri[:, :], -1.0))
            sel(neg_tri[:, :], ALU.is_ge, 0.0, 1, -1)
            g.memset(ident[0:1, 0:1], 1.0).then_inc(cst, 1)

            def low(n):
                kts = BLOCKS[n][3]
                g.wait_ge(hi_s, n + 1)
                g.tensor_tensor(w_lo[:, n % 2, 0:kts, :], raw[:, n % 2, 0:kts, :],
                                w_hi[:, n % 2, 0:kts, :].bitcast(F32), ALU.subtract).then_inc(lo_s, 1)

            def diag(t, s):
                v3 = t[:, 0:1152].rearrange("p (a b) -> p a b", b=128)[:, 0:9:4, :]
                v1 = t[:, 896:1024]
                g.affine_select(out=v3, in_=v3, compare_op=ALU.is_gt, fill=0.0, base=0,
                                pattern=[[0, 3], [1, P]], channel_multiplier=-1).then_inc(s, 1)
                g.affine_select(out=v1, in_=v1, compare_op=ALU.is_gt, fill=0.0, base=0,
                                pattern=[[1, P]], channel_multiplier=-1).then_inc(s, 1)

            for kind, k in STEPS:
                if kind == "tile" and k % 2 == 0 and k // 2 + 1 < NB:
                    low(k // 2 + 1)
                elif kind == "norm":
                    if k == 0:
                        low(0)
                    for t in range(1, KT, 2):
                        g.wait_ge(hhi_s, 8 * k + t + 1)
                        g.tensor_tensor(hL[:, t, :], hf[:, t % 4, :], hH[:, t, :].bitcast(F32),
                                        ALU.subtract).then_inc(glo_s, 1)
                    if k == 1:
                        pass
                elif kind == "sb_scores":
                    g.wait_ge(s_sp, k + 1)
                    diag(sp, s_spm)
                elif kind == "sb_av":
                    g.wait_ge(s_w, k + 1)
                    diag(sw[k % 2], s_wm)
            with g.Fori(0, 2) as half:
                for ph in range(2):
                    with g.Fori(0, 4) as i:
                        for s in range(2):
                            g.wait_ge(hi_s, half * 16 + i * 2 + (NB + 8 * ph + s + 1))
                            g.tensor_tensor(w_lo[:, (NB + s) % 2], raw[:, (NB + s) % 2],
                                            w_hi[:, (NB + s) % 2].bitcast(F32), ALU.subtract).then_inc(lo_s, 1)
            for t in range(1, 6):
                g.wait_ge(sq_s, 12 + t + 1)
                if t > 1:
                    g.wait_ge(own_g, n_own[0])
                n_own[0] += 1
                g.tensor_tensor(sq[:, 0, :], sq[:, 0, :], sq[:, t, :], ALU.add).then_inc(own_g, 1)
            g.wait_ge(own_g, n_own[0])
            g.memset(small[:, 60:61], 0.0).then_inc(gsq_s, 1)
            g.wait_ge(wr_in, 16)
            for t in range(1, TT):
                g.wait_ge(y_a, t)
                o = yrow[:, t, 512:1024]
                g.tensor_tensor(o, o, wrow[:, 512:1024], ALU.mult).then_inc(y_m, 1)

        @block.scalar
        def _(a):
            n_own = [0]

            def own(i):
                i.then_inc(own_a, 1)
                n_own[0] += 1
                a.wait_ge(own_a, n_own[0])

            def high(n):
                kts = BLOCKS[n][3]
                a.wait_ge(w_in_s[n % 2], 16 * (n // 2 + 1))
                if n >= 2:
                    a.wait_ge(tile_s, 2 * (n - 1))
                a.activation(w_hi[:, n % 2, 0:kts, :], raw[:, n % 2, 0:kts, :], ACT.Copy).then_inc(hi_s, 1)

            roots = [0]

            def root(n):
                roots[0] += 1
                a.wait_ge(ri_s, roots[0])
                a.activation(stat[:, 0:n], stat[:, 0:n], ACT.Sqrt).then_inc(ro_s, 1)

            def square(k, count):
                a.wait_ge(x1_s, count)
                a.activation(sq[:, k, :], xT[:, k, :], ACT.Square).then_inc(sq_s, 1)

            def split(src, dst, m, scale=1.0):
                for k in range(m):
                    a.activation(dst[:, k, :], src[:, k, :], ACT.Copy, scale=scale).then_inc(shi, 1)

            def y_square(t):
                a.wait_ge(zy_s, t + 1)
                a.activation(ysq[:, t, :], xs[:, t, :], ACT.Square).then_inc(ysq_s, 1)

            for kind, k in STEPS:
                if kind == "load":
                    a.wait_ge(v_set, 1)
                    own(a.activation(stat[:, 30:31], stat[:, 30:31], ACT.Sqrt))
                    for t in range(TT):
                        a.wait_ge(x_in[t], 16)
                        a.activation(sq[:, 0:2, :], xin[:, t, :].rearrange("p (a b) -> p a b", a=2), ACT.Square,
                                     accum_out=stat[:, t:t + 1]).then_inc(sq_s, 1)
                        a.wait_ge(sq_s, t + 1)
                    a.wait_ge(x_tr, 1)
                    for t in range(1, KT, 2):
                        a.activation(xT[:, t, :], mx[:, t, :] if t < 6 else pj[1][:, :], ACT.Copy).then_inc(x_cpa, 1)
                elif kind == "norm":
                    if k == 1:
                        square(7, 8)
                    root(4)
                    if k == 0:
                        high(0)
                    for t in range(KT):
                        a.wait_ge(hf_s, 8 * k + t + 1)
                        a.activation(hH[:, t, :], hf[:, t % 4, :], ACT.Copy).then_inc(hhi_s, 1)
                elif kind == "tile":
                    if k % 2 == 0 and k // 2 + 1 < NB:
                        high(k // 2 + 1)
                    what, ct = BLOCKS[k // 2][0], BLOCKS[k // 2][5] + k % 2
                    if what == "gate":
                        a.wait_ge(tile_s, k + 1)
                        gi = gate_of(k)
                        if 2 <= gi < 16:
                            a.wait_ge(gu_s, gi - 1)
                        elif gi >= 20:
                            a.wait_ge(gu_s, gi - 3)
                        dst = gt[:, ct % 2, :] if gi < 16 else gt1[:, ct % 4, :]
                        a.activation(dst, bank(k), ACT.Tanh, scale=0.5).then_inc(gt_s, 1)
                    elif what == "z":
                        a.wait_ge(tile_s, k + 1)
                        a.wait_ge(*((zy_s, ct - 1) if ct >= 2 else (gu_s, 16)))
                        a.activation(gt[:, ct % 2, :], bank(k), ACT.Tanh, scale=0.5).then_inc(zt_s, 1)
                        if ct >= 1:
                            y_square(ct - 1)
                    elif what == "merge":
                        if ct == 0:
                            own(a.activation(stat[:, 30:31], stat[:, 30:31], ACT.Sqrt))
                        else:
                            square(ct - 1, ct)
                elif kind == "dt":
                    a.wait_ge(dt_in, 16)
                    a.activation(wdtH[:, :, :], wdt[:, :, :], ACT.Copy).then_inc(dws, 1)
                    a.wait_ge(row_in, 80)
                    own(a.activation(nega[:, :], nega[:, :], ACT.Exp))
                    a.wait_ge(dtx, 1)
                    a.activation(dtt[:, 1, :], dtt[:, 1, :], ACT.Exp).then_inc(dtu, 1)
                    a.wait_ge(dtx, 2)
                    a.activation(dtt[:, 3, :], dtt[:, 2, :], ACT.Ln).then_inc(dte, 1)
                    a.wait_ge(dtf, 1)
                    a.activation(dtaH[:, :, :], dta[:, :, :], ACT.Copy).then_inc(d_dh, 1)
                elif kind == "sb_scores":
                    a.wait_ge(s_cl, k + 1)
                    own(a.activation(sw[k % 2][:, :], sw[k % 2][:, :], ACT.Exp))
                    a.activation(sw[k % 2][:, :], sw[k % 2][:, :], ACT.Ln, bias=1.0).then_inc(s_ln, 1)
                    if k == 0:
                        a.wait_ge(s_spm, 2)
                        a.activation(spH[:, :], sp[:, :], ACT.Copy).then_inc(s_hi, 1)
                elif kind == "sb_cum":
                    if k + 1 < SB_HEADS:
                        a.wait_ge(s_spm, 2 * (k + 2))
                        a.wait_ge(s_cu, k + 1)
                        a.activation(spH[:, :], sp[:, :], ACT.Copy).then_inc(s_hi, 1)
                elif kind == "sb_av":
                    a.wait_ge(s_cu, k + 1)
                    b = 1536 * (k % 2)
                    a.activation(sw[k % 2][:, :], mxf[:, b:b + 1280], ACT.Exp).then_inc(s_w, 1)
                elif kind == "silu":
                    cc = tile_of("xbc", k)
                    a.wait_ge(free_s[cc % 2], read_count(cc))
                    a.wait_ge(*((th_s, k - 1) if k >= 2 else (slo, 4)))
                    a.activation(cth[:, k % 2, :], xs[:, k, :], ACT.Tanh).then_inc(zp_s, 1)
                elif kind == "swa_scores":
                    a.wait_ge(a_m, k + 1)
                    k0, o, p_ = (P if k // 2 == 0 else CHUNK), 16 * (k % 2), pr[k % 2]
                    for hh in range(4):
                        own(a.activation(p_[:, hh, k0:256], p_[:, hh, k0:256], ACT.Exp,
                                         bias=small[:, o + 4 + hh:o + 5 + hh],
                                         accum_out=small[:, o + 12 + hh:o + 13 + hh]))
                    a.activation(small[:, o + 8:o + 12], small[:, o + 8:o + 12], ACT.Exp).then_inc(a_e, 1)
                elif kind == "swa_turn":
                    a.wait_ge(a_t, k + 1)
                    if k:
                        a.wait_ge(a_pv, k)
                    lo = 1 if k // 2 == 0 else 0
                    a.activation(pT[:, lo:2, :], mx[:, 2 + lo:4, :], ACT.Copy).then_inc(a_tc, 1)
                elif kind == "split_c":
                    a.wait_ge(s_o, SB_HEADS)
                    split(qs, oH, 4)
                elif kind == "split_a":
                    a.wait_ge(a_o, 8)
                    a.wait_ge(tile_s, tile_of("u2", 7) + 1)
                    split(qa, oH, 4)
                elif kind == "y_norm":
                    y_square(7)
                    root(8)
                elif kind == "split_b":
                    for t in range(KT):
                        a.wait_ge(gr_s, t + 1)
                        a.activation(obH[:, t, :], xs[:, t, :], ACT.Copy).then_inc(shi, 1)
                elif kind == "split_m":
                    a.wait_ge(gu_s, 24)
                    split(mg, mH, 8, 0.5)
                elif kind == "decay":
                    a.wait_ge(d_da, 1)
                    a.activation(dec[:, :, :, :], dec[:, :, :, :], ACT.Exp).then_inc(d_w, 1)
                elif kind == "ssd_sum":
                    b = mx[:, 4 + k % 2, :].rearrange("p (q two t) -> p q two t", two=2, t=P)
                    a.wait_ge(d_d, k + 1)
                    if k >= 4:
                        if k >= 6:
                            a.wait_ge(d_yc, 2 * (k - 1))
                        a.activation(e2[k % 2][0:64, :, :], b[0:64, :, 0, :], ACT.Exp).then_inc(own_a, 1)
                        a.activation(e2[k % 2][64:128, :, :], b[64:128, :, 1, :], ACT.Exp).then_inc(own_a, 1)
                        n_own[0] += 2
                    a.activation(mt[k % 2][:, :, :], mt[k % 2][:, :, :], ACT.Exp).then_inc(d_e, 1)

            def ff_high(m, p):
                slot = (NB + p) % 2
                a.wait_ge(w_in_s[slot], m * 16 + 16 * ((NB + p) // 2 + 1))
                a.wait_ge(tile_s, m * 4 + 2 * (NB + p - 1))
                a.activation(w_hi[:, slot], raw[:, slot], ACT.Copy).then_inc(hi_s, 1)

            with a.Fori(0, 2) as half:
                ff_high(half * 8, 0)
                with a.Fori(0, 4) as i:
                    for s in range(4):
                        if s % 2 == 0:
                            ff_high(half * 8 + i + s // 2, 1 - s // 2)
                        n = half * 16 + i * 4 + s
                        a.wait_ge(r_s, n + 5)
                        a.activation(rsq[:, s % 2, :], rel[:, s % 2, :], ACT.Square).then_inc(rq_s, 1)
                        a.wait_ge(rq_s, n + 1)
                        a.activation(aH[:, bass.ds(i * 4 + s, 1), :], rsq[:, s % 2, :].unsqueeze(1),
                                     ACT.Copy).then_inc(ah_s, 1)
                with a.Fori(0, 3) as i:
                    ff_high(half * 8 + i + 4, 1)
                    ff_high(half * 8 + i + 5, 0)
                ff_high(half * 8 + 7, 1)
            for k in range(KT):
                square(k, 16 + k + 1)
            root(4)
            a.wait_ge(ro_s, 4)
            for t in range(1, TT):
                a.wait_ge(y2_s, t + 1)
                a.activation(yrow[:, t, 512:1024], outb[1][t], ACT.Copy, scale=stat[:, t:t + 1]).then_inc(y_a, 1)

        @block.vector
        def _(v):
            n_own = [0]

            def own(i):
                i.then_inc(own_v, 1)
                n_own[0] += 1
                v.wait_ge(own_v, n_own[0])

            roots = [0]

            def mean(src, n, m):
                own(v.tensor_scalar(stat[:, 0:n], src, 1.0 / m, EPS, ALU.mult, ALU.add))
                v.reciprocal(stat[:, 0:n], stat[:, 0:n]).then_inc(ri_s, 1)

            def norm(n, col, rs):
                def lo(k):
                    v.wait_ge(hhi_s, 8 * n + k + 1)
                    v.tensor_tensor(hL[:, k, :], hf[:, k % 4, :], hH[:, k, :].bitcast(F32),
                                    ALU.subtract).then_inc(hlo_s, 1)
                for k in range(KT):
                    if k >= 4:
                        v.wait_ge(*((glo_s, 4 * n + k // 2 - 1) if k % 2 else (hlo_s, 4 * n + k // 2 - 1)))
                    v.scalar_tensor_tensor(out=hf[:, k % 4, :], in0=xT[:, k, :], scalar=vec[:, col + k:col + k + 1],
                                           in1=rs, op0=ALU.mult, op1=ALU.mult).then_inc(hf_s, 1)
                    if k % 2:
                        lo(k - 1)

            def split(start, src, hi, dst, m, scale=None):
                for k in range(m):
                    v.wait_ge(shi, start + k + 1)
                    if scale is None:
                        v.tensor_tensor(dst[:, k, :], src[:, k, :], hi[:, k, :].bitcast(F32),
                                        ALU.subtract).then_inc(slo, 1)
                    else:
                        v.scalar_tensor_tensor(out=dst[:, k, :], in0=src[:, k, :], scalar=scale,
                                               in1=hi[:, k, :].bitcast(F32), op0=ALU.mult,
                                               op1=ALU.subtract).then_inc(slo, 1)

            def by_head(t):
                return t.rearrange("p (h e) -> p h e", h=16)

            def over_head(t):
                return t.unsqueeze(2).broadcast_to([P, 16, HD])

            for kind, k in STEPS:
                if kind == "load":
                    v.memset(stat[:, :], 1.0).then_inc(v_set, 1)
                    own(v.memset(small[:, :], 0.0))
                    v.wait_ge(cst, 1)
                    for dst, src in ((neg_triR, neg_tri), (neg_oneR, neg_one), (triR, tri)):
                        v.tensor_copy(dst[:, :], src[:, :]).then_inc(cR, 1)
                    v.wait_ge(v_tr, 1)
                    own(v.tensor_copy(vec[:, 0:V_ROWS], pj[1][:, 0:V_ROWS]))
                    v.tensor_scalar(vec[:, V_CW:V_SSDN], vec[:, V_CW:V_SSDN], 0.5, None, ALU.mult).then_inc(v_cp, 1)
                    v.wait_ge(sq_s, 4)
                    mean(stat[:, 0:4], 4, D)
                    v.wait_ge(x_tr, 1)
                    for t in range(0, KT, 2):
                        v.tensor_copy(xT[:, t, :], mx[:, t, :] if t < 6 else pj[0][:, :]).then_inc(x_cp, 1)
                elif kind == "norm":
                    if k == 0:
                        v.wait_ge(v_cp, 1)
                        v.wait_ge(x_cp, 4)
                        v.wait_ge(x_cpa, 4)
                    else:
                        v.wait_ge(ms_s, 1)
                        mean(mx[:, 5, 0:4], 4, D)
                    v.wait_ge(bc_s, 1 if k == 0 else 3)
                    norm(k, V_MIX if k == 0 else V_FFN, mx[:, 0 if k == 0 else 4, :])
                    if k == 0:
                        v.wait_ge(b_f, 1)
                        v.tensor_copy(frow[0:SWA_HEADS, :], mx[0:SWA_HEADS, 4, 0:320]).then_inc(b_fc, 1)
                elif kind == "tile":
                    what, ct = BLOCKS[k // 2][0], BLOCKS[k // 2][5] + k % 2
                    src, fs = bank(k), free_s[k % 2]
                    if what == "gate":
                        continue
                    v.wait_ge(tile_s, k + 1)
                    if what == "qs":
                        v.tensor_scalar(qs[:, ct, :], src, HD ** -0.5, None, ALU.mult).then_inc(fs, 1)
                    elif what in ("ks", "vs", "qa"):
                        dst = {"ks": ks, "vs": vsT, "qa": qa}[what]
                        v.tensor_copy(dst[:, ct, :], src).then_inc(fs, 1)
                    elif what == "kava" and ct == 0:
                        for g2 in range(2):
                            for half in range(2):
                                o = v.tensor_copy(kd[64 * half:64 * half + 64, g2, :],
                                                  pj[k % 2][64 * g2:64 * g2 + 64, :])
                        o.then_inc(fs, 1)
                    elif what == "kava":
                        v.tensor_copy(vaT[:, :], src).then_inc(fs, 1)
                    elif what == "xbc":
                        if ct < 4:
                            v.wait_ge(vt_s, 4)
                        w = [vec[:, V_CW + 12 * j + ct:V_CW + 12 * j + ct + 1] for j in range(CONV)]
                        own(v.tensor_scalar(xs[:, ct, :], src, w[3], vec[:, V_CB + ct:V_CB + ct + 1],
                                            ALU.mult, ALU.add))
                        for j in range(3):
                            sh = 3 - j
                            add = v.scalar_tensor_tensor(
                                out=xs[:, ct, sh:T], in0=pj[k % 2][:, 0:T - sh], scalar=w[j],
                                in1=xs[:, ct, sh:T], op0=ALU.mult, op1=ALU.add)
                            if j < 2:
                                own(add)
                        add.then_inc(fs, 1)
                    elif what in ("u0", "u1", "u2"):
                        gi = gate_of(k)
                        v.wait_ge(gt_s, gi + 1)
                        gate = gt[:, ct % 2, :] if gi < 16 else gt1[:, ct % 4, :]
                        v.scalar_tensor_tensor(out=mg[:, ct, :] if gi < 8 else gu[:, :], in0=gate, scalar=1.0,
                                               in1=src, op0=ALU.add, op1=ALU.mult).then_inc(fs, 1)
                        v.wait_ge(fs, read_count(k))
                        if gi < 8:
                            v.tensor_copy(small[:, 79:80], small[:, 78:79]).then_inc(gu_s, 1)
                        else:
                            v.tensor_tensor(mg[:, ct, :], mg[:, ct, :], gu[:, :], ALU.add).then_inc(gu_s, 1)
                            v.wait_ge(gu_s, gi + 1)
                    elif what == "z":
                        v.wait_ge(zt_s, ct + 1)
                        v.scalar_tensor_tensor(out=gt[:, ct % 2, :], in0=gt[:, ct % 2, :], scalar=1.0, in1=src,
                                               op0=ALU.add, op1=ALU.mult).then_inc(fs, 1)
                        v.wait_ge(fs, read_count(k))
                        v.scalar_tensor_tensor(out=xs[:, ct, :], in0=gt[:, ct % 2, :], scalar=0.5, in1=xs[:, ct, :],
                                               op0=ALU.mult, op1=ALU.mult).then_inc(zy_s, 1)
                    elif what == "merge":
                        v.tensor_tensor(xT[:, ct, :], xT[:, ct, :], src, ALU.add).then_inc(x1_s, 1)
                elif kind == "vs_turn":
                    for ct in range(4):
                        v.wait_ge(vt_s, ct + 1)
                        v.tensor_copy(vs[:, :, P * ct:P * ct + P],
                                      mx[:, ct, :].rearrange("p (t c) -> p t c", t=TT)).then_inc(vc_s, 1)
                elif kind == "va_turn":
                    v.wait_ge(vt_s, 5)
                    v.tensor_copy(va[:, :, :], mx[:, 4, :].rearrange("p (t c) -> p t c", t=TT)).then_inc(vc_s, 1)
                elif kind == "dt":
                    v.wait_ge(dws, 1)
                    v.tensor_tensor(wdtL[:, :, :], wdt[:, :, :], wdtH[:, :, :].bitcast(F32),
                                    ALU.subtract).then_inc(dw, 1)
                    v.wait_ge(dtm, 1)
                    v.wait_ge(row_in, 80)
                    x_, u_, w_, l_ = (dtt[:, j, :] for j in range(4))
                    own(v.tensor_tensor(x_.rearrange("p (t h) -> p t h", t=TT),
                                        mx[:, 5, 0:64].rearrange("p (t h) -> p t h", t=TT),
                                        dtb[:, :].unsqueeze(1).broadcast_to([P, TT, 16]), ALU.add))
                    own(v.tensor_scalar(u_, x_, -1.0, None, ALU.mult))
                    v.tensor_tensor(u_, u_, x_, ALU.min).then_inc(dtx, 1)
                    v.wait_ge(dtu, 1)
                    v.tensor_scalar(w_, u_, 1.0, None, ALU.add).then_inc(dtx, 1)
                    v.wait_ge(dte, 1)
                    m_, d_ = dta[:, :, :].rearrange("p t h -> p (t h)"), dtv[:, :, :].rearrange("p t h -> p (t h)")
                    own(v.tensor_scalar(m_, w_, 1.0, None, ALU.is_equal))
                    own(v.tensor_scalar(d_, w_, -1.0, None, ALU.add))
                    own(v.tensor_tensor(d_, d_, m_, ALU.add))
                    own(v.tensor_tensor(l_, l_, m_, ALU.add))
                    own(v.reciprocal(d_, d_))
                    own(v.tensor_tensor(l_, l_, u_, ALU.mult))
                    own(v.tensor_tensor(l_, l_, d_, ALU.mult))
                    own(v.scalar_tensor_tensor(out=d_, in0=x_, scalar=0.0, in1=l_, op0=ALU.max, op1=ALU.add))
                    v.scalar_tensor_tensor(out=dta[:, :, :], in0=dtv[:, :, :], scalar=-1.0,
                                           in1=nega[:, :].unsqueeze(1).broadcast_to([P, TT, 16]),
                                           op0=ALU.mult, op1=ALU.mult).then_inc(dtf, 1)
                    v.wait_ge(d_dh, 1)
                    v.tensor_tensor(dtaL[:, :, :], dta[:, :, :], dtaH[:, :, :].bitcast(F32),
                                    ALU.subtract).then_inc(d_dl, 1)
                elif kind == "sb_scores":
                    b = 1536 * (k % 2)
                    v.wait_ge(s_sc, k + 1)
                    v.tensor_scalar(sw[k % 2][:, :], mxf[:, b:b + 1280], 40.0, None, ALU.min).then_inc(s_cl, 1)
                    v.wait_ge(s_ln, k + 1)
                    if k:
                        v.wait_ge(s_hi, k)
                    v.tensor_tensor(sp[:, :], mxf[:, b:b + 1280], sw[k % 2][:, :], ALU.max).then_inc(s_sp, 1)
                    if k == 0:
                        v.wait_ge(s_hi, 1)
                        v.tensor_tensor(spL[:, :], sp[:, :], spH[:, :].bitcast(F32), ALU.subtract).then_inc(s_lo, 1)
                        v.wait_ge(s_lo, 1)
                elif kind == "sb_cum":
                    if k + 1 < SB_HEADS:
                        v.wait_ge(s_hi, k + 2)
                        v.tensor_tensor(spL[:, :], sp[:, :], spH[:, :].bitcast(F32), ALU.subtract).then_inc(s_lo, 1)
                        v.wait_ge(s_lo, k + 2)
                elif kind == "sb_av":
                    r0 = 64 * (k % 2)
                    v.wait_ge(s_av, k + 1)
                    v.tensor_copy(qs[r0:r0 + 64, k // 2, :], mx[r0:r0 + 64, 3 * (k % 2), :]).then_inc(s_o, 1)
                elif kind == "bias":
                    v.wait_ge(b_t, 1)
                    own(v.tensor_copy(tbias[:, :, :].rearrange("p h k -> p (h k)"), mxf[:, 0:1536]))
                    v.wait_ge(row_in, 80)
                    own(v.tensor_copy(small[:, 64:72].rearrange("p (g two q) -> p g q two", g=2, two=2),
                                      sink[:, :].rearrange("p (g q two) -> p g q two", g=2, two=2)))
                    own(v.memset(tbias[0:64, :, P:KEYS], -3.0e38))
                    v.memset(tbias[64:128, :, 0:CHUNK], -3.0e38).then_inc(b_tc, 1)
                elif kind == "p_zero":
                    for j in range(2):
                        own(v.memset(pr[j][:, :, 0:CHUNK], 0.0))
                elif kind == "silu":
                    v.wait_ge(zp_s, k + 1)
                    v.scalar_tensor_tensor(out=xs[:, k, :], in0=cth[:, k % 2, :], scalar=1.0, in1=xs[:, k, :],
                                           op0=ALU.add, op1=ALU.mult).then_inc(th_s, 1)
                elif kind == "swa_scores":
                    i, gq, o, p_ = k // 2, k % 2, 16 * (k % 2), pr[k % 2]
                    k0 = CHUNK if i == 0 else 0
                    s4 = mxf[:, 0:1024].rearrange("p (h k) -> p h k", h=4)
                    snk = small[:, 64 + 4 * gq:68 + 4 * gq]
                    v.wait_ge(a_sc, k + 1)
                    if k >= 2:
                        v.wait_ge(a_t, k - 1)
                    v.scalar_tensor_tensor(out=p_[:, :, CHUNK + k0:256], in0=s4[:, :, k0:KEYS], scalar=HD ** -0.5,
                                           in1=tbias[:, 4 * gq:4 * gq + 4, k0:KEYS], op0=ALU.mult,
                                           op1=ALU.add).then_inc(a_p, 1)
                    v.wait_ge(a_p, k + 1)
                    own(v.tensor_reduce(small[:, o:o + 4], p_[:, :, CHUNK + k0:256], AX.X, ALU.max))
                    own(v.tensor_tensor(small[:, o:o + 4], small[:, o:o + 4], snk, ALU.max))
                    own(v.tensor_scalar(small[:, o + 4:o + 8], small[:, o:o + 4], -1.0, None, ALU.mult))
                    v.tensor_tensor(small[:, o + 8:o + 12], snk, small[:, o + 4:o + 8], ALU.add).then_inc(a_m, 1)
                elif kind == "swa_turn":
                    o, k0, p_ = 16 * (k % 2), (P if k // 2 == 0 else CHUNK), pr[k % 2]
                    v.wait_ge(a_e, k + 1)
                    own(v.tensor_tensor(small[:, o + 8:o + 12], small[:, o + 8:o + 12], small[:, o + 12:o + 16],
                                        ALU.add))
                    own(v.reciprocal(small[:, o + 8:o + 12], small[:, o + 8:o + 12]))
                    v.tensor_tensor(p_[:, :, k0:256], p_[:, :, k0:256],
                                    small[:, o + 8:o + 12].unsqueeze(2).broadcast_to([P, 4, 256 - k0]),
                                    ALU.mult).then_inc(a_n, 1)
                elif kind == "swa_pv":
                    i, gq = k // 2, k % 2
                    v.wait_ge(a_pv, k + 1)
                    v.tensor_copy(qa[:, 2 * gq:2 * gq + 2, P * i:P * i + P],
                                  mx[:, 4, 0:256].rearrange("p (q t) -> p q t", q=2)).then_inc(a_o, 1)
                elif kind == "split_c":
                    split(SPLIT[kind], qs, oH, oL, 4)
                elif kind == "split_a":
                    split(SPLIT[kind], qa, oH, oL, 4)
                elif kind == "y_norm":
                    v.wait_ge(gms_s, 1)
                    mean(mx[:, 5, 0:8], 8, 512)
                elif kind == "split_b":
                    v.wait_ge(bc_s, 2)
                    for t in range(KT + 2):
                        if t < KT:
                            v.scalar_tensor_tensor(out=xs[:, t, :], in0=xs[:, t, :],
                                                   scalar=vec[:, V_SSDN + t:V_SSDN + t + 1], in1=mx[:, 3 + t // 4, :],
                                                   op0=ALU.mult, op1=ALU.mult).then_inc(gr_s, 1)
                        if t >= 2:
                            v.wait_ge(shi, SPLIT[kind] + t - 1)
                            v.tensor_tensor(obL[:, t - 2, :], xs[:, t - 2, :], obH[:, t - 2, :].bitcast(F32),
                                            ALU.subtract).then_inc(slo, 1)
                elif kind == "split_m":
                    split(SPLIT[kind], mg, mH, mL, 8, 0.5)
                elif kind == "decay":
                    v.wait_ge(d_ac, 1)
                    own(v.tensor_copy(acum[:, :, :].rearrange("p t h -> p (t h)"), mx[:, 5, 0:64]))
                    own(v.tensor_tensor(dec[:, 0, :, :].rearrange("p t h -> p (t h)"), mx[:, 5, 64:128],
                                        acum[:, :, :].rearrange("p t h -> p (t h)"), ALU.subtract))
                    v.tensor_copy(dec[:, 1, :, :].rearrange("p t h -> p (t h)"), mx[:, 5, 64:128]).then_inc(d_da, 1)
                elif kind == "ssd_prep":
                    v.wait_ge(d_pr, k + 1)
                    v.wait_ge(d_w, 1)
                    if k:
                        v.wait_ge(d_y, 4 * k)
                    own(v.tensor_copy(bt[:, :, :].rearrange("p g n -> p (g n)"), mx[:, 2, 0:256]))
                    own(v.tensor_tensor(cbm[:, :, :], mx[:, 2, 256:512].rearrange("p (g t) -> p g t", g=2),
                                        tri[:, :].unsqueeze(1).broadcast_to([P, 2, P]), ALU.mult))
                    own(v.tensor_tensor(by_head(xd[:, :]), by_head(mxf[:, 0:1024]), over_head(dtv[:, k, :]), ALU.mult))
                    v.tensor_tensor(by_head(xw[:, :]), by_head(xd[:, :]), over_head(dec[:, 0, k, :]),
                                    ALU.mult).then_inc(d_xw, 1)
                elif kind == "ssd_sum":
                    c, r = k // 4, k % 4
                    v.wait_ge(d_ab, k + 1)
                    if k >= 2:
                        v.wait_ge(d_y, k - 1)
                    b = mx[:, 4 + k % 2, :].rearrange("p (h t) -> p h t", h=4)
                    for hh in range(4):
                        o = v.tensor_scalar(mt[k % 2][:, hh, :], b[:, hh, :], acum[:, c, 4 * r + hh:4 * r + hh + 1],
                                            0.0, ALU.subtract, ALU.min)
                    o.then_inc(d_d, 1)
                elif kind == "ssd_y":
                    c, r = k
                    n = 4 * c + r
                    m_ = mt[n % 2]
                    v.wait_ge(d_e, n + 1)
                    v.tensor_tensor(m_[:, :, :], m_[:, :, :],
                                    cbm[:, r // 2, :].unsqueeze(1).broadcast_to([P, 4, P]), ALU.mult).then_inc(d_m, 1)
                    v.wait_ge(d_y, n + 1)
                    yd = mx[:, 3, 0:256].rearrange("p (q t) -> p q t", q=2)
                    yo = mx[:, 3, 256:512].rearrange("p (q t) -> p q t", q=2)
                    if c > 0:
                        own(v.tensor_tensor(t1[:, :, :], yo, e2[n % 2][:, :, :], ALU.mult))
                        own(v.tensor_tensor(t1[:, :, :], t1[:, :, :], yd, ALU.add))
                    for q in range(2):
                        pt = 2 * r + q
                        tile = xs[:, pt, P * c:P * c + P]
                        v.scalar_tensor_tensor(out=tile, in0=tile, scalar=dsk[:, pt:pt + 1],
                                               in1=t1[:, q, :] if c > 0 else yd[:, q, :],
                                               op0=ALU.mult, op1=ALU.add).then_inc(d_yc, 1)
                    v.wait_ge(d_yc, 2 * n + 2)
                elif kind == "ssd_state":
                    v.wait_ge(d_st, k + 1)
                    new = mxf[:, 0:1024]
                    if k == 0:
                        v.tensor_copy(st[0][:, :], new).then_inc(d_stc, 1)
                    else:
                        own(v.tensor_tensor(by_head(st[k % 2][:, :]), by_head(st[(k - 1) % 2][:, :]),
                                            over_head(dec[:, 1, k, :]), ALU.mult))
                        v.tensor_tensor(st[k % 2][:, :], st[k % 2][:, :], new, ALU.add).then_inc(d_stc, 1)
                    v.wait_ge(d_stc, k + 1)

            v.tensor_copy(small[:, 76:77], small[:, 78:79]).then_inc(r_s, 4)
            with v.Fori(0, 2) as half:
                with v.Fori(0, 4) as i:
                    for s in range(4):
                        n = half * 16 + i * 4 + s
                        v.wait_ge(tile_s, half * 32 + i * 4 + (2 * NB + s + 1))
                        v.tensor_scalar(rel[:, s % 2, :], ffb[s], 0.0, None, ALU.max).then_inc(r_s, 1)
                        v.wait_ge(ah_s, n + 1)
                        v.tensor_tensor(aL[:, bass.ds(i * 4 + s, 1), :], rsq[:, s % 2, :].unsqueeze(1),
                                        aH[:, bass.ds(i * 4 + s, 1), :].bitcast(F32), ALU.subtract).then_inc(al_s, 1)
                        v.wait_ge(al_s, n + 1)
                with v.Fori(0, 4) as i:
                    for s in range(2):
                        v.wait_ge(tile_s, half * 32 + i * 4 + (2 * NB + 16 + 3 + s))
                        o = xT[:, bass.ds(i * 2 + s, 1), :]
                        v.tensor_tensor(o, o, mx[:, 2 + s, :].unsqueeze(1), ALU.add).then_inc(x1_s, 1)
                        v.wait_ge(x1_s, half * 8 + i * 2 + (8 + s + 1))
            v.wait_ge(ms_s, 2)
            mean(mx[:, 4, 0:4], 4, D)
            v.wait_ge(ro_s, 4)
            v.wait_ge(wr_in, 16)
            for t, hh in ((0, 0), (0, 1), (1, 0), (2, 0), (3, 0)):
                v.wait_ge(*((y2_s, 1) if hh else (y1_s, t + 1)))
                v.scalar_tensor_tensor(out=yrow[:, t, 512 * hh:512 * hh + 512], in0=outb[hh][t],
                                       scalar=stat[:, t:t + 1], in1=wrow[:, 512 * hh:512 * hh + 512],
                                       op0=ALU.mult, op1=ALU.mult).then_inc(own_t, 1)

        @block.tensor
        def _(pe):
            def bank_free(c):
                if c < 2:
                    pe.wait_ge(x_cp, 4)
                    pe.wait_ge(x_cpa, 4)
                    return
                what, p = BLOCKS[(c - 2) // 2][0], c - 2
                if what == "gate":
                    pe.wait_ge(gt_s, gate_of(p) + 1)
                elif what == "merge":
                    pe.wait_ge(x1_s, BLOCKS[p // 2][5] + p % 2 + 1)
                else:
                    pe.wait_ge(free_s[p % 2], read_count(p))

            def pass3(dst, slot, s, k, hi, lo, start, stop):
                wh, wl = w_hi[:, slot, k, P * s:P * s + P], w_lo[:, slot, k, P * s:P * s + P]
                pe.matmul(dst, wh, hi, start=start, stop=False)
                pe.matmul(dst, wl, hi, start=False, stop=False)
                return pe.matmul(dst, wh, lo, start=False, stop=stop)

            def product(dst, slot, s, hi, lo, kts, k0=0, start=True, stop=True):
                for k in range(kts):
                    m = pass3(dst, slot, s, k, hi[:, k0 + k, :], lo[:, k0 + k, :], start and k == 0,
                              stop and k == kts - 1)
                return m

            def pair(dst, slot, hi, lo, kts, ready):
                order = [(k, s) for k in range(kts - 2) for s in range(2)]
                order += [(k, s) for s in range(2) for k in range(kts - 2, kts)]
                seen = -1
                for k, s in order:
                    if k > seen:
                        ready(k)
                        seen = k
                    m = pass3(dst[s], slot, s, k, hi[:, k, :], lo[:, k, :], k == 0, k == kts - 1)
                    if k == kts - 1:
                        m.then_inc(tile_s, 1)

            def h_ready(n):
                def ready(k):
                    pe.wait_ge(*((glo_s, 4 * n + k // 2 + 1) if k % 2 else (hlo_s, 4 * n + k // 2 + 1)))
                return ready

            def stats(dst, src, first):
                for t in range(TT):
                    m = pe.matmul(dst[:, t:t + 1], src[:, P * t:P * t + P], ones[:, 0:1], start=first and t == 0,
                                  stop=False, skip_group_check=True)
                return m

            def spread(dst, col):
                for t in range(TT):
                    m = pe.matmul(dst[:, P * t:P * t + P], stat[:, col + t:col + t + 1].broadcast_to([P, P]),
                                  ident[:, :], start=True, stop=True)
                return m

            def kv_ready(kind, ct):
                cc = tile_of(kind, ct)
                pe.wait_ge(free_s[cc % 2], read_count(cc))

            pe.wait_ge(cst, 1)
            for kind, k in STEPS:
                if kind == "load":
                    pe.wait_ge(vec_in, 96)
                    pe.transpose(pj[1][:, 0:V_ROWS], vrow[0:V_ROWS, :], ident[0:V_ROWS, 0:V_ROWS]).then_inc(v_tr, 1)
                    pe.wait_ge(v_cp, 1)
                    for t in range(TT):
                        pe.wait_ge(x_in[t], 16)
                        for j in range(KT):
                            dst = mx[:, j, :] if j < 6 else pj[j - 6][:, :]
                            m = pe.transpose(dst[:, P * t:P * t + P], xin[:, t, P * j:P * j + P], ident[:, :])
                    m.then_inc(x_tr, 1)
                elif kind == "norm":
                    if k == 0:
                        pe.wait_ge(x_cp, 3)
                        pe.wait_ge(ro_s, 1)
                        spread(mx[:, 0, :], 0).then_inc(bc_s, 1)
                        pe.wait_ge(rel_in, 32)
                        pe.matmul(mx[0:SWA_HEADS, 4, 0:320], relb[0:BUCKETS, :], onehot[0:BUCKETS, :],
                                  start=True, stop=True).then_inc(b_f, 1)
                    else:
                        pe.wait_ge(sq_s, 12)
                        stats(mx[:, 5, :], sq[:, 7, :], False).then_inc(ms_s, 1)
                        pe.wait_ge(ro_s, 3)
                        spread(mx[:, 4, :], 0).then_inc(bc_s, 1)
                elif kind == "tile":
                    n, s = k // 2, k % 2
                    what, _, _, kts, _, first = BLOCKS[n]
                    hi, lo, at = {"u0": (oH, oL, 4), "u2": (oH, oL, 0), "u1": (obH, obL, 8),
                                  "merge": (mH, mL, 16)}.get(what, (hH, hL, None))
                    if n in FUSED:
                        if s:
                            continue
                        pe.wait_ge(lo_s, n + 1)
                        bank_free(k)
                        bank_free(k + 1)
                        pair([bank(k), bank(k + 1)], n % 2, hi, lo, kts,
                             h_ready(0) if at is None else lambda j: pe.wait_ge(slo, at + j + 1))
                        continue
                    if s == 0:
                        pe.wait_ge(lo_s, n + 1)
                    bank_free(k)
                    product(bank(k), n % 2, s, hi, lo, kts).then_inc(tile_s, 1)
                    if what == "merge":
                        if first + s == 2:
                            pe.wait_ge(sq_s, 5)
                            stats(mx[:, 5, :], sq[:, 0, :], True)
                        if first + s >= 2:
                            pe.wait_ge(sq_s, 4 + first + s)
                            stats(mx[:, 5, :], sq[:, first + s - 1, :], False)
                elif kind == "vs_turn":
                    for ct in range(4):
                        kv_ready("vs", ct)
                        for t in range(TT):
                            m = pe.transpose(mx[:, ct, P * t:P * t + P], vsT[:, ct, P * t:P * t + P], ident[:, :])
                        m.then_inc(vt_s, 1)
                elif kind == "va_turn":
                    kv_ready("kava", 1)
                    pe.wait_ge(s_o, SB_HEADS)
                    for t in range(TT):
                        m = pe.transpose(mx[:, 4, P * t:P * t + P], vaT[:, P * t:P * t + P], ident[:, :])
                    m.then_inc(vt_s, 1)
                elif kind == "dt":
                    pe.wait_ge(dw, 1)
                    for t in range(TT):
                        for kt in range(KT):
                            for n, (l, r) in enumerate(((hH, wdtH), (hL, wdtH), (hH, wdtL))):
                                m = pe.matmul(mx[:, 5, 16 * t:16 * t + 16], l[:, kt, P * t:P * t + P], r[:, kt, :],
                                              start=kt == 0 and n == 0, stop=kt == KT - 1 and n == 2)
                    m.then_inc(dtm, 1)
                elif kind == "sb_scores":
                    r0, pt, b = 64 * (k % 2), k // 2, 1536 * (k % 2)
                    if k == 0:
                        kv_ready("ks", 3)
                        pe.wait_ge(vc_s, 4)
                        pe.wait_ge(b_tc, 1)
                    elif k == 1:
                        pe.wait_ge(dtx, 1)
                    else:
                        pe.wait_ge(s_o, k - 1)
                    for j in range(TT):
                        m = pe.matmul(mxf[:, b + cols[j]:b + cols[j] + T - P * j], ks[r0:r0 + 64, pt, P * j:P * j + P],
                                      qs[r0:r0 + 64, pt, P * j:T], start=j < 3, stop=False, skip_group_check=True)
                    m.then_inc(s_sc, 1)
                elif kind == "sb_cum":
                    b = 1536 * (k % 2)
                    pe.wait_ge(cR, 3)
                    pe.wait_ge(s_sp, k + 1)
                    pe.wait_ge(s_lo, k + 1)
                    for j in range(TT):
                        for i in range(j, TT):
                            dst = mxf[:, b + cols[j] + P * (i - j):b + cols[j] + T - P * j]
                            for part in (spH, spL):
                                m = pe.matmul(dst, (neg_triR if i == j else neg_oneR)[:, :],
                                              part[:, cols[i]:cols[i] + T - P * i], start=False,
                                              stop=i == TT - 1 and part is spL, skip_group_check=True)
                    m.then_inc(s_cu, 1)
                elif kind == "sb_av":
                    r0 = 64 * (k % 2)
                    pe.wait_ge(s_wm, 2 * (k + 1))
                    for j in range(TT):
                        m = pe.matmul(mx[r0:r0 + 64, 3 * (k % 2), P * j:T], vs[:, j, HD * k:HD * k + HD],
                                      sw[k % 2][:, cols[j]:cols[j] + T - P * j], start=j == 0, stop=j == TT - 1,
                                      skip_group_check=True)
                    m.then_inc(s_av, 1)
                elif kind == "bias":
                    pe.wait_ge(trev_in, 64)
                    tr = trev[:, :, :].rearrange("p h k -> p (h k)")
                    for j in range(3):
                        m = pe.matmul(mx[:, j, :], flip[:, :], tr[:, 512 * j:512 * j + 512], start=True, stop=True)
                    m.then_inc(b_t, 1)
                elif kind == "swa_scores":
                    i, gq = k // 2, k % 2
                    k0 = CHUNK if i == 0 else 0
                    if k == 0:
                        kv_ready("kava", 1)
                        pe.wait_ge(s_o, SB_HEADS)
                    else:
                        pe.wait_ge(a_p, k)
                    for hh in range(4):
                        h = 4 * gq + 2 * (hh % 2) + hh // 2
                        r0 = 64 * (h % 2)
                        m = pe.matmul(mxf[:, 256 * hh + k0:256 * hh + KEYS], qa[r0:r0 + 64, h // 2, P * i:P * i + P],
                                      kd[r0:r0 + 64, gq, P * i - CHUNK + k0:P * i + P], start=True, stop=True)
                    m.then_inc(a_sc, 1)
                elif kind == "swa_turn":
                    pe.wait_ge(a_n, k + 1)
                    if k:
                        pe.wait_ge(a_tc, k)
                    for part in range(1 if k // 2 == 0 else 0, 2):
                        for hh in range(4):
                            m = pe.transpose(mx[:, 2 + part, P * hh:P * hh + P],
                                             pr[k % 2][:, hh, P * part:P * part + P], ident[:, :])
                    m.then_inc(a_t, 1)
                elif kind == "swa_pv":
                    i, gq = k // 2, k % 2
                    pe.wait_ge(a_tc, k + 1)
                    pe.wait_ge(*((a_o, k) if k else (vc_s, 5)))
                    for par in range(2):
                        for part in range(1 if i == 0 else 0, 2):
                            m = pe.matmul(mx[64 * par:64 * par + 64, 4, 0:256],
                                          va[:, i - 1 + part, HD * gq:HD * gq + HD],
                                          pT[:, part, 256 * par:256 * par + 256],
                                          start=part == 0 or i == 0, stop=part == 1)
                    m.then_inc(a_pv, 1)
                elif kind == "y_norm":
                    for t in range(KT):
                        pe.wait_ge(ysq_s, t + 1)
                        g2 = t // 4
                        for j in range(TT):
                            m = pe.matmul(mx[:, 5, 4 * g2 + j:4 * g2 + j + 1], ysq[:, t, P * j:P * j + P], ones[:, 0:1],
                                          start=t == 0 and j == 0, stop=False, skip_group_check=True)
                    m.then_inc(gms_s, 1)
                elif kind == "y_spread":
                    pe.wait_ge(ro_s, 2)
                    spread(mx[:, 3, :], 0)
                    spread(mx[:, 4, :], 4).then_inc(bc_s, 1)
                elif kind == "decay":
                    pe.wait_ge(dtf, 1)
                    pe.wait_ge(s_o, SB_HEADS)
                    for c in range(TT):
                        pe.matmul(mx[:, 5, 16 * c:16 * c + 16], tri[:, :], dta[:, c, :], start=True, stop=True)
                        m = pe.matmul(mx[:, 5, 64 + 16 * c:80 + 16 * c], ones[:, :], dta[:, c, :], start=True, stop=True)
                    m.then_inc(d_ac, 1)
                elif kind == "ssd_prep":
                    c = k
                    if c == 0:
                        pe.wait_ge(th_s, CONV_T)
                        pe.wait_ge(a_o, 8)
                    else:
                        pe.wait_ge(d_stc, c)
                    for t in range(8):
                        pe.transpose(mxf[:, P * t:P * t + P], xs[:, t, P * c:P * c + P], ident[:, :])
                    for g2 in range(2):
                        pe.transpose(mx[:, 2, P * g2:P * g2 + P], xs[:, 8 + g2, P * c:P * c + P], ident[:, :])
                    for g2 in range(2):
                        m = pe.matmul(mx[:, 2, 256 + P * g2:256 + P * g2 + P], xs[:, 8 + g2, P * c:P * c + P],
                                      xs[:, 10 + g2, P * c:P * c + P], start=True, stop=True)
                    m.then_inc(d_pr, 1)
                elif kind == "ssd_sum":
                    c, r = k // 4, k % 4
                    if k == 0:
                        pe.wait_ge(d_dl, 1)
                        pe.wait_ge(d_da, 1)
                    if k >= 2:
                        pe.wait_ge(d_e, k - 1)
                    for hh in range(4):
                        h = 4 * r + hh
                        for part in (dtaH, dtaL):
                            m = pe.matmul(mx[:, 4 + k % 2, P * hh:P * hh + P],
                                          part[:, c, h:h + 1].broadcast_to([P, P]), triR[:, :],
                                          start=part is dtaH, stop=part is dtaL)
                    m.then_inc(d_ab, 1)
                elif kind == "ssd_y":
                    c, r = k
                    n = 4 * c + r
                    pe.wait_ge(d_m, n + 1)
                    if n:
                        pe.wait_ge(d_yc, 2 * n)
                    for hh in range(4):
                        h = 4 * r + hh
                        par, q = hh % 2, hh // 2
                        m = pe.matmul(mx[64 * par:64 * par + 64, 3, P * q:P * q + P], xd[:, HD * h:HD * h + HD],
                                      mt[n % 2][:, hh, :], start=True, stop=True)
                    if c > 0:
                        pe.wait_ge(d_stc, c)
                        for q in range(2):
                            pt = 2 * r + q
                            m = pe.matmul(mx[:, 3, 256 + P * q:256 + P * q + P], st[(c - 1) % 2][:, P * pt:P * pt + P],
                                          xs[:, 10 + r // 2, P * c:P * c + P], start=True, stop=True)
                    m.then_inc(d_y, 1)
                elif kind == "ssd_state":
                    pe.wait_ge(d_xw, k + 1)
                    for g2 in range(2):
                        m = pe.matmul(mx[:, g2, :], bt[:, g2, :], xw[:, 512 * g2:512 * g2 + 512],
                                      start=True, stop=True)
                    m.then_inc(d_st, 1)

            with pe.Fori(0, 2) as half:
                with pe.Fori(0, 4) as i:
                    for b in range(2):
                        pe.wait_ge(lo_s, half * 16 + i * 2 + (NB + b + 1))
                        pe.wait_ge(r_s, half * 16 + i * 4 + (2 * b + 2))
                        pair(ffb[2 * b:2 * b + 2], (NB + b) % 2, hH, hL, KT, h_ready(1))
                with pe.Fori(0, 4) as i:
                    for b in range(2):
                        pe.wait_ge(lo_s, half * 16 + i * 2 + (NB + 8 + b + 1))
                        pe.wait_ge(al_s, half * 16 + 8 * (b + 1))
                        for s in range(2):
                            if b == 0:
                                pe.wait_ge(x1_s, half * 8 + i * 2 + (7 + s))
                            product(mx[:, 2 + s, :], (NB + b) % 2, s, aH, aL, KT, k0=8 * b, start=b == 0,
                                    stop=b == 1).then_inc(tile_s, 1)
            pe.wait_ge(r_s, 36)
            for t in range(TT):
                for j in range(4):
                    m = pe.transpose(outb[0][t][:, P * j:P * j + P], xT[:, j, P * t:P * t + P], ident[:, :])
                m.then_inc(y1_s, 1)
            pe.wait_ge(gsq_s, 1)
            stats(mx[:, 4, :], sq[:, 0, :], True)
            for t in (6, 7):
                pe.wait_ge(sq_s, 12 + t + 1)
                m = stats(mx[:, 4, :], sq[:, t, :], False)
            m.then_inc(ms_s, 1)
            pe.wait_ge(x1_s, 24)
            for t in range(TT):
                if t == 3:
                    pe.wait_ge(ri_s, 4)
                for j in range(4):
                    m = pe.transpose(outb[1][t][:, P * j:P * j + P], xT[:, 4 + j, P * t:P * t + P], ident[:, :])
                m.then_inc(y2_s, 1)


def relative_onehot():
    r = np.arange(320) - (P + CHUNK - 1)
    nb = BUCKETS // 2
    exact = nb // 2
    n = np.abs(r)
    large = exact + (np.log(np.maximum(n, 1) / exact) / np.log(MAX_DIST / exact) * (nb - exact)).astype(np.int32)
    b = np.where(r > 0, nb, 0) + np.where(n < exact, n, np.minimum(large, nb - 1))
    return (np.arange(BUCKETS)[:, None] == b[None, :]).astype(np.float32)


INS = ["x", "norm_mix_w", "w_in", "swa_sinks", "rel_bias", "conv_w", "conv_b", "dt_bias", "a_log", "d_skip",
       "ssd_norm_w", "w_out", "w_merge", "norm_ffn_w", "w_ff1", "w_ff2", "final_norm_w"]


def kernel(**inputs):
    import concourse.bacc as bacc
    from concourse.bass_utils import run_bass_kernel_spmd

    nc = bacc.Bacc("TRN2", target_bir_lowering=False, num_devices=1)
    arrays = {n: np.ascontiguousarray(inputs[n]) for n in INS}
    arrays["onehot"] = relative_onehot()
    args = {n: nc.dram_tensor(n, a.shape, mybir.dt.from_np(a.dtype), kind="ExternalInput").ap()
            for n, a in arrays.items()}
    out = nc.dram_tensor("out", (1, T, D), F32, kind="ExternalOutput").ap()
    build(nc, args, out)
    r = run_bass_kernel_spmd(nc, [arrays], core_ids=[0])
    return r.results[0]["out"]
```

```python
from contextlib import ExitStack

import concourse.bass as bass
import numpy as np
from concourse import mybir

F32 = mybir.dt.float32
F32R = mybir.dt.float32r
ALU = mybir.AluOpType
ACT = mybir.ActivationFunctionType
AX = mybir.AxisListType

P = 128
T = 512
TT = T // P
D = 1024
KT = D // P
HD = 64
EPS = 1e-6
KIB = 1024

SWA_HEADS, KV_HEADS, CHUNK, BUCKETS, MAX_DIST = 8, 2, 64, 32, 128
KEYS = P + CHUNK
SB_HEADS = 8
CONV = 4
CONV_T = 12

C_QA, C_KA, C_Z, C_XBC, C_DT, C_QS, C_KS, C_VS, C_G = 0, 512, 768, 1792, 3328, 3344, 3856, 4368, 4880
BC = 256
V_MIX, V_CW, V_CB, V_SSDN, V_FFN, V_ROWS = 0, 8, 56, 68, 76, 84


def plan():
    blocks = []

    def block(kind, matrix, row, kts, col, first):
        blocks.append((kind, matrix, row, kts, col, first))
        return [("tile", 2 * len(blocks) - 2), ("tile", 2 * len(blocks) - 1)]

    def w_in(kind, col, n, first=0):
        return sum([block(kind, "w_in", 0, KT, col + BC * i, first + 2 * i) for i in range(n)], [])

    def gate(b, i):
        return block("gate", "w_in", 0, KT, C_G + b * D + BC * i, 2 * i)

    def branch_out(b, row, kts, i):
        return block("u%d" % b, "w_out", row, kts, BC * i, 2 * i)

    def branch(b, row, kts, start=0):
        out = [] if start == 0 else branch_out(b, row, kts, 0)
        return out + sum([gate(b, i) + branch_out(b, row, kts, i) for i in range(start, D // BC)], [])

    def halves(tiles):
        return sum([([("half", t[1])] if blocks[t[1] // 2][3] == KT else []) + [t] for t in tiles], [])

    def weave(places, others):
        out, at = [], 0
        for i, s in enumerate(places):
            out.append(s)
            upto = (i + 1) * len(others) // len(places)
            out += others[at:upto]
            at = upto
        return sum([o if isinstance(o, list) else [o] for o in out], [])

    def scores(h):
        if h + 1 == SB_HEADS:
            return [("sb_scores", h)]
        return [("sb_parts_hi", h + 1), ("sb_scores", h), ("sb_parts_lo", h + 1)]

    sb = [scores(0), [("sb_ln", 0), ("sb_max", 0)] + scores(1), ("sb_split", 0), [], []]
    for h in range(SB_HEADS):
        more = h + 1 < SB_HEADS
        sb.append([("sb_cum", h)] + ([("sb_ln", h + 1)] if more else []))
        sb.append([("sb_av", h)] + ([("sb_max", h + 1)] if more else []))
        if more:
            sb += [[("sb_split", h + 1)] + (scores(h + 2) if h + 2 < SB_HEADS else []), []]
    swa = [[("p_zero", 0), ("swa_scores", 0)], ("swa_scores", 1), ("swa_norm", 0)]
    for u in range(8):
        swa.append([("swa_turn", u)] + ([("swa_norm", u + 1)] if u < 7 else []))
        swa.append([("swa_pv", u)] + ([("swa_scores", u + 2)] if u < 6 else []))
    ssd = []
    for n in range(4 * TT):
        c, r = n // 4, n % 4
        more = n + 2 < 4 * TT
        ssd.append(([("ssd_mul", n + 1)] if n + 1 < 4 * TT else []) + [("ssd_y", (c, r))] +
                   ([("ssd_sum", n + 2)] if more else []))
        if c < TT - 1 and r < 2:
            ssd.append([("ssd_state", c), ("ssd_prep", c + 1)][r])

    steps = [("load", 0), ("norm", 0)]
    steps += w_in("qs", C_QS, 2) + [("bias", 0)]
    steps += w_in("ks", C_KS, 1) + [("dt_w", 0)] + w_in("ks", C_KS + BC, 1, 2) + [("dt", 0)]
    t = w_in("vs", C_VS, 2)
    steps += [("sb_parts_hi", 0), ("sb_parts_lo", 0)] + t[:1] + [("dt_turn", 0)] + t[1:] + [("vs_turn", 0)]
    steps += weave(halves(w_in("qa", C_QA, 2) + w_in("kava", C_KA, 1) + w_in("xbc", C_XBC, 6)), sb)
    t = gate(2, 0)
    steps += t[:1] + [("va_turn", 0), ("decay", 0), ("split_c", 0)] + t[1:]
    places, n, just = [], 0, False
    for t in halves(branch(2, 1536, 4, 1)):
        with_silu = t[0] == "tile" and blocks[t[1] // 2][0] == "gate"
        late = [("silu_mul", m) for m in (n - 2, n - 1)] if n and just else []
        places.append(late + ([t, ("silu", n), ("silu", n + 1)] if with_silu else [t]))
        n += 2 * with_silu
        just = with_silu
    steps += weave(places, swa)
    t = gate(0, 0)
    steps += t[:1] + [("ssd_prep", 0), ("ssd_sum", 0), ("split_a", 0), ("half", t[1][1]), ("ssd_sum", 1)]
    steps += t[1:] + [("ssd_mul", 0)]
    steps += weave(halves(branch(0, 0, 4, 1) + w_in("z", C_Z, 1)), ssd)
    steps += w_in("z", C_Z + BC, 3, 2)
    t = gate(1, 0)
    steps += [("y_sum", 0)] + t[:1] + [("half", t[1][1]), ("y_norm", 0)] + t[1:] + [("y_spread", 0)]
    t, b = gate(1, 1), [("split_b", i) for i in range(KT + 2)]
    steps += b[:3] + [("half", t[0][1])] + b[3:6] + t[:1] + b[6:] + t[1:] + branch_out(1, 512, 8, 0) + gate(1, 2)
    u = branch_out(1, 512, 8, 1) + gate(1, 3) + branch_out(1, 512, 8, 2) + branch_out(1, 512, 8, 3)
    steps += u[:2] + [("split_m", 0), ("split_m", 1)] + u[2:4] + [("split_m", 2), ("split_m", 3)]
    for i, t in enumerate(u[4:]):
        steps += [t, ("split_m", 3 + i)] if i else [t]
    steps += [("split_m", 7)]
    for i in range(4):
        steps += block("merge", "w_merge", 0, KT, BC * i, 2 * i)
    return blocks, steps


BLOCKS, STEPS = plan()
HALVED = {k for kind, k in STEPS if kind == "half"}
NB = len(BLOCKS)


def gate_of(c):
    kind, ct = BLOCKS[c // 2][0], BLOCKS[c // 2][5] + c % 2
    if kind != "gate":
        return {"u2": 0, "u0": 8, "u1": 16}[kind] + ct
    return {2: 0, 0: 8, 1: 16}[(BLOCKS[c // 2][4] - C_G) // D] + ct


def tile_of(kind, i=0):
    return [2 * n for n, b in enumerate(BLOCKS) if b[0] == kind][i // 2] + i % 2


def build(nc, ins, out):
    with ExitStack() as ctx:
        def sem(name):
            return ctx.enter_context(nc.semaphore(name))

        base = -(-nc.sbuf_base // 32) * 32
        arena = ctx.enter_context(nc.sbuf_tensor("arena", [P, 207 * KIB // 4], F32))
        del arena

        def at(name, kib, shape, dt=F32):
            return nc.alloc_sbuf_tensor_at(name, [P] + shape, dt, offset=base + int(kib * KIB))

        raw = at("raw", 0, [2, KT, BC])
        w_hi = at("w_hi", 16, [2, KT, BC], F32R)
        w_lo = at("w_lo", 32, [2, KT, BC], F32R)
        xT = at("xT", 48, [KT, T])
        hH = at("hH", 64, [KT, T], F32R)
        hL = at("hL", 80, [KT, T], F32R)
        ident = at("ident", 96, [P])
        flip = at("flip", 96.5, [P])
        tri = at("tri", 97, [P])
        ones = at("ones", 97.5, [P])
        neg_tri = at("neg_tri", 98, [P])
        neg_one = at("neg_one", 98.5, [P])
        vec = at("vec", 99, [96])
        dtb = at("dtb", 99.5, [16])
        nega = at("nega", 99.5625, [16])
        sink = at("sink", 99.625, [8])
        dsk = at("dsk", 99.65625, [8])
        small = at("small", 99.6875, [80])
        stat = at("stat", 99.375, [32])
        dta = at("dta", 100, [TT, 16])
        dtv = at("dtv", 100.25, [TT, 16])
        dtt = at("dtt", 100.5, [4, TT * 16])
        acum = at("acum", 101.5, [TT, 16])
        dec = at("dec", 100.5, [2, TT, 16])
        neg_triR = at("neg_triR", 102, [P], F32R)
        neg_oneR = at("neg_oneR", 102.5, [P], F32R)
        triR = at("triR", 103, [P], F32R)
        dtaH = at("dtaH", 103.5, [TT, 16], F32R)
        dtaL = at("dtaL", 103.75, [TT, 16], F32R)
        tbias = at("tbias", 104, [SWA_HEADS, KEYS])
        xin = at("xin", 110, [TT, D])
        sq = at("sq", 174, [KT, T])
        hf = at("hf", 190, [4, T])
        vrow = at("vrow", 144, [P])
        onehot = at("onehot", 144.5, [320])
        relb = at("relb", 146, [8])
        frow = at("frow", 146.25, [320])
        wdt = at("wdt", 148, [KT, P])
        wdtH = at("wdtH", 152, [KT, P], F32R)
        wdtL = at("wdtL", 156, [KT, P], F32R)
        dtr = at("dtr", 182, [T])
        trev = at("trev", 136, [SWA_HEADS, KEYS])
        qs = at("qs", 110, [4, T])
        ks = at("ks", 118, [4, T])
        vs = at("vs", 126, [TT, 512])
        sp = at("sp", 134, [1280])
        spH = at("spH", 184, [1280], F32R)
        spL = at("spL", 189, [1280], F32R)
        sw = [at("sw0", 139, [1280]), at("sw1", 194, [1280])]
        qHL = at("qHL", 199, [T], F32R)
        kHH = at("kHH", 201, [T], F32R)
        kL = at("kL", 203, [T], F32R)
        qa = at("qa", 144, [4, T])
        kd = at("kd", 152, [KV_HEADS, T])
        va = at("va", 156, [TT, P])
        xs = at("xs", 158, [12, T])
        vsT = at("vsT", 158, [4, T])
        vaT = at("vaT", 182, [T])
        pr = [at("pr0", 118, [4, 256]), at("pr1", 110, [4, 256])]
        cth = at("cth", 114, [2, T])
        pT = at("pT", 122, [2, T])
        oH = at("oH", 126, [4, T], F32R)
        oL = at("oL", 134, [4, T], F32R)
        mg = at("mg", 184, [KT, T])
        gt = at("gt", 200, [2, T])
        gu = at("gu", 204, [T])
        xd = [at("xd0", 110, [D]), at("xd1", 144, [D])]
        xw = at("xw", 114, [D])
        bt = at("bt", 118, [2, P])
        cbm = [at("cbm0", 119, [2, P]), at("cbm1", 107, [2, P])]
        st = [at("st0", 120, [D]), at("st1", 152, [D])]
        mt = [at("mt0", 124, [4, P]), at("mt1", 156, [4, P])]
        e2 = [at("e20", 104, [2, P]), at("e21", 105, [2, P])]
        t1 = at("t1", 106, [2, P])
        gt1 = at("gt1", 174, [4, T])
        obH = at("obH", 110, [KT, T], F32R)
        obL = at("obL", 126, [KT, T], F32R)
        ysq = at("ysq", 142, [KT, T])
        mH = at("mH", 142, [KT, T], F32R)
        mL = at("mL", 158, [KT, T], F32R)
        aH = at("aH", 110, [16, T], F32R)
        aL = at("aL", 142, [16, T], F32R)
        rel = at("rel", 194, [2, T])
        rsq = at("rsq", 198, [2, T])
        wrow = at("wrow", 202, [D])
        yrow = at("yrow", 110, [TT, D])
        r2 = at("r2", 190, [T])
        fsc = at("fsc", 192, [T])

        pj = [ctx.enter_context(nc.psum_tensor("pj%d" % i, [P, 512], F32)) for i in range(2)]
        mx = ctx.enter_context(nc.psum_tensor("mx", [P, 6, 512], F32))
        mxf = mx[:, :, :].rearrange("p b n -> p (b n)")
        scr = nc.dram_tensor("rel_rows", [SWA_HEADS, 320], F32).ap()

        x_in = [sem("x_in%d" % i) for i in range(TT)]
        vec_in = sem("vec_in")
        row_in = sem("row_in")
        rel_in = sem("rel_in")
        rows_out = sem("rows_out")
        rows_in = sem("rows_in")
        dt_in = sem("dt_in")
        final_w_in = sem("final_w_in")
        weights_in = [sem("weights_in%d" % i) for i in range(2)]
        done = sem("done")
        weights_hi = sem("weights_hi")
        weights_lo = sem("weights_lo")
        tile_done = sem("tile_done")
        bank_read = [sem("bank_read%d" % i) for i in range(2)]
        operand_hi = sem("operand_hi")
        operand_lo = sem("operand_lo")
        gate_tanh = sem("gate_tanh")
        gate_used = sem("gate_used")
        constants = sem("constants")
        constants_r = sem("constants_r")
        stat_set = sem("stat_set")
        vec_turned = sem("vec_turned")
        vec_ready = sem("vec_ready")
        x_turned = sem("x_turned")
        x_even_ready = sem("x_even_ready")
        x_odd_ready = sem("x_odd_ready")
        squares = sem("squares")
        squares_added = sem("squares_added")
        squares_summed = sem("squares_summed")
        mean_sq = sem("mean_sq")
        root_in = sem("root_in")
        root_out = sem("root_out")
        rstd_spread = sem("rstd_spread")
        h_made = sem("h_made")
        h_hi = sem("h_hi")
        h_lo_even = sem("h_lo_even")
        h_lo_odd = sem("h_lo_odd")
        v_turned = sem("v_turned")
        v_copied = sem("v_copied")
        sb_parts_hi = sem("sb_parts_hi")
        sb_parts_lo = sem("sb_parts_lo")
        sb_scored = sem("sb_scored")
        sb_clipped = sem("sb_clipped")
        sb_exp = sem("sb_exp")
        sb_ln = sem("sb_ln")
        sb_softplus = sem("sb_softplus")
        sb_softplus_masked = sem("sb_softplus_masked")
        sb_softplus_hi = sem("sb_softplus_hi")
        sb_softplus_lo = sem("sb_softplus_lo")
        sb_summed = sem("sb_summed")
        sb_weights = sem("sb_weights")
        sb_weights_masked = sem("sb_weights_masked")
        sb_product = sem("sb_product")
        sb_out = sem("sb_out")
        bias_rows = sem("bias_rows")
        bias_copied = sem("bias_copied")
        bias_flipped = sem("bias_flipped")
        bias_ready = sem("bias_ready")
        swa_scored = sem("swa_scored")
        swa_biased = sem("swa_biased")
        swa_max = sem("swa_max")
        swa_exp = sem("swa_exp")
        swa_normed = sem("swa_normed")
        swa_turned = sem("swa_turned")
        swa_turned_copied = sem("swa_turned_copied")
        swa_turned_first = sem("swa_turned_first")
        swa_product = sem("swa_product")
        swa_out = sem("swa_out")
        dt_w_hi = sem("dt_w_hi")
        dt_w_lo = sem("dt_w_lo")
        dt_product = sem("dt_product")
        dt_rows = sem("dt_rows")
        dt_softplus_in = sem("dt_softplus_in")
        dt_exp = sem("dt_exp")
        dt_ln = sem("dt_ln")
        dt_ready = sem("dt_ready")
        dta_hi = sem("dta_hi")
        dta_lo = sem("dta_lo")
        ssd_cumsums = sem("ssd_cumsums")
        ssd_decay_in = sem("ssd_decay_in")
        ssd_decay_exp = sem("ssd_decay_exp")
        conv_tanh = sem("conv_tanh")
        conv_silu = sem("conv_silu")
        ssd_turned = sem("ssd_turned")
        ssd_inputs = sem("ssd_inputs")
        ssd_sums_spread = sem("ssd_sums_spread")
        ssd_diff = sem("ssd_diff")
        ssd_exp = sem("ssd_exp")
        ssd_matrix = sem("ssd_matrix")
        ssd_product = sem("ssd_product")
        ssd_y_made = sem("ssd_y_made")
        ssd_state_product = sem("ssd_state_product")
        ssd_state_made = sem("ssd_state_made")
        z_tanh = sem("z_tanh")
        y_gated = sem("y_gated")
        y_squares = sem("y_squares")
        y_squares_added = sem("y_squares_added")
        y_mean_sq = sem("y_mean_sq")
        y_normed = sem("y_normed")
        residual = sem("residual")
        ff_input_lo = sem("ff_input_lo")
        r2_made = sem("r2_made")
        relu = sem("relu")
        relu_sq = sem("relu_sq")
        act_hi = sem("act_hi")
        act_lo = sem("act_lo")
        ff_scaled = sem("ff_scaled")
        rows_turned0 = sem("rows_turned0")
        rows_turned1 = sem("rows_turned1")
        row_scaled = sem("row_scaled")
        rows_of_pool = sem("rows_of_pool")
        rows_of_vector = sem("rows_of_vector")
        scalar_chain = sem("scalar_chain")
        vector_chain = sem("vector_chain")
        pool_chain = sem("pool_chain")

        block = ctx.enter_context(nc.Block())

        matrices = {k: ins[k][0] for k in ("w_in", "w_out", "w_merge", "w_ff1", "w_ff2")}
        SPLIT = {"split_c": 0, "split_a": 4, "split_b": 8, "split_m": 16}
        cols = [0, 512, 1024, 896]
        ffb = [pj[0][:, :], pj[1][:, :], mx[:, 0, :], mx[:, 1, :]]
        outb = [ffb, [mx[:, 2, :], mx[:, 3, :], mx[:, 5, :], mx[:, 4, :]]]

        def piece_rows(n, p):
            m = (BLOCKS[n][3] if n < NB else KT) // 2
            return (0, m) if p == 0 else (m, 2 * m)

        def pieces_here(kind, k):
            if kind not in ("half", "tile") or k % 2:
                return ()
            return (0,) if kind == "half" else (1,) if k in HALVED else (0, 1)

        def read_count(c):
            return sum(1 for p in range(c % 2, c + 1, 2) if BLOCKS[p // 2][0] not in ("gate", "merge"))

        def bank(c):
            return pj[c % 2][:, :]

        @block.sync
        def _(sy):
            for t in range(TT):
                sy.dma_start(xin[:, t, :], ins["x"][0, P * t:P * t + P, :]).then_inc(x_in[t], 16)
            for row, end, src in ((V_MIX, V_CW, ins["norm_mix_w"][0]), (V_CB, V_SSDN, ins["conv_b"][0]),
                                  (V_SSDN, V_FFN, ins["ssd_norm_w"][0]), (V_FFN, V_ROWS, ins["norm_ffn_w"][0])):
                sy.dma_start(vrow[row:end, :], src.rearrange("(a p) -> a p", p=P)).then_inc(vec_in, 16)
            sy.dma_start(vrow[V_CW:V_CB, :], ins["conv_w"][0].rearrange("k (a p) -> (k a) p", p=P)).then_inc(vec_in, 16)

            def load_block(n):
                _, matrix, row, kts, col, _ = BLOCKS[n]
                if n >= 2:
                    sy.wait_ge(weights_lo, 2 * (n - 1))
                src = matrices[matrix][row:row + P * kts, col:col + BC].rearrange("(k p) c -> p k c", p=P)
                sy.dma_start(raw[:, n % 2, 0:kts, :], src).then_inc(weights_in[n % 2], 16)

            load_block(0)
            sy.dma_start(onehot[0:BUCKETS, :], ins["onehot"]).then_inc(rel_in, 16)
            sy.dma_start(relb[0:BUCKETS, :], ins["rel_bias"]).then_inc(rel_in, 16)
            load_block(1)

            def on_all(row, n):
                return row[0:1, :].broadcast_to([P, n])

            sy.dma_start(dtb[:, :], on_all(ins["dt_bias"], 16)).then_inc(row_in, 16)
            sy.dma_start(nega[:, :], on_all(ins["a_log"], 16)).then_inc(row_in, 16)
            sy.dma_start(sink[:, :], on_all(ins["swa_sinks"], 8)).then_inc(row_in, 16)
            for half in range(2):
                src = ins["d_skip"].rearrange("a (q two) -> a two q", two=2)[0:1, half, :]
                sy.dma_start(dsk[64 * half:64 * half + 64, :], src.broadcast_to([64, 8]),
                             allow_slow_non_contiguous=True).then_inc(row_in, 16)
            src = matrices["w_in"][:, C_DT:C_DT + P].rearrange("(k p) c -> p k c", p=P)
            sy.dma_start(wdt[:, :, :], src).then_inc(dt_in, 16)
            sy.wait_ge(bias_copied, 1)
            sy.dma_start(scr, frow[0:SWA_HEADS, :]).then_inc(rows_out, 16)
            sy.wait_ge(rows_out, 16)
            for n in range(4):
                src = bass.AP(tensor=scr.tensor, offset=320 * (4 * (n // 2) + n % 2), ap=[[1, P], [640, 2], [1, KEYS]])
                sy.dma_start(trev[:, 2 * n:2 * n + 2, :], src).then_inc(rows_in, 16)
            for n in range(2, NB):
                load_block(n)
            sy.wait_ge(gate_used, 24)
            sy.dma_start(wrow[:, :], ins["final_norm_w"].rearrange("(a n) -> a n", a=1).broadcast_to([P, D])
                         ).then_inc(final_w_in, 16)
            with sy.Fori(0, 2) as half:
                with sy.Fori(0, 4) as i:
                    for s in range(2):
                        sy.wait_ge(weights_lo, half * 32 + i * 4 + 2 * (NB + s - 1))
                        src = matrices["w_ff1"][:, bass.ds(half * 2048 + i * 512 + s * BC, BC)]
                        sy.dma_start(raw[:, (NB + s) % 2, :, :], src.rearrange("(k p) c -> p k c", p=P)
                                     ).then_inc(weights_in[(NB + s) % 2], 16)
                with sy.Fori(0, 4) as i:
                    for s in range(2):
                        sy.wait_ge(weights_lo, half * 32 + i * 4 + 2 * (NB + 8 + s - 1))
                        src = matrices["w_ff2"][bass.ds(half * 2048 + s * 1024, 1024), bass.ds(i * BC, BC)]
                        sy.dma_start(raw[:, (NB + s) % 2, :, :], src.rearrange("(k p) c -> p k c", p=P)
                                     ).then_inc(weights_in[(NB + s) % 2], 16)
            for t, hh, ready, count in (
                    (0, 0, rows_of_vector, 1), (0, 1, rows_of_vector, 2), (1, 0, rows_of_vector, 3),
                    (1, 1, rows_of_pool, 1), (2, 0, rows_of_vector, 4), (3, 0, rows_of_vector, 5),
                    (2, 1, rows_of_pool, 2), (3, 1, rows_of_pool, 3)):
                sy.wait_ge(ready, count)
                sy.dma_start(out[0, P * t:P * t + P, 512 * hh:512 * hh + 512],
                             yrow[:, t, 512 * hh:512 * hh + 512]).then_inc(done, 16)
            sy.wait_ge(done, 16 * 2 * TT)

        @block.gpsimd
        def _(g):
            n_own = [0]

            def own(i):
                i.then_inc(pool_chain, 1)
                n_own[0] += 1
                g.wait_ge(pool_chain, n_own[0])

            def sel(t, op, fill, mult, step, start=0):
                own(g.affine_select(out=t, in_=t, compare_op=op, fill=fill, base=start,
                                    pattern=[[step, P]], channel_multiplier=mult))

            own(g.memset(ident[:, :], 0.0))
            sel(ident[:, :], ALU.not_equal, 1.0, 1, -1)
            own(g.memset(flip[:, :], 0.0))
            sel(flip[:, :], ALU.not_equal, 1.0, 1, 1, -(P - 1))
            own(g.memset(ones[:, :], 1.0))
            own(g.memset(tri[:, :], 1.0))
            sel(tri[:, :], ALU.is_ge, 0.0, -1, 1)
            own(g.memset(neg_one[:, :], -1.0))
            own(g.memset(neg_tri[:, :], -1.0))
            sel(neg_tri[:, :], ALU.is_ge, 0.0, 1, -1)
            g.memset(ident[0:1, 0:1], 1.0).then_inc(constants, 1)

            def low(n, p):
                low_piece(n % 2, *piece_rows(n, p), 2 * n + p + 1)

            def low_piece(slot, k0, k1, count):
                g.wait_ge(weights_hi, count)
                g.tensor_tensor(w_lo[:, slot, k0:k1, :], raw[:, slot, k0:k1, :],
                                w_hi[:, slot, k0:k1, :].bitcast(F32), ALU.subtract).then_inc(weights_lo, 1)

            def add_to(dst, src):
                own(g.tensor_tensor(dst, dst, src, ALU.add))

            def y_sum(t):
                g.wait_ge(y_squares, t + 1)
                if t % 4 < 3:
                    add_to(ysq[:, t // 4 * 4, :], ysq[:, t, :])
                else:
                    o = ysq[:, t // 4 * 4, :]
                    g.tensor_tensor(o, o, ysq[:, t, :], ALU.add).then_inc(y_squares_added, 1)

            def diag(t, s):
                v3 = t[:, 0:1152].rearrange("p (a b) -> p a b", b=128)[:, 0:9:4, :]
                v1 = t[:, 896:1024]
                g.affine_select(out=v3, in_=v3, compare_op=ALU.is_gt, fill=0.0, base=0,
                                pattern=[[0, 3], [1, P]], channel_multiplier=-1).then_inc(s, 1)
                g.affine_select(out=v1, in_=v1, compare_op=ALU.is_gt, fill=0.0, base=0,
                                pattern=[[1, P]], channel_multiplier=-1).then_inc(s, 1)

            for kind, k in STEPS:
                for p in pieces_here(kind, k):
                    low(k // 2 + 1, p)
                if kind == "tile":
                    what, ct = BLOCKS[k // 2][0], BLOCKS[k // 2][5] + k % 2
                    if what == "z" and ct >= 2 and (ct - 1) % 4:
                        y_sum(ct - 1)
                    elif what == "merge" and ct == 2:
                        g.wait_ge(squares, 6)
                        add_to(sq[:, 0, :], sq[:, 1, :])
                    elif what == "merge" and ct > 2:
                        g.wait_ge(squares, 4 + ct)
                        o = g.tensor_tensor(sq[:, 0, :], sq[:, 0, :], sq[:, ct - 1, :], ALU.add)
                        o.then_inc(squares_added, 1)
                        if ct < 7:
                            g.wait_ge(squares_added, ct - 2)
                elif kind == "y_sum":
                    y_sum(7)
                elif kind == "norm":
                    for t in range(1, KT, 2):
                        if t < 4:
                            low_piece(0, t // 2 * 4, t // 2 * 4 + 4, t // 2 + 1)
                        g.wait_ge(h_hi, t + 1)
                        g.tensor_tensor(hL[:, t, :], hf[:, t % 4, :], hH[:, t, :].bitcast(F32),
                                        ALU.subtract).then_inc(h_lo_odd, 1)
                elif kind == "sb_max":
                    g.wait_ge(sb_softplus, k + 1)
                    diag(sp, sb_softplus_masked)
                elif kind == "sb_cum":
                    g.wait_ge(sb_weights, k + 1)
                    diag(sw[k % 2], sb_weights_masked)
            def ff_low(slot, count):
                low_piece(slot, 0, KT // 2, count)
                low_piece(slot, KT // 2, KT, count + 1)

            with g.Fori(0, 15) as i:
                ff_low((NB + 1) % 2, i * 4 + (2 * NB + 3))
                ff_low(NB % 2, i * 4 + (2 * NB + 5))
            ff_low((NB + 1) % 2, 2 * NB + 63)
            for t in range(1, 7):
                g.wait_ge(squares, 12 + t + 1)
                if t > 1:
                    g.wait_ge(pool_chain, n_own[0])
                n_own[0] += 1
                g.tensor_tensor(sq[:, 0, :], sq[:, 0, :], sq[:, t, :], ALU.add).then_inc(pool_chain, 1)
            g.wait_ge(pool_chain, n_own[0])
            g.memset(small[:, 60:61], 0.0).then_inc(squares_summed, 1)
            g.wait_ge(final_w_in, 16)
            for t in range(1, TT):
                g.wait_ge(row_scaled, t)
                o = yrow[:, t, 512:1024]
                g.tensor_tensor(o, o, wrow[:, 512:1024], ALU.mult).then_inc(rows_of_pool, 1)

        @block.scalar
        def _(a):
            n_own = [0]

            def own(i):
                i.then_inc(scalar_chain, 1)
                n_own[0] += 1
                a.wait_ge(scalar_chain, n_own[0])

            def high_piece(slot, k0, k1):
                a.activation(w_hi[:, slot, k0:k1, :], raw[:, slot, k0:k1, :], ACT.Copy).then_inc(weights_hi, 1)

            def high(n, p):
                a.wait_ge(weights_in[n % 2], 16 * (n // 2 + 1))
                if n >= 2:
                    a.wait_ge(tile_done, 2 * (n - 1))
                high_piece(n % 2, *piece_rows(n, p))

            roots = [0]

            def root(n):
                roots[0] += 1
                a.wait_ge(root_in, roots[0])
                a.activation(stat[:, 0:n], stat[:, 0:n], ACT.Sqrt).then_inc(root_out, 1)

            def square(k, count):
                a.wait_ge(residual, count)
                a.activation(sq[:, k, :], xT[:, k, :], ACT.Square).then_inc(squares, 1)

            def ff_in(k):
                square(k, k + 1)
                a.activation(hH[:, k, :], xT[:, k, :], ACT.Copy,
                             scale=vec[:, V_FFN + k:V_FFN + k + 1]).then_inc(h_hi, 1)

            def split(src, dst, m):
                for k in range(m):
                    a.activation(dst[:, k, :], src[:, k, :], ACT.Copy).then_inc(operand_hi, 1)

            def y_square(t):
                a.wait_ge(y_gated, t + 1)
                a.activation(ysq[:, t, :], xs[:, t, :], ACT.Square).then_inc(y_squares, 1)

            for kind, k in STEPS:
                for p in pieces_here(kind, k):
                    high(k // 2 + 1, p)
                if kind == "load":
                    a.wait_ge(stat_set, 1)
                    own(a.activation(stat[:, 30:31], stat[:, 30:31], ACT.Sqrt))
                    for t in range(TT):
                        a.wait_ge(x_in[t], 16)
                        a.activation(sq[:, 0:2, :], xin[:, t, :].rearrange("p (a b) -> p a b", a=2), ACT.Square,
                                     accum_out=stat[:, t:t + 1]).then_inc(squares, 1)
                        a.wait_ge(squares, t + 1)
                    root(4)
                    a.wait_ge(weights_in[0], 16)
                    high_piece(0, 0, KT // 2)
                    a.wait_ge(x_turned, 1)
                    for t in (7, 1, 3, 5):
                        a.activation(xT[:, t, :], mx[:, t, :] if t < 6 else pj[1][:, :], ACT.Copy).then_inc(x_odd_ready, 1)
                elif kind == "norm":
                    high_piece(0, KT // 2, KT)
                    for t in range(KT):
                        a.wait_ge(h_made, t + 1)
                        a.activation(hH[:, t, :], hf[:, t % 4, :], ACT.Copy).then_inc(h_hi, 1)
                elif kind == "tile":
                    what, ct = BLOCKS[k // 2][0], BLOCKS[k // 2][5] + k % 2
                    if what == "gate":
                        a.wait_ge(tile_done, k + 1)
                        gi = gate_of(k)
                        if 2 <= gi < 16:
                            a.wait_ge(gate_used, gi - 1)
                        elif gi >= 20:
                            a.wait_ge(gate_used, gi - 3)
                        dst = gt[:, ct % 2, :] if gi < 16 else gt1[:, ct % 4, :]
                        a.activation(dst, bank(k), ACT.Tanh, scale=0.5).then_inc(gate_tanh, 1)
                    elif what == "z":
                        a.wait_ge(tile_done, k + 1)
                        a.wait_ge(*((y_gated, ct - 1) if ct >= 2 else (gate_used, 16)))
                        a.activation(gt[:, ct % 2, :], bank(k), ACT.Tanh, scale=0.5).then_inc(z_tanh, 1)
                        if ct >= 1:
                            y_square(ct - 1)
                    elif what == "merge":
                        if ct:
                            ff_in(ct - 1)
                elif kind == "dt_w":
                    a.wait_ge(dt_in, 16)
                    a.activation(wdtH[:, :, :], wdt[:, :, :], ACT.Copy).then_inc(dt_w_hi, 1)
                elif kind == "dt_turn":
                    a.wait_ge(row_in, 80)
                    own(a.activation(nega[:, :], nega[:, :], ACT.Exp))
                    a.wait_ge(dt_softplus_in, 1)
                    a.activation(dtt[:, 1, :], dtt[:, 1, :], ACT.Exp).then_inc(dt_exp, 1)
                    a.wait_ge(dt_softplus_in, 2)
                    a.activation(dtt[:, 3, :], dtt[:, 2, :], ACT.Ln).then_inc(dt_ln, 1)
                    a.wait_ge(dt_ready, 1)
                    a.activation(dtaH[:, :, :], dta[:, :, :], ACT.Copy).then_inc(dta_hi, 1)
                elif kind == "sb_parts_hi":
                    r0, o0, pt = 64 * (k % 2), 64 - 64 * (k % 2), k // 2
                    if k == 0:
                        cc = tile_of("ks", 3)
                        a.wait_ge(bank_read[cc % 2], read_count(cc))
                    else:
                        a.wait_ge(sb_scored, k)
                    for dst, src, d0 in ((qHL, qs, r0), (kHH, ks, r0), (kHH, ks, o0)):
                        a.activation(dst[d0:d0 + 64, :], src[r0:r0 + 64, pt, :], ACT.Copy).then_inc(sb_parts_hi, 1)
                elif kind == "sb_scores":
                    a.wait_ge(sb_clipped, k + 1)
                    a.activation(sw[k % 2][:, :], sw[k % 2][:, :], ACT.Exp).then_inc(sb_exp, 1)
                elif kind == "sb_ln":
                    a.wait_ge(sb_exp, k + 1)
                    a.activation(sw[k % 2][:, :], sw[k % 2][:, :], ACT.Ln, bias=1.0).then_inc(sb_ln, 1)
                elif kind == "sb_split":
                    a.wait_ge(sb_softplus_masked, 2 * (k + 1))
                    if k:
                        a.wait_ge(sb_summed, k)
                    a.activation(spH[:, :], sp[:, :], ACT.Copy).then_inc(sb_softplus_hi, 1)
                elif kind == "sb_cum":
                    a.wait_ge(sb_summed, k + 1)
                    b = 1536 * (k % 2)
                    a.activation(sw[k % 2][:, :], mxf[:, b:b + 1280], ACT.Exp).then_inc(sb_weights, 1)
                elif kind == "silu":
                    cc = tile_of("xbc", k)
                    a.wait_ge(bank_read[cc % 2], read_count(cc))
                    a.wait_ge(*((conv_silu, k - 1) if k >= 2 else (operand_lo, 4)))
                    a.activation(cth[:, k % 2, :], xs[:, k, :], ACT.Tanh).then_inc(conv_tanh, 1)
                elif kind == "swa_scores":
                    a.wait_ge(swa_max, k + 1)
                    k0, o, p_ = (P if k // 2 == 0 else CHUNK), 16 * (k % 2), pr[k % 2]
                    for hh in range(4):
                        own(a.activation(p_[:, hh, k0:256], p_[:, hh, k0:256], ACT.Exp,
                                         bias=small[:, o + 4 + hh:o + 5 + hh],
                                         accum_out=small[:, o + 12 + hh:o + 13 + hh]))
                    a.activation(small[:, o + 8:o + 12], small[:, o + 8:o + 12], ACT.Exp).then_inc(swa_exp, 1)
                elif kind == "swa_turn":
                    if k >= 2:
                        a.wait_ge(swa_turned, k + 1)
                        a.wait_ge(swa_product, k)
                        a.activation(pT[:, 0, :], mx[:, 2, :], ACT.Copy).then_inc(swa_turned_first, 1)
                elif kind == "split_c":
                    a.wait_ge(sb_out, SB_HEADS)
                    split(qs, oH, 4)
                elif kind == "split_a":
                    a.wait_ge(swa_out, 8)
                    a.wait_ge(tile_done, tile_of("u2", 7) + 1)
                    split(qa, oH, 4)
                elif kind == "y_sum":
                    y_square(7)
                elif kind == "y_norm":
                    root(8)
                elif kind == "split_b":
                    if k < KT:
                        a.wait_ge(y_normed, k + 1)
                        a.activation(obH[:, k, :], xs[:, k, :], ACT.Copy).then_inc(operand_hi, 1)
                elif kind == "split_m":
                    a.wait_ge(gate_used, 16 + k + 1)
                    a.activation(mH[:, k, :], mg[:, k, :], ACT.Copy, scale=0.5).then_inc(operand_hi, 1)
                elif kind == "decay":
                    a.wait_ge(ssd_decay_in, 1)
                    a.activation(dec[:, :, :, :], dec[:, :, :, :], ACT.Exp).then_inc(ssd_decay_exp, 1)
                elif kind == "ssd_sum":
                    b = mx[:, 4 + k % 2, :].rearrange("p (q two t) -> p q two t", two=2, t=P)
                    a.wait_ge(ssd_diff, k + 1)
                    if k >= 4:
                        if k >= 6:
                            a.wait_ge(ssd_y_made, 2 * (k - 1))
                        a.activation(e2[k % 2][0:64, :, :], b[0:64, :, 0, :], ACT.Exp).then_inc(scalar_chain, 1)
                        a.activation(e2[k % 2][64:128, :, :], b[64:128, :, 1, :], ACT.Exp).then_inc(scalar_chain, 1)
                        n_own[0] += 2
                    a.activation(mt[k % 2][:, :, :], mt[k % 2][:, :, :], ACT.Exp).then_inc(ssd_exp, 1)

            def ff_high(m, p):
                slot = (NB + p) % 2
                a.wait_ge(weights_in[slot], m * 16 + 16 * ((NB + p) // 2 + 1))
                a.wait_ge(tile_done, m * 4 + 2 * (NB + p - 1))
                high_piece(slot, 0, KT // 2)
                high_piece(slot, KT // 2, KT)

            ff_in(7)
            for half in range(2):
                if half:
                    ff_high(half * 8, 0)
                with a.Fori(0, 4) as i:
                    for s in range(4):
                        if s % 2 == 0:
                            ff_high(half * 8 + i + s // 2, 1 - s // 2)
                        n = half * 16 + i * 4 + s
                        a.wait_ge(relu, n + 5)
                        a.activation(rsq[:, s % 2, :], rel[:, s % 2, :], ACT.Square).then_inc(relu_sq, 1)
                        a.wait_ge(relu_sq, n + 1)
                        a.activation(aH[:, bass.ds(i * 4 + s, 1), :], rsq[:, s % 2, :].unsqueeze(1),
                                     ACT.Copy).then_inc(act_hi, 1)
                with a.Fori(0, 3) as i:
                    ff_high(half * 8 + i + 4, 1)
                    ff_high(half * 8 + i + 5, 0)
                ff_high(half * 8 + 7, 1)
            own(a.activation(stat[:, 30:31], stat[:, 30:31], ACT.Sqrt))
            for k in range(KT):
                square(k, 16 + k + 1)
            root(4)
            a.wait_ge(root_out, 3)
            for t in range(1, TT):
                a.wait_ge(rows_turned1, t + 1)
                a.activation(yrow[:, t, 512:1024], outb[1][t], ACT.Copy, scale=stat[:, t:t + 1]).then_inc(row_scaled, 1)

        @block.vector
        def _(v):
            n_own = [0]

            def own(i):
                i.then_inc(vector_chain, 1)
                n_own[0] += 1
                v.wait_ge(vector_chain, n_own[0])

            roots = [0]

            def mean(src, n, m):
                own(v.tensor_scalar(stat[:, 0:n], src, 1.0 / m, EPS, ALU.mult, ALU.add))
                v.reciprocal(stat[:, 0:n], stat[:, 0:n]).then_inc(root_in, 1)

            def norm(rs):
                def lo(k):
                    v.wait_ge(h_hi, k + 1)
                    v.tensor_tensor(hL[:, k, :], hf[:, k % 4, :], hH[:, k, :].bitcast(F32),
                                    ALU.subtract).then_inc(h_lo_even, 1)
                for k in range(KT):
                    if k % 2:
                        v.wait_ge(x_odd_ready, min(4, k // 2 + 2))
                    if k >= 4:
                        v.wait_ge(*((h_lo_odd, k // 2 - 1) if k % 2 else (h_lo_even, k // 2 - 1)))
                    v.scalar_tensor_tensor(out=hf[:, k % 4, :], in0=xT[:, k, :],
                                           scalar=vec[:, V_MIX + k:V_MIX + k + 1],
                                           in1=rs, op0=ALU.mult, op1=ALU.mult).then_inc(h_made, 1)
                    if k % 2:
                        lo(k - 1)

            def ff_in_lo(k):
                v.wait_ge(h_hi, 8 + k + 1)
                v.scalar_tensor_tensor(out=hL[:, k, :], in0=xT[:, k, :], scalar=vec[:, V_FFN + k:V_FFN + k + 1],
                                       in1=hH[:, k, :].bitcast(F32), op0=ALU.mult,
                                       op1=ALU.subtract).then_inc(ff_input_lo, 1)

            def split(start, src, hi, dst, m):
                for k in range(m):
                    v.wait_ge(operand_hi, start + k + 1)
                    v.tensor_tensor(dst[:, k, :], src[:, k, :], hi[:, k, :].bitcast(F32),
                                    ALU.subtract).then_inc(operand_lo, 1)

            def by_head(t):
                return t.rearrange("p (h e) -> p h e", h=16)

            def over_head(t):
                return t.unsqueeze(2).broadcast_to([P, 16, HD])

            for kind, k in STEPS:
                if kind == "load":
                    v.memset(stat[:, :], 1.0).then_inc(stat_set, 1)
                    own(v.memset(small[:, :], 0.0))
                    v.wait_ge(constants, 1)
                    for dst, src in ((neg_triR, neg_tri), (neg_oneR, neg_one), (triR, tri)):
                        v.tensor_copy(dst[:, :], src[:, :]).then_inc(constants_r, 1)
                    v.wait_ge(squares, 4)
                    mean(stat[:, 0:4], 4, D)
                    v.wait_ge(x_turned, 1)
                    for t in range(0, KT, 2):
                        v.tensor_copy(xT[:, t, :], mx[:, t, :] if t < 6 else pj[0][:, :]).then_inc(x_even_ready, 1)
                elif kind == "norm":
                    v.wait_ge(vec_turned, 1)
                    own(v.tensor_copy(vec[:, 0:V_ROWS], pj[1][:, 0:V_ROWS]))
                    v.tensor_scalar(vec[:, V_CW:V_SSDN], vec[:, V_CW:V_SSDN], 0.5, None, ALU.mult).then_inc(vec_ready, 1)
                    v.wait_ge(vec_ready, 1)
                    v.wait_ge(x_even_ready, 4)
                    v.wait_ge(rstd_spread, 1)
                    norm(mx[:, 0, :])
                    v.wait_ge(bias_rows, 1)
                    v.tensor_copy(frow[0:SWA_HEADS, :], mx[0:SWA_HEADS, 4, 0:320]).then_inc(bias_copied, 1)
                elif kind == "tile":
                    what, ct = BLOCKS[k // 2][0], BLOCKS[k // 2][5] + k % 2
                    src, fs = bank(k), bank_read[k % 2]
                    if what == "gate":
                        continue
                    v.wait_ge(tile_done, k + 1)
                    if what == "qs":
                        v.tensor_scalar(qs[:, ct, :], src, HD ** -0.5, None, ALU.mult).then_inc(fs, 1)
                    elif what in ("ks", "vs", "qa"):
                        dst = {"ks": ks, "vs": vsT, "qa": qa}[what]
                        v.tensor_copy(dst[:, ct, :], src).then_inc(fs, 1)
                    elif what == "kava" and ct == 0:
                        for g2 in range(2):
                            for half in range(2):
                                o = v.tensor_copy(kd[64 * half:64 * half + 64, g2, :],
                                                  pj[k % 2][64 * g2:64 * g2 + 64, :])
                        o.then_inc(fs, 1)
                    elif what == "kava":
                        v.tensor_copy(vaT[:, :], src).then_inc(fs, 1)
                    elif what == "xbc":
                        if ct < 4:
                            v.wait_ge(v_turned, 4)
                        w = [vec[:, V_CW + 12 * j + ct:V_CW + 12 * j + ct + 1] for j in range(CONV)]
                        own(v.tensor_scalar(xs[:, ct, :], src, w[3], vec[:, V_CB + ct:V_CB + ct + 1],
                                            ALU.mult, ALU.add))
                        for j in range(3):
                            sh = 3 - j
                            add = v.scalar_tensor_tensor(
                                out=xs[:, ct, sh:T], in0=pj[k % 2][:, 0:T - sh], scalar=w[j],
                                in1=xs[:, ct, sh:T], op0=ALU.mult, op1=ALU.add)
                            if j < 2:
                                own(add)
                        add.then_inc(fs, 1)
                    elif what in ("u0", "u1", "u2"):
                        gi = gate_of(k)
                        v.wait_ge(gate_tanh, gi + 1)
                        gate = gt[:, ct % 2, :] if gi < 16 else gt1[:, ct % 4, :]
                        v.scalar_tensor_tensor(out=mg[:, ct, :] if gi < 8 else gu[:, :], in0=gate, scalar=1.0,
                                               in1=src, op0=ALU.add, op1=ALU.mult).then_inc(fs, 1)
                        v.wait_ge(fs, read_count(k))
                        if gi < 8:
                            v.tensor_copy(small[:, 79:80], small[:, 78:79]).then_inc(gate_used, 1)
                        else:
                            v.tensor_tensor(mg[:, ct, :], mg[:, ct, :], gu[:, :], ALU.add).then_inc(gate_used, 1)
                            v.wait_ge(gate_used, gi + 1)
                    elif what == "z":
                        v.wait_ge(z_tanh, ct + 1)
                        v.scalar_tensor_tensor(out=gt[:, ct % 2, :], in0=gt[:, ct % 2, :], scalar=1.0, in1=src,
                                               op0=ALU.add, op1=ALU.mult).then_inc(fs, 1)
                        v.wait_ge(fs, read_count(k))
                        v.scalar_tensor_tensor(out=xs[:, ct, :], in0=gt[:, ct % 2, :], scalar=0.5, in1=xs[:, ct, :],
                                               op0=ALU.mult, op1=ALU.mult).then_inc(y_gated, 1)
                    elif what == "merge":
                        v.tensor_tensor(xT[:, ct, :], xT[:, ct, :], src, ALU.add).then_inc(residual, 1)
                        if ct:
                            ff_in_lo(ct - 1)
                elif kind == "vs_turn":
                    for ct in range(4):
                        v.wait_ge(v_turned, ct + 1)
                        v.tensor_copy(vs[:, :, P * ct:P * ct + P],
                                      mx[:, ct, :].rearrange("p (t c) -> p t c", t=TT)).then_inc(v_copied, 1)
                elif kind == "va_turn":
                    v.wait_ge(v_turned, 5)
                    v.tensor_copy(va[:, :, :], mx[:, 4, :].rearrange("p (t c) -> p t c", t=TT)).then_inc(v_copied, 1)
                elif kind == "dt_w":
                    v.wait_ge(dt_w_hi, 1)
                    v.tensor_tensor(wdtL[:, :, :], wdt[:, :, :], wdtH[:, :, :].bitcast(F32),
                                    ALU.subtract).then_inc(dt_w_lo, 1)
                elif kind == "dt":
                    v.wait_ge(dt_product, 1)
                    v.tensor_copy(dtr[0:16, :], mx[0:16, 5, :]).then_inc(dt_rows, 1)
                elif kind == "dt_turn":
                    v.wait_ge(dt_product, 2)
                    v.wait_ge(row_in, 80)
                    x_, u_, w_, l_ = (dtt[:, j, :] for j in range(4))
                    own(v.tensor_tensor(x_.rearrange("p (t h) -> p t h", t=TT),
                                        mx[:, 5, 0:64].rearrange("p (t h) -> p t h", t=TT),
                                        dtb[:, :].unsqueeze(1).broadcast_to([P, TT, 16]), ALU.add))
                    own(v.tensor_scalar(u_, x_, -1.0, None, ALU.mult))
                    v.tensor_tensor(u_, u_, x_, ALU.min).then_inc(dt_softplus_in, 1)
                    v.wait_ge(dt_exp, 1)
                    v.tensor_scalar(w_, u_, 1.0, None, ALU.add).then_inc(dt_softplus_in, 1)
                    v.wait_ge(dt_ln, 1)
                    m_, d_ = dta[:, :, :].rearrange("p t h -> p (t h)"), dtv[:, :, :].rearrange("p t h -> p (t h)")
                    own(v.tensor_scalar(m_, w_, 1.0, None, ALU.is_equal))
                    own(v.tensor_scalar(d_, w_, -1.0, None, ALU.add))
                    own(v.tensor_tensor(d_, d_, m_, ALU.add))
                    own(v.tensor_tensor(l_, l_, m_, ALU.add))
                    own(v.reciprocal(d_, d_))
                    own(v.tensor_tensor(l_, l_, u_, ALU.mult))
                    own(v.tensor_tensor(l_, l_, d_, ALU.mult))
                    own(v.scalar_tensor_tensor(out=d_, in0=x_, scalar=0.0, in1=l_, op0=ALU.max, op1=ALU.add))
                    v.scalar_tensor_tensor(out=dta[:, :, :], in0=dtv[:, :, :], scalar=-1.0,
                                           in1=nega[:, :].unsqueeze(1).broadcast_to([P, TT, 16]),
                                           op0=ALU.mult, op1=ALU.mult).then_inc(dt_ready, 1)
                    v.wait_ge(dta_hi, 1)
                    v.tensor_tensor(dtaL[:, :, :], dta[:, :, :], dtaH[:, :, :].bitcast(F32),
                                    ALU.subtract).then_inc(dta_lo, 1)
                elif kind == "sb_parts_lo":
                    r0, o0, pt = 64 * (k % 2), 64 - 64 * (k % 2), k // 2
                    v.wait_ge(sb_parts_hi, 3 * k + 1)
                    v.tensor_tensor(qHL[o0:o0 + 64, :], qs[r0:r0 + 64, pt, :], qHL[r0:r0 + 64, :].bitcast(F32),
                                    ALU.subtract).then_inc(sb_parts_lo, 1)
                    v.wait_ge(sb_parts_hi, 3 * k + 2)
                    v.tensor_tensor(kL[r0:r0 + 64, :], ks[r0:r0 + 64, pt, :], kHH[r0:r0 + 64, :].bitcast(F32),
                                    ALU.subtract).then_inc(sb_parts_lo, 1)
                elif kind == "sb_scores":
                    b = 1536 * (k % 2)
                    v.wait_ge(sb_scored, k + 1)
                    v.tensor_scalar(sw[k % 2][:, :], mxf[:, b:b + 1280], 40.0, None, ALU.min).then_inc(sb_clipped, 1)
                elif kind == "sb_max":
                    b = 1536 * (k % 2)
                    v.wait_ge(sb_ln, k + 1)
                    if k:
                        v.wait_ge(sb_softplus_lo, k)
                    v.tensor_tensor(sp[:, :], mxf[:, b:b + 1280], sw[k % 2][:, :], ALU.max).then_inc(sb_softplus, 1)
                elif kind == "sb_split":
                    v.wait_ge(sb_softplus_hi, k + 1)
                    v.tensor_tensor(spL[:, :], sp[:, :], spH[:, :].bitcast(F32), ALU.subtract).then_inc(sb_softplus_lo, 1)
                elif kind == "sb_av":
                    r0 = 64 * (k % 2)
                    v.wait_ge(sb_product, k + 1)
                    v.tensor_copy(qs[r0:r0 + 64, k // 2, :], mx[r0:r0 + 64, 3 * (k % 2), :]).then_inc(sb_out, 1)
                elif kind == "bias":
                    v.wait_ge(bias_flipped, 1)
                    own(v.tensor_copy(tbias[:, :, :].rearrange("p h k -> p (h k)"), mxf[:, 0:1536]))
                    v.wait_ge(row_in, 80)
                    own(v.tensor_copy(small[:, 64:72].rearrange("p (g two q) -> p g q two", g=2, two=2),
                                      sink[:, :].rearrange("p (g q two) -> p g q two", g=2, two=2)))
                    own(v.memset(tbias[0:64, :, P:KEYS], -3.0e38))
                    v.memset(tbias[64:128, :, 0:CHUNK], -3.0e38).then_inc(bias_ready, 1)
                elif kind == "p_zero":
                    for j in range(2):
                        own(v.memset(pr[j][:, :, 0:CHUNK], 0.0))
                elif kind == "silu_mul":
                    v.wait_ge(conv_tanh, k + 1)
                    v.scalar_tensor_tensor(out=xs[:, k, :], in0=cth[:, k % 2, :], scalar=1.0, in1=xs[:, k, :],
                                           op0=ALU.add, op1=ALU.mult).then_inc(conv_silu, 1)
                elif kind == "swa_scores":
                    i, gq, o, p_ = k // 2, k % 2, 16 * (k % 2), pr[k % 2]
                    k0 = CHUNK if i == 0 else 0
                    s4 = mxf[:, 0:1024].rearrange("p (h k) -> p h k", h=4)
                    snk = small[:, 64 + 4 * gq:68 + 4 * gq]
                    v.wait_ge(swa_scored, k + 1)
                    if k >= 2:
                        v.wait_ge(swa_turned, k - 1)
                    v.scalar_tensor_tensor(out=p_[:, :, CHUNK + k0:256], in0=s4[:, :, k0:KEYS], scalar=HD ** -0.5,
                                           in1=tbias[:, 4 * gq:4 * gq + 4, k0:KEYS], op0=ALU.mult,
                                           op1=ALU.add).then_inc(swa_biased, 1)
                    v.wait_ge(swa_biased, k + 1)
                    own(v.tensor_reduce(small[:, o:o + 4], p_[:, :, CHUNK + k0:256], AX.X, ALU.max))
                    own(v.tensor_tensor(small[:, o:o + 4], small[:, o:o + 4], snk, ALU.max))
                    own(v.tensor_scalar(small[:, o + 4:o + 8], small[:, o:o + 4], -1.0, None, ALU.mult))
                    v.tensor_tensor(small[:, o + 8:o + 12], snk, small[:, o + 4:o + 8], ALU.add).then_inc(swa_max, 1)
                elif kind == "swa_norm":
                    o, k0, p_ = 16 * (k % 2), (P if k // 2 == 0 else CHUNK), pr[k % 2]
                    v.wait_ge(swa_exp, k + 1)
                    own(v.tensor_tensor(small[:, o + 8:o + 12], small[:, o + 8:o + 12], small[:, o + 12:o + 16],
                                        ALU.add))
                    own(v.reciprocal(small[:, o + 8:o + 12], small[:, o + 8:o + 12]))
                    v.tensor_tensor(p_[:, :, k0:256], p_[:, :, k0:256],
                                    small[:, o + 8:o + 12].unsqueeze(2).broadcast_to([P, 4, 256 - k0]),
                                    ALU.mult).then_inc(swa_normed, 1)
                elif kind == "swa_turn":
                    v.wait_ge(swa_turned, k + 1)
                    if k:
                        v.wait_ge(swa_product, k)
                    v.tensor_copy(pT[:, 1, :], mx[:, 3, :]).then_inc(swa_turned_copied, 1)
                elif kind == "swa_pv":
                    i, gq = k // 2, k % 2
                    v.wait_ge(swa_product, k + 1)
                    v.tensor_copy(qa[:, 2 * gq:2 * gq + 2, P * i:P * i + P],
                                  mx[:, 4, 0:256].rearrange("p (q t) -> p q t", q=2)).then_inc(swa_out, 1)
                elif kind == "split_c":
                    split(SPLIT[kind], qs, oH, oL, 4)
                elif kind == "split_a":
                    split(SPLIT[kind], qa, oH, oL, 4)
                elif kind == "y_norm":
                    v.wait_ge(y_mean_sq, 1)
                    mean(mx[:, 5, 0:8], 8, 512)
                elif kind == "split_b":
                    v.wait_ge(rstd_spread, 2)
                    if k < KT:
                        v.scalar_tensor_tensor(out=xs[:, k, :], in0=xs[:, k, :],
                                               scalar=vec[:, V_SSDN + k:V_SSDN + k + 1], in1=mx[:, 3 + k // 4, :],
                                               op0=ALU.mult, op1=ALU.mult).then_inc(y_normed, 1)
                    if k >= 2:
                        v.wait_ge(operand_hi, SPLIT[kind] + k - 1)
                        v.tensor_tensor(obL[:, k - 2, :], xs[:, k - 2, :], obH[:, k - 2, :].bitcast(F32),
                                        ALU.subtract).then_inc(operand_lo, 1)
                elif kind == "split_m":
                    v.wait_ge(operand_hi, SPLIT[kind] + k + 1)
                    v.scalar_tensor_tensor(out=mL[:, k, :], in0=mg[:, k, :], scalar=0.5,
                                           in1=mH[:, k, :].bitcast(F32), op0=ALU.mult,
                                           op1=ALU.subtract).then_inc(operand_lo, 1)
                elif kind == "decay":
                    v.wait_ge(ssd_cumsums, 1)
                    own(v.tensor_copy(acum[:, :, :].rearrange("p t h -> p (t h)"), mx[:, 5, 0:64]))
                    own(v.tensor_tensor(dec[:, 0, :, :].rearrange("p t h -> p (t h)"), mx[:, 5, 64:128],
                                        acum[:, :, :].rearrange("p t h -> p (t h)"), ALU.subtract))
                    v.tensor_copy(dec[:, 1, :, :].rearrange("p t h -> p (t h)"), mx[:, 5, 64:128]).then_inc(ssd_decay_in, 1)
                elif kind == "ssd_prep":
                    v.wait_ge(ssd_turned, k + 1)
                    v.wait_ge(ssd_decay_exp, 1)
                    if k == 1:
                        v.wait_ge(operand_lo, 8)
                    own(v.tensor_copy(bt[:, :, :].rearrange("p g n -> p (g n)"), mx[:, 2, 0:256]))
                    own(v.tensor_tensor(cbm[k % 2][:, :, :], mx[:, 2, 256:512].rearrange("p (g t) -> p g t", g=2),
                                        tri[:, :].unsqueeze(1).broadcast_to([P, 2, P]), ALU.mult))
                    own(v.tensor_tensor(by_head(xd[k % 2][:, :]), by_head(mxf[:, 0:1024]), over_head(dtv[:, k, :]), ALU.mult))
                    v.tensor_tensor(by_head(xw[:, :]), by_head(xd[k % 2][:, :]), over_head(dec[:, 0, k, :]),
                                    ALU.mult).then_inc(ssd_inputs, 1)
                elif kind == "ssd_sum":
                    c, r = k // 4, k % 4
                    v.wait_ge(ssd_sums_spread, k + 1)
                    if k >= 2:
                        v.wait_ge(ssd_product, k - 1)
                    b = mx[:, 4 + k % 2, :].rearrange("p (h t) -> p h t", h=4)
                    for hh in range(4):
                        o = v.tensor_scalar(mt[k % 2][:, hh, :], b[:, hh, :], acum[:, c, 4 * r + hh:4 * r + hh + 1],
                                            0.0, ALU.subtract, ALU.min)
                    o.then_inc(ssd_diff, 1)
                elif kind == "ssd_mul":
                    m_, cb = mt[k % 2], cbm[k // 4 % 2]
                    v.wait_ge(ssd_exp, k + 1)
                    if k % 4 == 0:
                        v.wait_ge(ssd_inputs, k // 4 + 1)
                    v.tensor_tensor(m_[:, :, :], m_[:, :, :],
                                    cb[:, k % 4 // 2, :].unsqueeze(1).broadcast_to([P, 4, P]),
                                    ALU.mult).then_inc(ssd_matrix, 1)
                elif kind == "ssd_y":
                    c, r = k
                    n = 4 * c + r
                    v.wait_ge(ssd_product, n + 1)
                    yd = mx[:, 3, 0:256].rearrange("p (q t) -> p q t", q=2)
                    yo = mx[:, 3, 256:512].rearrange("p (q t) -> p q t", q=2)
                    if c > 0:
                        own(v.tensor_tensor(t1[:, :, :], yo, e2[n % 2][:, :, :], ALU.mult))
                        own(v.tensor_tensor(t1[:, :, :], t1[:, :, :], yd, ALU.add))
                    for q in range(2):
                        pt = 2 * r + q
                        tile = xs[:, pt, P * c:P * c + P]
                        v.scalar_tensor_tensor(out=tile, in0=tile, scalar=dsk[:, pt:pt + 1],
                                               in1=t1[:, q, :] if c > 0 else yd[:, q, :],
                                               op0=ALU.mult, op1=ALU.add).then_inc(ssd_y_made, 1)
                    v.wait_ge(ssd_y_made, 2 * n + 2)
                elif kind == "ssd_state":
                    v.wait_ge(ssd_state_product, k + 1)
                    new = mxf[:, 0:1024]
                    if k == 0:
                        v.tensor_copy(st[0][:, :], new).then_inc(ssd_state_made, 1)
                    else:
                        own(v.tensor_tensor(by_head(st[k % 2][:, :]), by_head(st[(k - 1) % 2][:, :]),
                                            over_head(dec[:, 1, k, :]), ALU.mult))
                        v.tensor_tensor(st[k % 2][:, :], st[k % 2][:, :], new, ALU.add).then_inc(ssd_state_made, 1)
                    v.wait_ge(ssd_state_made, k + 1)

            ff_in_lo(7)
            v.wait_ge(mean_sq, 1)
            own(v.tensor_scalar(stat[:, 0:4], mx[:, 5, 0:4], 1.0 / D, EPS, ALU.mult, ALU.add))
            v.reciprocal(stat[:, 0:4], stat[:, 0:4]).then_inc(r2_made, 1)
            v.tensor_copy(small[:, 76:77], small[:, 78:79]).then_inc(relu, 4)
            for half in range(2):
                with v.Fori(0, 4) as i:
                    for s in range(4):
                        n = half * 16 + i * 4 + s
                        v.wait_ge(tile_done, half * 32 + i * 4 + (2 * NB + s + 1))
                        v.tensor_scalar(rel[:, s % 2, :], ffb[s], 0.0, None, ALU.max).then_inc(relu, 1)
                        v.wait_ge(act_hi, n + 1)
                        v.tensor_tensor(aL[:, bass.ds(i * 4 + s, 1), :], rsq[:, s % 2, :].unsqueeze(1),
                                        aH[:, bass.ds(i * 4 + s, 1), :].bitcast(F32), ALU.subtract).then_inc(act_lo, 1)
                        v.wait_ge(act_lo, n + 1)
                if half == 0:
                    v.wait_ge(rstd_spread, 3)
                    own(v.tensor_copy(r2[:, :], mx[:, 4, :]))
                with v.Fori(0, 4) as i:
                    for s in range(2):
                        v.wait_ge(tile_done, half * 32 + i * 4 + (2 * NB + 16 + 3 + s))
                        o = xT[:, bass.ds(i * 2 + s, 1), :]
                        v.tensor_tensor(fsc[:, :], mx[:, 2 + s, :], r2[:, :], ALU.mult).then_inc(ff_scaled, 1)
                        v.wait_ge(ff_scaled, half * 8 + i * 2 + (s + 1))
                        v.tensor_tensor(o, o, fsc[:, :].unsqueeze(1), ALU.add).then_inc(residual, 1)
                        v.wait_ge(residual, half * 8 + i * 2 + (8 + s + 1))
            v.wait_ge(mean_sq, 2)
            mean(mx[:, 4, 0:4], 4, D)
            v.wait_ge(root_out, 3)
            v.wait_ge(final_w_in, 16)
            for t, hh in ((0, 0), (0, 1), (1, 0), (2, 0), (3, 0)):
                v.wait_ge(*((rows_turned1, 1) if hh else (rows_turned0, t + 1)))
                v.scalar_tensor_tensor(out=yrow[:, t, 512 * hh:512 * hh + 512], in0=outb[hh][t],
                                       scalar=stat[:, t:t + 1], in1=wrow[:, 512 * hh:512 * hh + 512],
                                       op0=ALU.mult, op1=ALU.mult).then_inc(rows_of_vector, 1)

        @block.tensor
        def _(pe):
            def bank_free(c):
                if c < 2:
                    pe.wait_ge(*((vec_ready, 1) if c else (x_even_ready, 4)))
                    return
                what, p = BLOCKS[(c - 2) // 2][0], c - 2
                if what == "gate":
                    pe.wait_ge(gate_tanh, gate_of(p) + 1)
                elif what == "merge":
                    pe.wait_ge(residual, BLOCKS[p // 2][5] + p % 2 + 1)
                else:
                    pe.wait_ge(bank_read[p % 2], read_count(p))

            def pass3(dst, slot, s, k, hi, lo, start, stop):
                wh, wl = w_hi[:, slot, k, P * s:P * s + P], w_lo[:, slot, k, P * s:P * s + P]
                pe.matmul(dst, wh, hi, start=start, stop=False)
                pe.matmul(dst, wl, hi, start=False, stop=False)
                return pe.matmul(dst, wh, lo, start=False, stop=stop)

            def product(dst, slot, s, hi, lo, kts, k0=0, start=True, stop=True, ks=None, ready=None):
                for k in ks or range(kts):
                    if ready:
                        ready(k)
                    m = pass3(dst, slot, s, k, hi[:, k0 + k, :], lo[:, k0 + k, :], start and k == 0,
                              stop and k == kts - 1)
                return m

            def pair(dst, slot, hi, lo, kts, ready):
                order = [(k, s) for k in range(kts - 2) for s in range(2)]
                order += [(k, s) for s in range(2) for k in range(kts - 2, kts)]
                seen = -1
                for k, s in order:
                    if k > seen:
                        ready(k)
                        seen = k
                    m = pass3(dst[s], slot, s, k, hi[:, k, :], lo[:, k, :], k == 0, k == kts - 1)
                    if k == kts - 1:
                        m.then_inc(tile_done, 1)

            def h_ready(k):
                weights_ready(k, KT, 2)
                pe.wait_ge(*((h_lo_odd, k // 2 + 1) if k % 2 else (h_lo_even, k // 2 + 1)))

            def weights_ready(k, kts, count):
                if k == 0:
                    pe.wait_ge(weights_lo, count - 1)
                elif k == kts // 2:
                    pe.wait_ge(weights_lo, count)

            def stats(dst, src, first):
                for t in range(TT):
                    m = pe.matmul(dst[:, t:t + 1], src[:, P * t:P * t + P], ones[:, 0:1], start=first and t == 0,
                                  stop=False, skip_group_check=True)
                return m

            def spread(dst, col):
                for t in range(TT):
                    m = pe.matmul(dst[:, P * t:P * t + P], stat[:, col + t:col + t + 1].broadcast_to([P, P]),
                                  ident[:, :], start=True, stop=True)
                return m

            def kv_ready(kind, ct):
                cc = tile_of(kind, ct)
                pe.wait_ge(bank_read[cc % 2], read_count(cc))

            pe.wait_ge(constants, 1)
            for kind, k in STEPS:
                if kind == "load":
                    for t in range(TT):
                        pe.wait_ge(x_in[t], 16)
                        for j in range(KT):
                            dst = mx[:, j, :] if j < 6 else pj[j - 6][:, :]
                            m = pe.transpose(dst[:, P * t:P * t + P], xin[:, t, P * j:P * j + P], ident[:, :])
                    m.then_inc(x_turned, 1)
                elif kind == "norm":
                    pe.wait_ge(vec_in, 80)
                    pe.wait_ge(x_odd_ready, 1)
                    pe.transpose(pj[1][:, 0:V_ROWS], vrow[0:V_ROWS, :], ident[0:V_ROWS, 0:V_ROWS]).then_inc(vec_turned, 1)
                    pe.wait_ge(x_even_ready, 1)
                    pe.wait_ge(root_out, 1)
                    spread(mx[:, 0, :], 0).then_inc(rstd_spread, 1)
                    pe.wait_ge(rel_in, 32)
                    pe.wait_ge(x_even_ready, 3)
                    pe.matmul(mx[0:SWA_HEADS, 4, 0:320], relb[0:BUCKETS, :], onehot[0:BUCKETS, :],
                              start=True, stop=True).then_inc(bias_rows, 1)
                elif kind in ("half", "tile"):
                    n, s = k // 2, k % 2
                    what, _, _, kts, _, first = BLOCKS[n]
                    hi, lo, at = {"u0": (oH, oL, 4), "u2": (oH, oL, 0), "u1": (obH, obL, 8),
                                  "merge": (mH, mL, 16)}.get(what, (hH, hL, None))
                    if n == 0:
                        if s == 0:
                            bank_free(0)
                            bank_free(1)
                            pair([bank(0), bank(1)], 0, hi, lo, kts, h_ready)
                        continue
                    rows = range(kts)
                    if k in HALVED:
                        rows = rows[:kts // 2] if kind == "half" else rows[kts // 2:]
                    if rows[0] == 0:
                        bank_free(k)

                    def ready(j):
                        if s == 0:
                            weights_ready(j, kts, 2 * n + 2)
                        if at is not None and first + s == 0:
                            pe.wait_ge(operand_lo, at + j + 1)

                    m = product(bank(k), n % 2, s, hi, lo, kts, ks=rows, ready=ready)
                    if rows[-1] == kts - 1:
                        m.then_inc(tile_done, 1)
                elif kind == "vs_turn":
                    for ct in range(4):
                        kv_ready("vs", ct)
                        for t in range(TT):
                            m = pe.transpose(mx[:, ct, P * t:P * t + P], vsT[:, ct, P * t:P * t + P], ident[:, :])
                        m.then_inc(v_turned, 1)
                elif kind == "va_turn":
                    kv_ready("kava", 1)
                    pe.wait_ge(sb_out, SB_HEADS)
                    for t in range(TT):
                        m = pe.transpose(mx[:, 4, P * t:P * t + P], vaT[:, P * t:P * t + P], ident[:, :])
                    m.then_inc(v_turned, 1)
                elif kind == "dt":
                    pe.wait_ge(dt_w_lo, 1)
                    for k in range(KT):
                        for n, (l, r) in enumerate(((wdtH, hH), (wdtL, hH), (wdtH, hL))):
                            m = pe.matmul(mx[:, 5, :], l[:, k, :], r[:, k, :], start=k == 0 and n == 0,
                                          stop=k == KT - 1 and n == 2)
                    m.then_inc(dt_product, 1)
                elif kind == "dt_turn":
                    pe.wait_ge(dt_rows, 1)
                    for t in range(TT):
                        m = pe.transpose(mx[:, 5, 16 * t:16 * t + 16], dtr[0:16, P * t:P * t + P], ident[0:16, 0:16])
                    m.then_inc(dt_product, 1)
                elif kind == "sb_scores":
                    r0, b = 64 * (k % 2), 1536 * (k % 2)
                    pe.wait_ge(sb_parts_hi, 3 * (k + 1))
                    pe.wait_ge(sb_parts_lo, 2 * (k + 1))
                    if k == 0:
                        pe.wait_ge(v_copied, 4)
                        pe.wait_ge(bias_ready, 1)
                    elif k == 1:
                        pe.wait_ge(dt_softplus_in, 1)
                    else:
                        pe.wait_ge(sb_out, k - 1)
                    for j in range(TT):
                        dst, ky, qu = mxf[:, b + cols[j]:b + cols[j] + T - P * j], slice(P * j, P * j + P), slice(P * j, T)
                        pe.matmul(dst, kHH[:, ky], qHL[:, qu], start=j < 3, stop=False, skip_group_check=True)
                        m = pe.matmul(dst, kL[r0:r0 + 64, ky], qHL[r0:r0 + 64, qu], start=False, stop=False,
                                      skip_group_check=True)
                    m.then_inc(sb_scored, 1)
                elif kind == "sb_cum":
                    b = 1536 * (k % 2)
                    pe.wait_ge(constants_r, 3)
                    pe.wait_ge(sb_softplus, k + 1)
                    pe.wait_ge(sb_softplus_lo, k + 1)
                    for j in range(TT):
                        for i in range(j, TT):
                            dst = mxf[:, b + cols[j] + P * (i - j):b + cols[j] + T - P * j]
                            for part in (spH, spL):
                                m = pe.matmul(dst, (neg_triR if i == j else neg_oneR)[:, :],
                                              part[:, cols[i]:cols[i] + T - P * i], start=False,
                                              stop=i == TT - 1 and part is spL, skip_group_check=True)
                    m.then_inc(sb_summed, 1)
                elif kind == "sb_av":
                    r0 = 64 * (k % 2)
                    pe.wait_ge(sb_weights_masked, 2 * (k + 1))
                    for j in range(TT):
                        m = pe.matmul(mx[r0:r0 + 64, 3 * (k % 2), P * j:T], vs[:, j, HD * k:HD * k + HD],
                                      sw[k % 2][:, cols[j]:cols[j] + T - P * j], start=j == 0, stop=j == TT - 1,
                                      skip_group_check=True)
                    m.then_inc(sb_product, 1)
                elif kind == "bias":
                    pe.wait_ge(rows_in, 64)
                    tr = trev[:, :, :].rearrange("p h k -> p (h k)")
                    for j in range(3):
                        m = pe.matmul(mx[:, j, :], flip[:, :], tr[:, 512 * j:512 * j + 512], start=True, stop=True)
                    m.then_inc(bias_flipped, 1)
                elif kind == "swa_scores":
                    i, gq = k // 2, k % 2
                    k0 = CHUNK if i == 0 else 0
                    if k == 0:
                        kv_ready("kava", 1)
                        pe.wait_ge(sb_out, SB_HEADS)
                    else:
                        pe.wait_ge(swa_biased, k)
                    for hh in range(4):
                        h = 4 * gq + 2 * (hh % 2) + hh // 2
                        r0 = 64 * (h % 2)
                        m = pe.matmul(mxf[:, 256 * hh + k0:256 * hh + KEYS], qa[r0:r0 + 64, h // 2, P * i:P * i + P],
                                      kd[r0:r0 + 64, gq, P * i - CHUNK + k0:P * i + P], start=True, stop=True)
                    m.then_inc(swa_scored, 1)
                elif kind == "swa_turn":
                    pe.wait_ge(swa_normed, k + 1)
                    if k:
                        pe.wait_ge(swa_turned_copied, k)
                    if k >= 3:
                        pe.wait_ge(swa_turned_first, k - 2)
                    for part in range(1 if k // 2 == 0 else 0, 2):
                        for hh in range(4):
                            m = pe.transpose(mx[:, 2 + part, P * hh:P * hh + P],
                                             pr[k % 2][:, hh, P * part:P * part + P], ident[:, :])
                    m.then_inc(swa_turned, 1)
                elif kind == "swa_pv":
                    i, gq = k // 2, k % 2
                    pe.wait_ge(swa_turned_copied, k + 1)
                    if k >= 2:
                        pe.wait_ge(swa_turned_first, k - 1)
                    pe.wait_ge(*((swa_out, k) if k else (v_copied, 5)))
                    for par in range(2):
                        for part in range(1 if i == 0 else 0, 2):
                            m = pe.matmul(mx[64 * par:64 * par + 64, 4, 0:256],
                                          va[:, i - 1 + part, HD * gq:HD * gq + HD],
                                          pT[:, part, 256 * par:256 * par + 256],
                                          start=part == 0 or i == 0, stop=part == 1)
                    m.then_inc(swa_product, 1)
                elif kind == "y_norm":
                    pe.wait_ge(y_squares_added, 2)
                    for g2 in range(2):
                        m = stats(mx[:, 5, 4 * g2:4 * g2 + 4], ysq[:, 4 * g2, :], g2 == 0)
                    m.then_inc(y_mean_sq, 1)
                elif kind == "y_spread":
                    pe.wait_ge(root_out, 2)
                    spread(mx[:, 3, :], 0)
                    spread(mx[:, 4, :], 4).then_inc(rstd_spread, 1)
                elif kind == "decay":
                    pe.wait_ge(dt_ready, 1)
                    pe.wait_ge(sb_out, SB_HEADS)
                    for c in range(TT):
                        pe.matmul(mx[:, 5, 16 * c:16 * c + 16], tri[:, :], dta[:, c, :], start=True, stop=True)
                        m = pe.matmul(mx[:, 5, 64 + 16 * c:80 + 16 * c], ones[:, :], dta[:, c, :], start=True, stop=True)
                    m.then_inc(ssd_cumsums, 1)
                elif kind == "ssd_prep":
                    c = k
                    if c == 0:
                        pe.wait_ge(conv_silu, CONV_T)
                        pe.wait_ge(swa_out, 8)
                    else:
                        pe.wait_ge(ssd_state_made, c)
                    for t in range(8):
                        pe.transpose(mxf[:, P * t:P * t + P], xs[:, t, P * c:P * c + P], ident[:, :])
                    for g2 in range(2):
                        pe.transpose(mx[:, 2, P * g2:P * g2 + P], xs[:, 8 + g2, P * c:P * c + P], ident[:, :])
                    for g2 in range(2):
                        m = pe.matmul(mx[:, 2, 256 + P * g2:256 + P * g2 + P], xs[:, 8 + g2, P * c:P * c + P],
                                      xs[:, 10 + g2, P * c:P * c + P], start=True, stop=True)
                    m.then_inc(ssd_turned, 1)
                elif kind == "ssd_sum":
                    c, r = k // 4, k % 4
                    if k == 0:
                        pe.wait_ge(dta_lo, 1)
                        pe.wait_ge(ssd_decay_in, 1)
                    if k >= 2:
                        pe.wait_ge(ssd_exp, k - 1)
                    for hh in range(4):
                        h = 4 * r + hh
                        for part in (dtaH, dtaL):
                            m = pe.matmul(mx[:, 4 + k % 2, P * hh:P * hh + P],
                                          part[:, c, h:h + 1].broadcast_to([P, P]), triR[:, :],
                                          start=part is dtaH, stop=part is dtaL)
                    m.then_inc(ssd_sums_spread, 1)
                elif kind == "ssd_y":
                    c, r = k
                    n = 4 * c + r
                    pe.wait_ge(ssd_matrix, n + 1)
                    if n:
                        pe.wait_ge(ssd_y_made, 2 * n)
                    for hh in range(4):
                        h = 4 * r + hh
                        par, q = hh % 2, hh // 2
                        m = pe.matmul(mx[64 * par:64 * par + 64, 3, P * q:P * q + P], xd[c % 2][:, HD * h:HD * h + HD],
                                      mt[n % 2][:, hh, :], start=True, stop=True)
                    if c > 0:
                        pe.wait_ge(ssd_state_made, c)
                        for q in range(2):
                            pt = 2 * r + q
                            m = pe.matmul(mx[:, 3, 256 + P * q:256 + P * q + P], st[(c - 1) % 2][:, P * pt:P * pt + P],
                                          xs[:, 10 + r // 2, P * c:P * c + P], start=True, stop=True)
                    m.then_inc(ssd_product, 1)
                elif kind == "ssd_state":
                    pe.wait_ge(ssd_inputs, k + 1)
                    for g2 in range(2):
                        m = pe.matmul(mx[:, g2, :], bt[:, g2, :], xw[:, 512 * g2:512 * g2 + 512],
                                      start=True, stop=True)
                    m.then_inc(ssd_state_product, 1)

            def ff1(half, i, b):
                pe.wait_ge(relu, half * 16 + i * 4 + (2 * b + 2))
                pair(ffb[2 * b:2 * b + 2], (NB + b) % 2, hH, hL, KT,
                     lambda k: weights_ready(k, KT, half * 32 + i * 4 + 2 * (NB + b + 1)))

            def ff1_first(b):
                if b == 0:
                    pe.wait_ge(residual, 8)

                def ready(k):
                    weights_ready(k, KT, 2 * (NB + b + 1))
                    if b == 0:
                        pe.wait_ge(ff_input_lo, k + 1)

                pair(ffb[2 * b:2 * b + 2], (NB + b) % 2, hH, hL, KT, ready)
                if b == 0:
                    pe.wait_ge(squares_added, 5)
                    stats(mx[:, 5, :], sq[:, 0, :], True)
                    pe.wait_ge(squares, 12)
                    stats(mx[:, 5, :], sq[:, 7, :], False).then_inc(mean_sq, 1)

            for half in range(2):
                if half == 0:
                    for b in range(2):
                        ff1_first(b)
                    pe.wait_ge(r2_made, 1)
                    spread(mx[:, 4, :], 0).then_inc(rstd_spread, 1)
                with pe.Fori(1 - half, 4) as i:
                    for b in range(2):
                        ff1(half, i, b)
                with pe.Fori(0, 4) as i:
                    for b in range(2):
                        pe.wait_ge(act_lo, half * 16 + 8 * (b + 1))
                        for s in range(2):
                            if b == 0:
                                pe.wait_ge(residual, half * 8 + i * 2 + (7 + s))

                            def ready(k):
                                if s == 0:
                                    weights_ready(k, KT, half * 32 + i * 4 + 2 * (NB + 8 + b + 1))

                            product(mx[:, 2 + s, :], (NB + b) % 2, s, aH, aL, KT, k0=8 * b, start=b == 0,
                                    stop=b == 1, ready=ready).then_inc(tile_done, 1)
            pe.wait_ge(relu, 36)
            for t in range(TT):
                for j in range(4):
                    m = pe.transpose(outb[0][t][:, P * j:P * j + P], xT[:, j, P * t:P * t + P], ident[:, :])
                m.then_inc(rows_turned0, 1)
            pe.wait_ge(squares_summed, 1)
            stats(mx[:, 4, :], sq[:, 0, :], True)
            pe.wait_ge(squares, 20)
            stats(mx[:, 4, :], sq[:, 7, :], False).then_inc(mean_sq, 1)
            pe.wait_ge(residual, 24)
            for t in range(TT):
                if t == 3:
                    pe.wait_ge(root_in, 3)
                for j in range(4):
                    m = pe.transpose(outb[1][t][:, P * j:P * j + P], xT[:, 4 + j, P * t:P * t + P], ident[:, :])
                m.then_inc(rows_turned1, 1)


def relative_onehot():
    r = np.arange(320) - (P + CHUNK - 1)
    nb = BUCKETS // 2
    exact = nb // 2
    n = np.abs(r)
    large = exact + (np.log(np.maximum(n, 1) / exact) / np.log(MAX_DIST / exact) * (nb - exact)).astype(np.int32)
    b = np.where(r > 0, nb, 0) + np.where(n < exact, n, np.minimum(large, nb - 1))
    return (np.arange(BUCKETS)[:, None] == b[None, :]).astype(np.float32)


INS = ["x", "norm_mix_w", "w_in", "swa_sinks", "rel_bias", "conv_w", "conv_b", "dt_bias", "a_log", "d_skip",
       "ssd_norm_w", "w_out", "w_merge", "norm_ffn_w", "w_ff1", "w_ff2", "final_norm_w"]


def kernel(**inputs):
    import concourse.bacc as bacc
    from concourse.bass_utils import run_bass_kernel_spmd

    nc = bacc.Bacc("TRN2", target_bir_lowering=False, num_devices=1)
    arrays = {n: np.ascontiguousarray(inputs[n]) for n in INS}
    arrays["onehot"] = relative_onehot()
    args = {n: nc.dram_tensor(n, a.shape, mybir.dt.from_np(a.dtype), kind="ExternalInput").ap()
            for n, a in arrays.items()}
    out = nc.dram_tensor("out", (1, T, D), F32, kind="ExternalOutput").ap()
    build(nc, args, out)
    r = run_bass_kernel_spmd(nc, [arrays], core_ids=[0])
    return r.results[0]["out"]
```
